# Optimizing a Trainium2 kernel written in Bass

```python
import math
import jax, jax.numpy as jnp
from jax import lax
import numpy as np

D_MODEL = 1024
BATCH = 1
SEQ = 1024
DEPTH = 2
DEC_BATCH = 1
DEC_SEQ = 64
PAST_LEN = 256

CHUNK = 64
HEAD_DIM = 64
ROPE_THETA = 10000.0
LN_EPS = 1e-5
D_FF = 4 * D_MODEL

A_WIDTH = D_MODEL // 2
A_GROUPS = 8
A_GROUP_DIM = A_WIDTH // A_GROUPS
A_CHUNK = 128

B_HEADS = (D_MODEL // 2) // HEAD_DIM
B_KV_HEADS = 2
B_GROUP = B_HEADS // B_KV_HEADS
B_WINDOW = 128
B_WIN_CHUNKS = B_WINDOW // CHUNK

C_HEADS = D_MODEL // HEAD_DIM
C_KV_HEADS = 4
C_GROUP = C_HEADS // C_KV_HEADS
IDX_HEADS = 4
IDX_DIM = 64
TOPK_MAX = 256
ATTN_QBLOCK = 128

N_EVEN = (DEPTH + 1) // 2
N_ODD = DEPTH // 2
ALPHA = (2.0 * DEPTH) ** 0.25
BETA = (8.0 * DEPTH) ** -0.25

B_Q = B_HEADS * HEAD_DIM
B_KV = B_KV_HEADS * HEAD_DIM
AB_IN = 2 * A_WIDTH + B_Q + 2 * B_KV
AB_OUT = A_WIDTH + B_Q
AB_SPLITS = (A_WIDTH, 2 * A_WIDTH, 2 * A_WIDTH + B_Q, 2 * A_WIDTH + B_Q + B_KV)

C_Q = C_HEADS * HEAD_DIM
C_KV = C_KV_HEADS * HEAD_DIM
C_QI = IDX_HEADS * IDX_DIM
C_IN = C_Q + 2 * C_KV + C_QI + IDX_DIM + IDX_HEADS
C_OUT = C_Q
C_SPLITS = (C_Q, C_Q + C_KV, C_Q + 2 * C_KV, C_Q + 2 * C_KV + C_QI, C_Q + 2 * C_KV + C_QI + IDX_DIM)

kernel_name = "chunk_causal_gmlp_swa_dsa_encoder_step"

def layer_norm(x, g, b):
    xf = x.astype(jnp.float32)
    mu = xf.mean(-1, keepdims=True)
    var = jnp.square(xf - mu).mean(-1, keepdims=True)
    return ((xf - mu) * lax.rsqrt(var + LN_EPS) * g + b).astype(x.dtype)

def rope(x, pos):
    half = x.shape[-1] // 2
    inv_freq = jnp.exp(-math.log(ROPE_THETA) * jnp.arange(half, dtype=jnp.float32) / half)
    ang = pos.astype(jnp.float32)[:, None] * inv_freq[None, :]
    cos = jnp.cos(ang)[None, :, None, :]
    sin = jnp.sin(ang)[None, :, None, :]
    xf = x.astype(jnp.float32)
    x1, x2 = xf[..., :half], xf[..., half:]
    return jnp.concatenate([x1 * cos - x2 * sin, x2 * cos + x1 * sin], axis=-1).astype(x.dtype)

def gmlp_spatial(v, w_s, b_s):
    t = v.shape[2]
    w = jnp.tril(w_s[:, :t, :t])
    return jnp.einsum('gij,bnjgc->bnigc', w, v) + b_s[:, :t].T[None, None, :, :, None]

def sink_attention(q, k, v, mask, sinks):
    s = jnp.einsum('bcqhgd,bcnhd->bchgqn', q, k).astype(jnp.float32) * HEAD_DIM ** -0.5
    s = jnp.where(mask[None, :, None, None, None, :], s, -jnp.inf)
    sk = sinks.astype(jnp.float32)[None, None, :, :, None, None]
    m = jnp.maximum(s.max(-1, keepdims=True), sk)
    e = jnp.exp(s - m)
    p = e / (e.sum(-1, keepdims=True) + jnp.exp(sk - m))
    return jnp.einsum('bchgqn,bcnhd->bcqhgd', p.astype(v.dtype), v)

def indexer_scores(qi, wi, ki):
    s = jnp.einsum('bqhd,bsd->bqhs', qi, ki).astype(jnp.float32)
    return jnp.einsum('bqhs,bqh->bqs', jax.nn.relu(s), wi.astype(jnp.float32)) * (IDX_DIM ** -0.5 * IDX_HEADS ** -0.5)

def gather_rows(x, idx):
    return jax.vmap(lambda xb, ib: xb[ib])(x, idx)

def selected_attention(q, ksel, vsel, valid):
    s = jnp.einsum('bqhgd,bqnhd->bqhgn', q, ksel).astype(jnp.float32) * HEAD_DIM ** -0.5
    if valid is not None:
        s = jnp.where(valid[:, :, None, None, :], s, -jnp.inf)
    p = jax.nn.softmax(s, axis=-1)
    return jnp.einsum('bqhgn,bqnhd->bqhgd', p.astype(vsel.dtype), vsel)

def ab_mixer(h, pos, w_in, a_ln_g, a_ln_b, a_ws, a_bs, sinks, w_out, cache_k, cache_v):
    bsz, t, _ = h.shape
    u, va, qb, kb, vb = jnp.split(h @ w_in, AB_SPLITS, axis=-1)
    u = jax.nn.gelu(u)
    va = layer_norm(jax.nn.gelu(va), a_ln_g, a_ln_b)
    if cache_k is None:
        vch = va.reshape(bsz, t // A_CHUNK, A_CHUNK, A_GROUPS, A_GROUP_DIM)
    else:
        vch = va.reshape(bsz, 1, t, A_GROUPS, A_GROUP_DIM)
    a_out = u * gmlp_spatial(vch, a_ws, a_bs).reshape(bsz, t, A_WIDTH)
    q = rope(qb.reshape(bsz, t, B_HEADS, HEAD_DIM), pos)
    k = rope(kb.reshape(bsz, t, B_KV_HEADS, HEAD_DIM), pos)
    v = vb.reshape(bsz, t, B_KV_HEADS, HEAD_DIM)
    sk = sinks.reshape(B_KV_HEADS, B_GROUP)
    if cache_k is None:
        nc = t // CHUNK
        qc = q.reshape(bsz, nc, CHUNK, B_KV_HEADS, B_GROUP, HEAD_DIM)
        pad = ((0, 0), (B_WIN_CHUNKS, 0), (0, 0), (0, 0), (0, 0))
        kp = jnp.pad(k.reshape(bsz, nc, CHUNK, B_KV_HEADS, HEAD_DIM), pad)
        vp = jnp.pad(v.reshape(bsz, nc, CHUNK, B_KV_HEADS, HEAD_DIM), pad)
        kband = jnp.concatenate([kp[:, i:i + nc] for i in range(B_WIN_CHUNKS + 1)], axis=2)
        vband = jnp.concatenate([vp[:, i:i + nc] for i in range(B_WIN_CHUNKS + 1)], axis=2)
        key_chunk = (jnp.arange(nc)[:, None] - B_WIN_CHUNKS
                     + jnp.arange((B_WIN_CHUNKS + 1) * CHUNK)[None, :] // CHUNK)
        o = sink_attention(qc, kband, vband, key_chunk >= 0, sk)
        new_k, new_v = k[:, -B_WINDOW:], v[:, -B_WINDOW:]
    else:
        kall = jnp.concatenate([cache_k, k], axis=1)[:, None]
        vall = jnp.concatenate([cache_v, v], axis=1)[:, None]
        qc = q.reshape(bsz, 1, t, B_KV_HEADS, B_GROUP, HEAD_DIM)
        o = sink_attention(qc, kall, vall, jnp.ones((1, kall.shape[2]), dtype=bool), sk)
        new_k, new_v = k, v
    b_out = o.reshape(bsz, t, B_Q)
    y = jnp.concatenate([a_out, b_out], axis=-1) @ w_out
    return y, va, new_k, new_v

def c_mixer(h, pos, w_in, w_out, cache_k, cache_v, cache_i):
    bsz, t, _ = h.shape
    qb, kb, vb, qib, kib, wi = jnp.split(h @ w_in, C_SPLITS, axis=-1)
    q = rope(qb.reshape(bsz, t, C_HEADS, HEAD_DIM), pos).reshape(bsz, t, C_KV_HEADS, C_GROUP, HEAD_DIM)
    k = rope(kb.reshape(bsz, t, C_KV_HEADS, HEAD_DIM), pos)
    v = vb.reshape(bsz, t, C_KV_HEADS, HEAD_DIM)
    qi = rope(qib.reshape(bsz, t, IDX_HEADS, IDX_DIM), pos)
    ki = rope(kib.reshape(bsz, t, 1, IDX_DIM), pos)[:, :, 0]
    if cache_k is None:
        nb = t // ATTN_QBLOCK
        k_sel = min(TOPK_MAX, t // 4)
        key_chunk = jnp.arange(t) // CHUNK

        def block(args):
            qblk, qiblk, wblk, qpos = args
            q_chunk = qpos // CHUNK
            sc = indexer_scores(qiblk, wblk, ki)
            sc = jnp.where((key_chunk[None, :] <= q_chunk[:, None])[None], sc, -jnp.inf)
            _, idx = lax.top_k(sc, k_sel)
            valid = (idx // CHUNK) <= q_chunk[None, :, None]
            return selected_attention(qblk, gather_rows(k, idx), gather_rows(v, idx), valid)

        to_blocks = lambda a: jnp.moveaxis(a.reshape((bsz, nb, ATTN_QBLOCK) + a.shape[2:]), 1, 0)
        o = lax.map(block, (to_blocks(q), to_blocks(qi), to_blocks(wi), pos.reshape(nb, ATTN_QBLOCK)))
        o = jnp.moveaxis(o, 0, 1)
    else:
        kall = jnp.concatenate([cache_k, k], axis=1)
        vall = jnp.concatenate([cache_v, v], axis=1)
        iall = jnp.concatenate([cache_i, ki], axis=1)
        k_sel = min(TOPK_MAX, kall.shape[1] // 4)
        _, idx = lax.top_k(indexer_scores(qi, wi, iall), k_sel)
        o = selected_attention(q, gather_rows(kall, idx), gather_rows(vall, idx), None)
    y = o.reshape(bsz, t, C_OUT) @ w_out
    return y, k, v, ki

def sq_relu_mlp(x, w1, w2):
    return jnp.square(jax.nn.relu(x @ w1)) @ w2

def trunk(x, pos, cache_b_k, cache_b_v, cache_c_k, cache_c_v, cache_c_idx,
          ab_w_in, a_ln_g, a_ln_b, a_ws, a_bs, b_sinks, ab_w_out, c_w_in, c_w_out,
          ln1_g, ln1_b, ln2_g, ln2_b, ff_w1, ff_w2):
    sample = cache_b_k is not None
    a_v, b_k, b_v, c_k, c_v, c_i = [], [], [], [], [], []
    for layer in range(DEPTH):
        i = layer // 2
        if layer % 2 == 0:
            y, va, nk, nv = ab_mixer(x, pos, ab_w_in[i], a_ln_g[i], a_ln_b[i], a_ws[i], a_bs[i], b_sinks[i], ab_w_out[i],
                                     cache_b_k[i] if sample else None, cache_b_v[i] if sample else None)
            a_v.append(va); b_k.append(nk); b_v.append(nv)
        else:
            y, nk, nv, ni = c_mixer(x, pos, c_w_in[i], c_w_out[i],
                                    cache_c_k[i] if sample else None, cache_c_v[i] if sample else None,
                                    cache_c_idx[i] if sample else None)
            c_k.append(nk); c_v.append(nv); c_i.append(ni)
        x = layer_norm(ALPHA * x + y, ln1_g[layer], ln1_b[layer])
        x = layer_norm(ALPHA * x + sq_relu_mlp(x, ff_w1[layer], ff_w2[layer]), ln2_g[layer], ln2_b[layer])
    return (x, jnp.stack(a_v, 0), jnp.stack(b_k, 0), jnp.stack(b_v, 0),
            jnp.stack(c_k, 0), jnp.stack(c_v, 0), jnp.stack(c_i, 0))

def setup_inputs(seed: int = 0) -> dict:
    key = jax.random.key(seed)
    ks = jax.random.split(key, 24)
    nrm = lambda k, shape, scale: jax.random.normal(k, shape, jnp.float32) * scale
    b_cache = min(B_WINDOW, PAST_LEN)
    return {
        "x_prompt": nrm(ks[0], (BATCH, SEQ, D_MODEL), 1.0),
        "x_sample": nrm(ks[1], (DEC_BATCH, DEC_SEQ, D_MODEL), 1.0),
        "cache_b_k": nrm(ks[2], (N_EVEN, DEC_BATCH, b_cache, B_KV_HEADS, HEAD_DIM), 1.0),
        "cache_b_v": nrm(ks[3], (N_EVEN, DEC_BATCH, b_cache, B_KV_HEADS, HEAD_DIM), 1.0),
        "cache_c_k": nrm(ks[4], (N_ODD, DEC_BATCH, PAST_LEN, C_KV_HEADS, HEAD_DIM), 1.0),
        "cache_c_v": nrm(ks[5], (N_ODD, DEC_BATCH, PAST_LEN, C_KV_HEADS, HEAD_DIM), 1.0),
        "cache_c_idx": nrm(ks[6], (N_ODD, DEC_BATCH, PAST_LEN, IDX_DIM), 1.0),
        "ab_w_in": nrm(ks[7], (N_EVEN, D_MODEL, AB_IN), D_MODEL ** -0.5),
        "a_ln_g": 1.0 + nrm(ks[8], (N_EVEN, A_WIDTH), 0.01),
        "a_ln_b": nrm(ks[9], (N_EVEN, A_WIDTH), 0.01),
        "a_ws": nrm(ks[10], (N_EVEN, A_GROUPS, A_CHUNK, A_CHUNK), A_CHUNK ** -0.5),
        "a_bs": 1.0 + nrm(ks[11], (N_EVEN, A_GROUPS, A_CHUNK), 0.01),
        "b_sinks": nrm(ks[12], (N_EVEN, B_HEADS), 0.5),
        "ab_w_out": nrm(ks[13], (N_EVEN, AB_OUT, D_MODEL), BETA * AB_OUT ** -0.5),
        "c_w_in": nrm(ks[14], (N_ODD, D_MODEL, C_IN), D_MODEL ** -0.5),
        "c_w_out": nrm(ks[15], (N_ODD, C_OUT, D_MODEL), BETA * C_OUT ** -0.5),
        "ln1_g": 1.0 + nrm(ks[16], (DEPTH, D_MODEL), 0.01),
        "ln1_b": nrm(ks[17], (DEPTH, D_MODEL), 0.01),
        "ln2_g": 1.0 + nrm(ks[18], (DEPTH, D_MODEL), 0.01),
        "ln2_b": nrm(ks[19], (DEPTH, D_MODEL), 0.01),
        "ff_w1": nrm(ks[20], (DEPTH, D_MODEL, D_FF), D_MODEL ** -0.5),
        "ff_w2": nrm(ks[21], (DEPTH, D_FF, D_MODEL), BETA * D_FF ** -0.5),
    }

def reference(x_prompt, x_sample, cache_b_k, cache_b_v, cache_c_k, cache_c_v, cache_c_idx,
              ab_w_in, a_ln_g, a_ln_b, a_ws, a_bs, b_sinks, ab_w_out, c_w_in, c_w_out,
              ln1_g, ln1_b, ln2_g, ln2_b, ff_w1, ff_w2):
    weights = (ab_w_in, a_ln_g, a_ln_b, a_ws, a_bs, b_sinks, ab_w_out, c_w_in, c_w_out,
               ln1_g, ln1_b, ln2_g, ln2_b, ff_w1, ff_w2)
    pos_p = jnp.arange(x_prompt.shape[1], dtype=jnp.int32)
    pos_s = PAST_LEN + jnp.arange(x_sample.shape[1], dtype=jnp.int32)
    y_prompt, _, p_b_k, p_b_v, p_c_k, p_c_v, p_c_idx = trunk(
        x_prompt, pos_p, None, None, None, None, None, *weights)
    y_sample, s_a_v, s_b_k, s_b_v, s_c_k, s_c_v, s_c_idx = trunk(
        x_sample, pos_s, cache_b_k, cache_b_v, cache_c_k, cache_c_v, cache_c_idx, *weights)
    return (y_prompt, y_sample, p_b_k, p_b_v, p_c_k, p_c_v, p_c_idx,
            s_a_v, s_b_k, s_b_v, s_c_k, s_c_v, s_c_idx)


_drawn_inputs = setup_inputs


def setup_inputs(seed=0):
    import zlib

    import numpy as np

    out = dict(_drawn_inputs(seed))
    spreads = {}
    factors = {'a_ln_g': 5.936,
     'a_ln_b': 5.743,
     'a_bs': 8.0,
     'b_sinks': 8.0,
     'ln1_g': 3.422,
     'ln1_b': 3.203,
     'ln2_g': 3.463,
     'ln2_b': 3.395,
     'cache_c_v': 2.927}
    for name, (base, spread) in spreads.items():
        noise = np.random.default_rng([zlib.crc32(name.encode()), seed]).standard_normal(out[name].shape)
        drawn = base * np.exp(spread * noise) if base else spread * noise
        out[name] = __import__('jax').numpy.asarray(drawn.astype(out[name].dtype))
    for name, factor in factors.items():
        out[name] = (out[name] * factor).astype(out[name].dtype)
    return out
```

```python
from contextlib import ExitStack

import numpy as np

import concourse.bass as bass
from concourse import mybir

ALU = mybir.AluOpType
ACT = mybir.ActivationFunctionType
F32 = mybir.dt.float32
F32R = mybir.dt.float32r

P = 128
D = 1024
KT = D // P
SEQ = 1024
DEC = 64
TOK = SEQ + DEC
NP_TILES = SEQ // P
NT = NP_TILES + 1
SAMPLE = NP_TILES
CHUNK = 64
HD = 64
HALF = HD // 2
D_FF = 4 * D
DEPTH = 2
ALPHA = (2.0 * DEPTH) ** 0.25
EPS = 1e-5
THETA = 10000.0
PAST = 256

A_WIDTH = D // 2
A_GROUPS = 8
A_GD = A_WIDTH // A_GROUPS
B_HEADS = 8
B_KV = 2
B_WIN = 128
AB_IN = 2 * A_WIDTH + B_HEADS * HD + 2 * B_KV * HD

C_HEADS = 16
C_KV = 4
IDX_HEADS = 4
C_Q = C_HEADS * HD
C_KVW = C_KV * HD
C_QI = IDX_HEADS * HD
C_IN = C_Q + 2 * C_KVW + C_QI + HD + IDX_HEADS
TOPK = 256
TOPK_SAMPLE = min(TOPK, (PAST + DEC) // 4)

COLS = 512
QUARTER = 2
W_SLOTS = 5
FC = 256
N_FC = D_FF // FC
FT = FC // P

MASKED = -1e30
BARRED = -3.0e38
TAKEN = -3.3e38
LARGE = 3.0e38

IDX_COL = C_Q + 2 * C_KVW
IDX_W = C_QI + HD + IDX_HEADS


def rows(t):
    return P if t < SAMPLE else DEC


def tok(t):
    return t * P, t * P + rows(t)


RANGES = [(0, 384), (384, 768), (768, TOK)]


def encoder(nc, aps):
    with ExitStack() as ctx:
        c = ctx.enter_context
        A = c(nc.sbuf_tensor("act", [P, NT, D], F32))
        xt_hi = c(nc.sbuf_tensor("xt_hi", [P, KT, TOK], F32R))
        xt_lo = c(nc.sbuf_tensor("xt_lo", [P, KT, TOK], F32R))
        ident = c(nc.sbuf_tensor("ident", [P, P], F32))
        mhalf = c(nc.sbuf_tensor("minus_half", [P, 1], F32))
        ps = c(nc.psum_tensor("psum", [P, 8, COLS], F32))
        x2_dram = nc.dram_tensor("x2_scratch", (TOK, D), F32, kind="Internal").ap()
        aps = dict(aps, x2=x2_dram)
        with ExitStack() as ms:
            va = ms.enter_context(nc.sbuf_tensor("va", [P, NT, A_WIDTH], F32))
            kb = ms.enter_context(nc.sbuf_tensor("k_b", [P, NT + 1, P], F32))
            vb = ms.enter_context(nc.sbuf_tensor("v_b", [P, NT + 1, P], F32))
            block_ab_in(nc, aps, A, xt_hi, xt_lo, va, kb, vb, ident, mhalf, ps)
            block_ab_mixer(nc, aps, A, va, kb, vb, ident, ps)
        block_out(nc, aps, 0, aps["x"], aps["ab_w_out"], A, xt_hi, xt_lo, ident, mhalf, ps)
        block_mlp(nc, aps, 0, A, xt_hi, xt_lo, ident, mhalf, ps)
        with ExitStack() as cs:
            kc = cs.enter_context(nc.sbuf_tensor("k_c", [P, NT + 2, C_KVW], F32))
            vc = cs.enter_context(nc.sbuf_tensor("v_c", [P, NT + 2, C_KVW], F32))
            ki = cs.enter_context(nc.sbuf_tensor("k_idx", [P, NT + 2, 2 * HD], F32))
            qi = cs.enter_context(nc.sbuf_tensor("q_idx", [P, NT, C_QI], F32))
            wi = cs.enter_context(nc.sbuf_tensor("w_idx", [P, NT, IDX_HEADS], F32))
            block_c_in(nc, aps, A, xt_hi, xt_lo, kc, vc, ki, qi, wi, ps)
            block_c_mixer(nc, aps, A, kc, vc, ki, qi, wi, ident, ps)
        block_out(nc, aps, 1, aps["x2"], aps["c_w_out"], A, xt_hi, xt_lo, ident, mhalf, ps)
        block_mlp(nc, aps, 1, A, xt_hi, xt_lo, ident, mhalf, ps)


class Stream:

    def __init__(self, nc, c, tag, w, chunks, done):
        self.w = w.rearrange("(k p) n -> p k n", p=P)
        self.chunks = chunks
        self.n = 4 * len(chunks)
        self.raw = c(nc.sbuf_tensor(tag + "w_raw", [P, 2, QUARTER, COLS], F32))
        self.hi = c(nc.sbuf_tensor(tag + "w_hi", [P, W_SLOTS, QUARTER, COLS], F32R))
        self.lo = c(nc.sbuf_tensor(tag + "w_lo", [P, W_SLOTS, QUARTER, COLS], F32R))
        self.arrived = [c(nc.semaphore(tag + f"w_arrived{i}")) for i in range(2)]
        self.hi_made = c(nc.semaphore(tag + "w_hi_made"))
        self.lo_made = c(nc.semaphore(tag + "w_lo_made"))
        self.used = c(nc.semaphore(tag + "w_used"))
        self.done = done

    def load(self, eng, n):
        j, q = divmod(n, 4)
        c0, w = self.chunks[j]
        if n >= 2:
            eng.wait_ge(self.lo_made, n - 1)
        eng.dma_start(self.raw[:, n % 2, :, 0:w],
                      self.w[:, QUARTER * q:QUARTER * q + QUARTER, c0:c0 + w]).then_inc(self.arrived[n % 2], 16)

    def split_hi(self, act, n):
        w = self.chunks[n // 4][1]
        act.wait_ge(self.arrived[n % 2], 16 * (n // 2 + 1))
        if n >= W_SLOTS:
            j, q = divmod(n - W_SLOTS, 4)
            if q < 3:
                act.wait_ge(self.used, 3 * j + q + 1)
            else:
                act.wait_ge(self.done, NT * (j + 1))
        act.copy(self.hi[:, n % W_SLOTS, :, 0:w], self.raw[:, n % 2, :, 0:w]).then_inc(self.hi_made, 1)

    def split_lo(self, dve, n):
        w = self.chunks[n // 4][1]
        dve.wait_ge(self.hi_made, n + 1)
        dve.tensor_tensor(self.lo[:, n % W_SLOTS, :, 0:w], self.raw[:, n % 2, :, 0:w],
                          self.hi[:, n % W_SLOTS, :, 0:w], ALU.subtract).then_inc(self.lo_made, 1)

    def next_pieces(self, j):
        return range(4 * j + W_SLOTS, min(4 * j + 4 + W_SLOTS, self.n))

    def product(self, pe, out, t, j, xt_hi, xt_lo):
        a, b = tok(t)
        w = self.chunks[j][1]
        for q in range(4):
            n = 4 * j + q
            if t == 0:
                pe.wait_ge(self.lo_made, n + 1)
            s = n % W_SLOTS
            for k in range(QUARTER):
                kk = QUARTER * q + k
                first, last = kk == 0, kk == KT - 1
                pe.matmul(out[0:b - a, 0:w], xt_hi[:, kk, a:b], self.hi[:, s, k, 0:w], start=first, stop=False)
                pe.matmul(out[0:b - a, 0:w], xt_hi[:, kk, a:b], self.lo[:, s, k, 0:w], start=False, stop=False)
                mm = pe.matmul(out[0:b - a, 0:w], xt_lo[:, kk, a:b], self.hi[:, s, k, 0:w], start=False, stop=last)
            if t == NT - 1 and q < 3:
                mm.then_inc(self.used, 1)
        mm.then_inc(self.done, 1)


class Norm:

    def __init__(self, nc, c, tag, name, width, g_row, b_row):
        self.width, self.g_row, self.b_row = width, g_row, b_row
        self.g = c(nc.sbuf_tensor(tag + f"{name}_g", [P, width], F32))
        self.b = c(nc.sbuf_tensor(tag + f"{name}_b", [P, width], F32))
        self.stats = c(nc.sbuf_tensor(tag + f"{name}_stats", [P, 2, 6 * (width // COLS)], F32))
        self.mv = c(nc.sbuf_tensor(tag + f"{name}_mv", [P, NT, 2], F32))
        self.var = c(nc.sbuf_tensor(tag + f"{name}_var", [P, NT], F32))
        self.rstd = c(nc.sbuf_tensor(tag + f"{name}_rstd", [P, NT], F32))
        self.shift = c(nc.sbuf_tensor(tag + f"{name}_shift", [P, NT], F32))
        s = lambda what: c(nc.semaphore(tag + f"{name}_{what}"))
        self.loaded, self.chain, self.var_ready, self.rstd_ready = s("loaded"), s("chain"), s("var_ready"), s("rstd_ready")
        self.shift_ready, self.normalised, self.scaled, self.done = s("shift_ready"), s("normalised"), s("scaled"), s("done")
        self.links = 0

    def load(self, eng):
        eng.dma_start(self.g[:], self.g_row.to_broadcast([P, self.width])).then_inc(self.loaded, 16)
        eng.dma_start(self.b[:], self.b_row.to_broadcast([P, self.width])).then_inc(self.loaded, 16)

    def link(self, dve, ins):
        self.links += 1
        ins.then_inc(self.chain, 1)
        dve.wait_ge(self.chain, self.links)

    def statistics(self, dve, x, t):
        r, st = rows(t), self.stats[:, t % 2]
        for h in range(self.width // COLS):
            ins = dve.bn_stats(st[0:r, 6 * h:6 * h + 6], x[0:r, COLS * h:COLS * h + COLS])
        self.link(dve, ins)
        self.link(dve, dve.bn_aggr(self.mv[0:r, t], st[0:r]))
        dve.tensor_scalar(self.var[0:r, t:t + 1], self.mv[0:r, t, 1:2], EPS, None, ALU.add).then_inc(self.var_ready, 1)

    def rsqrt(self, pool, mhalf, t):
        r = rows(t)
        pool.wait_ge(self.var_ready, t + 1)
        pool.tensor_tensor(self.rstd[0:r, t:t + 1], self.var[0:r, t:t + 1], mhalf[0:r], ALU.pow).then_inc(self.rstd_ready, 1)
        pool.wait_ge(self.rstd_ready, t + 1)
        pool.tensor_scalar(self.shift[0:r, t:t + 1], self.mv[0:r, t, 0:1], self.rstd[0:r, t:t + 1], -1.0,
                           ALU.mult, ALU.mult).then_inc(self.shift_ready, 1)

    def normalise(self, act, x, t):
        r = rows(t)
        act.wait_ge(self.shift_ready, t + 1)
        act.activation(x[0:r], x[0:r], ACT.Identity, bias=self.shift[0:r, t:t + 1],
                       scale=self.rstd[0:r, t:t + 1]).then_inc(self.normalised, 1)

    def scale(self, dve, x, t):
        r = rows(t)
        if t == 0:
            dve.wait_ge(self.loaded, 32)
        dve.wait_ge(self.normalised, t + 1)
        dve.tensor_tensor(x[0:r], x[0:r], self.g[0:r], ALU.mult).then_inc(self.scaled, 1)

    def offset(self, pool, x, t):
        r = rows(t)
        if t == 0:
            pool.wait_ge(self.loaded, 32)
        pool.wait_ge(self.scaled, t + 1)
        pool.tensor_tensor(x[0:r], x[0:r], self.b[0:r], ALU.add).then_inc(self.done, 1)


def rope(dve, link, src, table, tmp, heads):
    r = src.shape[0]
    both = lambda c0, w: table[:, c0:c0 + w].unsqueeze(1).to_broadcast([r, heads, w])
    dve.tensor_tensor(tmp[:, 0, 0:heads], src, both(0, HD), ALU.mult)
    dve.tensor_tensor(tmp[:, 1, 0:heads, 0:HALF], src[:, :, HALF:HD], both(HD, HALF), ALU.mult)
    link(dve.tensor_tensor(tmp[:, 1, 0:heads, HALF:HD], src[:, :, 0:HALF], both(HD + HALF, HALF), ALU.mult))


def block_ab_in(nc, aps, A, xt_hi, xt_lo, va, kb, vb, ident, mhalf, ps):
    tag = "ab_in_"
    banks = [ps[:, i] for i in range(8)]
    with ExitStack() as s:
        c = s.enter_context
        chunks = [(0, COLS), (COLS, COLS), (2 * COLS, COLS), (3 * COLS, 2 * P)]
        done = c(nc.semaphore(tag + "products_done"))
        st = Stream(nc, c, tag, aps["ab_w_in"], chunks, done)
        ln = Norm(nc, c, tag, "a_ln", A_WIDTH, aps["a_ln_g"], aps["a_ln_b"])
        xr = c(nc.sbuf_tensor(tag + "xt_raw", [P, 2, TOK // 2], F32))
        table = c(nc.sbuf_tensor(tag + "rope_table", [P, NT, P], F32))
        tmp = c(nc.sbuf_tensor(tag + "rope_tmp", [P, 2, 2, 8, HD], F32))
        x_arrived = [c(nc.semaphore(tag + f"x_arrived{i}")) for i in range(2)]
        table_arrived = c(nc.semaphore(tag + "table_arrived"))
        x_hi = c(nc.semaphore(tag + "x_hi_made"))
        x_lo = c(nc.semaphore(tag + "x_lo_made"))
        evac_act = c(nc.semaphore(tag + "banks_read_by_scalar"))
        evac_dve = c(nc.semaphore(tag + "banks_read_by_vector"))
        chain = c(nc.semaphore(tag + "vector_chain"))
        consts = c(nc.semaphore(tag + "constants"))
        ready = c(nc.semaphore(tag + "outputs_ready"))
        stored = c(nc.semaphore(tag + "outputs_stored"))
        block = c(nc.Block())
        HT = TOK // 2
        xT = aps["xT"].rearrange("(k p) t -> p k t", p=P)

        @block.sync
        def _(sp):
            for n in range(2 * KT):
                k, h = divmod(n, 2)
                if n >= 2:
                    sp.wait_ge(x_lo, n - 1)
                sp.dma_start(xr[:, n % 2], xT[:, k, h * HT:h * HT + HT]).then_inc(x_arrived[n % 2], 16)
                if n < 2:
                    st.load(sp, n)
            sp.dma_start(table[:, 0:NP_TILES], aps["rope"][0:SEQ].rearrange("(t p) c -> p t c", p=P)).then_inc(table_arrived, 16)
            sp.dma_start(table[0:DEC, SAMPLE], aps["rope"][SEQ:TOK]).then_inc(table_arrived, 16)
            ln.load(sp)
            for n in range(2, st.n):
                st.load(sp, n)
            sp.wait_ge(ready, NT)
            sp.wait_ge(evac_dve, 2 * NT)
            sp.dma_start(aps["p_b_k"], kb[:, NP_TILES - 1]).then_inc(stored, 16)
            sp.dma_start(aps["p_b_v"], vb[:, NP_TILES - 1]).then_inc(stored, 16)
            sp.dma_start(aps["s_b_k"], kb[0:DEC, NT]).then_inc(stored, 16)
            sp.dma_start(aps["s_b_v"], vb[0:DEC, NT]).then_inc(stored, 16)
            sp.wait_ge(ln.done, NT)
            sp.dma_start(aps["s_a_v"], va[0:DEC, SAMPLE]).then_inc(stored, 16)
            sp.wait_ge(stored, 80)

        @block.gpsimd
        def _(pool):
            pool.memset(mhalf[:], -0.5).then_inc(consts, 1)
            pool.memset(ident[:], 0.0).then_inc(consts, 1)
            pool.wait_ge(consts, 2)
            pool.affine_select(out=ident[:], in_=ident[:], compare_op=ALU.not_equal, fill=1.0, base=0,
                               pattern=[[-1, P]], channel_multiplier=1).then_inc(consts, 1)
            for t in range(NT + 1):
                if t < NT:
                    ln.rsqrt(pool, mhalf, t)
                if t >= 1:
                    ln.offset(pool, va[:, t - 1], t - 1)

        @block.scalar
        def _(act):
            for n in range(2 * KT):
                k, h = divmod(n, 2)
                act.wait_ge(x_arrived[n % 2], 16 * (n // 2 + 1))
                act.copy(xt_hi[:, k, h * HT:h * HT + HT], xr[:, n % 2]).then_inc(x_hi, 1)
                if n < 2:
                    st.split_hi(act, n)
            for n in range(2, W_SLOTS):
                st.split_hi(act, n)
            for j in range(len(chunks)):
                for t in range(NT):
                    if t == NT - 1:
                        for n in st.next_pieces(j):
                            st.split_hi(act, n)
                    if j < 2:
                        g, r = j * NT + t, rows(t)
                        act.wait_ge(done, g + 1)
                        out = A[0:r, t, 0:A_WIDTH] if j == 0 else va[0:r, t]
                        act.activation(out, banks[g % 8][0:r], ACT.Gelu_apprx_tanh).then_inc(evac_act, 1)
                    if j == 1 and t >= 1:
                        ln.normalise(act, va[:, t - 1], t - 1)
                if j == 1:
                    ln.normalise(act, va[:, NT - 1], NT - 1)

        @block.vector
        def _(dve):
            links = [0]

            def link(ins):
                links[0] += 1
                ins.then_inc(chain, 1)
                dve.wait_ge(chain, links[0])

            for n in range(2 * KT):
                k, h = divmod(n, 2)
                dve.wait_ge(x_hi, n + 1)
                dve.tensor_tensor(xt_lo[:, k, h * HT:h * HT + HT], xr[:, n % 2],
                                  xt_hi[:, k, h * HT:h * HT + HT], ALU.subtract).then_inc(x_lo, 1)
                if n < 2:
                    st.split_lo(dve, n)
            for n in range(2, W_SLOTS):
                st.split_lo(dve, n)
            dve.wait_ge(table_arrived, 32)
            for j in range(len(chunks)):
                for t in range(NT):
                    g, r = j * NT + t, rows(t)
                    turn = tmp[0:r, g % 2]
                    if t == NT - 1:
                        for n in st.next_pieces(j):
                            st.split_lo(dve, n)
                    if j == 1:
                        dve.wait_ge(evac_act, g + 1)
                        ln.statistics(dve, va[:, t], t)
                        if t >= 1:
                            ln.scale(dve, va[:, t - 1], t - 1)
                    if j == 2:
                        dve.wait_ge(done, g + 1)
                        if t >= 2:
                            dve.wait_ge(evac_dve, t - 1)
                        src = banks[g % 8][0:r].rearrange("p (h d) -> p h d", d=HD)
                        rope(dve, link, src, table[0:r, t], turn, 8)
                        out = A[0:r, t, A_WIDTH:D].rearrange("p (g kv d) -> p kv g d", kv=B_KV, d=HD)
                        two = lambda i: turn[:, i].rearrange("p (kv g) d -> p kv g d", kv=B_KV)
                        dve.tensor_tensor(out, two(0), two(1), ALU.add).then_inc(evac_dve, 1)
                    if j == 3:
                        slot = t if t < SAMPLE else NT
                        dve.wait_ge(done, g + 1)
                        dve.wait_ge(evac_dve, g - 1 - 2 * NT)
                        src = banks[g % 8][0:r, 0:P].rearrange("p (h d) -> p h d", d=HD)
                        rope(dve, link, src, table[0:r, t], turn, 2)
                        dve.tensor_tensor(kb[0:r, slot].rearrange("p (h d) -> p h d", d=HD),
                                          turn[:, 0, 0:2], turn[:, 1, 0:2], ALU.add).then_inc(ready, 1)
                        dve.tensor_copy(vb[0:r, slot], banks[g % 8][0:r, P:2 * P]).then_inc(evac_dve, 1)
                if j == 1:
                    ln.scale(dve, va[:, NT - 1], NT - 1)

        @block.tensor
        def _(pe):
            pe.wait_ge(x_lo, 2 * KT)
            for j in range(len(chunks)):
                for t in range(NT):
                    g = j * NT + t
                    before = g - 8
                    if before >= 0:
                        if before < 2 * NT:
                            pe.wait_ge(evac_act, before + 1)
                        else:
                            pe.wait_ge(evac_dve, before + 1 - 2 * NT)
                    st.product(pe, banks[g % 8], t, j, xt_hi, xt_lo)


def block_ab_mixer(nc, aps, A, va, kb, vb, ident, ps):
    CACHE, OWN = SAMPLE, NT
    tag = "ab_mix_"
    banks = [ps[:, i] for i in range(8)]
    with ExitStack() as s:
        c = s.enter_context
        sb = lambda name, shape: c(nc.sbuf_tensor(tag + name, shape, F32))
        sem = lambda name: c(nc.semaphore(tag + name))
        wsT = sb("ws_T", [P, A_GROUPS, P])
        bs = sb("bs", [P, A_GROUPS])
        sinks = sb("sinks", [P, B_HEADS])
        nsinks = sb("minus_sinks", [P, B_HEADS])
        mask = sb("mask", [P, 3, 2 * P])
        kT = sb("kT", [P, NT + 1, P])
        qT = sb("qT", [P, 2, 4, P])
        S = sb("scores", [P, B_HEADS, 2 * P])
        E = sb("probs", [P, B_HEADS, 2 * P])
        pT = sb("probs_T", [P, B_HEADS, 2, P])
        nm = sb("minus_max", [P, 2, B_HEADS])
        rs = sb("row_sum", [P, 2, B_HEADS])
        es = sb("sink_shifted", [P, 2, B_HEADS])
        ee = sb("sink_exp", [P, 2, B_HEADS])
        den = sb("den", [P, 2, B_HEADS])
        rden = sb("rden", [P, 2, B_HEADS])
        loaded, wmask, masks = sem("loaded"), sem("ws_masked"), sem("masks_made")
        gate_done, gate_read, ns_made = sem("gate_done"), sem("gate_read"), sem("minus_sinks_made")
        kt_done, kt_read = sem("k_transposed"), sem("k_T_ready")
        qt_done, qt_read = sem("q_transposed"), sem("q_T_ready")
        s_done, s_read = sem("scores_done"), sem("scores_read")
        e_done, ee_done, es_done = sem("probs_ready"), sem("sink_exp_ready"), sem("sink_shifted_ready")
        pt_done, pt_read = sem("p_transposed"), sem("p_T_ready")
        o_done, o_read = sem("out_done"), sem("out_read")
        den_made, rden_made = sem("den_made"), sem("rden_made")
        block = c(nc.Block())
        nkeys = lambda t: P if t == 0 else (2 * P if t < SAMPLE else P + DEC)
        first_slot = lambda t: max(t - 1, 0) if t < SAMPLE else CACHE
        nblocks = lambda t: 1 if t == 0 else 2
        kwidth = lambda t, b: DEC if (t == SAMPLE and b == 1) else P

        def kT_keys(t, half):
            flat = kT[half * HD:half * HD + HD].rearrange("p s k -> p (s k)")
            s0 = first_slot(t) * P
            return flat[:, s0:s0 + nkeys(t)]

        @block.sync
        def _(sp):
            sp.dma_start(wsT[:], aps["ws_T"]).then_inc(loaded, 16)
            sp.dma_start(bs[:], aps["bs_T"]).then_inc(loaded, 16)
            sp.dma_start(sinks[:], aps["sinks"].to_broadcast([P, B_HEADS])).then_inc(loaded, 16)
            sp.dma_start(kb[:, CACHE], aps["cache_b_k"]).then_inc(loaded, 16)
            sp.dma_start(vb[:, CACHE], aps["cache_b_v"]).then_inc(loaded, 16)

        @block.gpsimd
        def _(pool):
            pool.wait_ge(loaded, 80)
            pool.affine_select(out=wsT[:], in_=wsT[:], compare_op=ALU.is_ge, fill=0.0, base=0,
                               pattern=[[0, A_GROUPS], [1, P]], channel_multiplier=-1).then_inc(wmask, 1)

        @block.scalar
        def _(act):
            for n in range(NT + 1):
                w = DEC if n == OWN else P
                act.wait_ge(kt_done, n + 1)
                act.copy(kT[:, n, 0:w], banks[4 + n % 2][:, 0:w]).then_inc(kt_read, 1)

            def q_copy(t):
                r = rows(t)
                act.wait_ge(qt_done, t + 1)
                if t >= 2:
                    act.wait_ge(s_done, t - 1)
                act.copy(qT[:, t % 2, :, 0:r], banks[7][:].rearrange("p (b q) -> p b q", q=P)[:, :, 0:r]).then_inc(qt_read, 1)

            def softmax(t):
                r, nk = rows(t), nkeys(t)
                for h in range(B_HEADS):
                    act.wait_ge(s_read, B_HEADS * t + h + 1)
                    if t >= 1 and h == 0:
                        act.wait_ge(pt_done, 4 * t)
                    act.activation(E[0:r, h, 0:nk], S[0:r, h, 0:nk], ACT.Exp, bias=nm[0:r, t % 2, h:h + 1], scale=-1.0,
                                   accum_out=rs[0:r, t % 2, h:h + 1]).then_inc(e_done, 1)
                act.wait_ge(es_done, t + 1)
                act.activation(ee[0:r, t % 2], es[0:r, t % 2], ACT.Exp).then_inc(ee_done, 1)

            def p_copy(t):
                r = rows(t)
                for n in range(4):
                    act.wait_ge(pt_done, 4 * t + n + 1)
                    if t >= 1 and n == 0:
                        act.wait_ge(o_done, t)
                    bank = banks[4 + n % 2][:].rearrange("p (h b q) -> p h b q", h=2, b=2)
                    if t == SAMPLE:
                        act.copy(pT[:, 2 * n:2 * n + 2, 0, 0:r], bank[:, :, 0, 0:r])
                        act.copy(pT[0:DEC, 2 * n:2 * n + 2, 1, 0:r], bank[0:DEC, :, 1, 0:r]).then_inc(pt_read, 1)
                    else:
                        nb = nblocks(t)
                        act.copy(pT[:, 2 * n:2 * n + 2, 0:nb, 0:r], bank[:, :, 0:nb, 0:r]).then_inc(pt_read, 1)

            q_copy(0)
            softmax(0)
            for t in range(NT):
                if t + 1 < NT:
                    q_copy(t + 1)
                p_copy(t)
                if t + 1 < NT:
                    softmax(t + 1)

        @block.vector
        def _(dve):
            dve.memset(mask[:], 0.0).then_inc(masks, 1)
            dve.wait_ge(masks, 1)
            dve.memset(mask[0:CHUNK, 0, CHUNK:P], MASKED)
            dve.memset(mask[0:CHUNK, 1, 3 * CHUNK:], MASKED)
            dve.memset(mask[CHUNK:P, 1, 0:CHUNK], MASKED).then_inc(masks, 1)
            dve.wait_ge(loaded, 80)
            dve.tensor_scalar(nsinks[:], sinks[:], -1.0, None, ALU.mult).then_inc(ns_made, 1)
            dve.wait_ge(masks, 2)
            dve.wait_ge(ns_made, 1)

            def gate(n):
                dve.wait_ge(gate_done, n + 1)
                if n < A_GROUPS:
                    u = A[:, 0:NP_TILES, n * A_GD:(n + 1) * A_GD]
                    dve.scalar_tensor_tensor(out=u, in0=banks[n % 2 + 2][:].rearrange("p (t c) -> p t c", c=A_GD),
                                             scalar=bs[:, n:n + 1], in1=u, op0=ALU.add, op1=ALU.mult).then_inc(gate_read, 1)
                else:
                    for g in range(A_GROUPS):
                        u = A[0:DEC, SAMPLE, g * A_GD:(g + 1) * A_GD]
                        ins = dve.scalar_tensor_tensor(out=u, in0=banks[n % 2 + 2][0:DEC, g * A_GD:(g + 1) * A_GD],
                                                       scalar=bs[0:DEC, g:g + 1], in1=u, op0=ALU.add, op1=ALU.mult)
                    ins.then_inc(gate_read, 1)

            def scores(t):
                r, nk = rows(t), nkeys(t)
                m = mask[0:r, min(t, 1) if t < SAMPLE else 2, 0:nk]
                dve.wait_ge(s_done, t + 1)
                if t >= 1:
                    dve.wait_ge(e_done, B_HEADS * t)
                for h in range(B_HEADS):
                    kv, g = divmod(h, 4)
                    src = banks[2 * kv + g // 2][0:r, (g % 2) * 2 * P:(g % 2) * 2 * P + nk]
                    dve.tensor_tensor_reduce(S[0:r, h, 0:nk], src, m, -HD ** -0.5, nsinks[0:r, h:h + 1],
                                             ALU.add, ALU.min, nm[0:r, t % 2, h:h + 1]).then_inc(s_read, 1)
                dve.wait_ge(s_read, B_HEADS * t + B_HEADS)
                dve.tensor_tensor(es[0:r, t % 2], sinks[0:r], nm[0:r, t % 2], ALU.add).then_inc(es_done, 1)

            def outputs(t):
                r = rows(t)
                dve.wait_ge(ee_done, t + 1)
                dve.wait_ge(e_done, B_HEADS * (t + 1))
                dve.tensor_tensor(den[0:r, t % 2], rs[0:r, t % 2], ee[0:r, t % 2], ALU.add).then_inc(den_made, 1)
                dve.wait_ge(den_made, t + 1)
                if t >= 2:
                    dve.wait_ge(o_read, t - 1)
                dve.reciprocal(rden[0:r, t % 2], den[0:r, t % 2]).then_inc(rden_made, 1)
                dve.wait_ge(rden_made, t + 1)
                dve.wait_ge(o_done, t + 1)
                dve.tensor_tensor(A[0:r, t, A_WIDTH:D].rearrange("p (h d) -> p h d", d=HD),
                                  banks[6][0:r].rearrange("p (h d) -> p h d", d=HD),
                                  rden[0:r, t % 2].unsqueeze(2).to_broadcast([r, B_HEADS, HD]), ALU.mult).then_inc(o_read, 1)

            for n in range(A_GROUPS + 1):
                gate(n)
            scores(0)
            for t in range(NT):
                if t + 1 < NT:
                    scores(t + 1)
                outputs(t)

        @block.tensor
        def _(pe):
            pe.wait_ge(loaded, 80)
            for n in range(NT + 1):
                r = DEC if n == OWN else P
                if n >= 2:
                    pe.wait_ge(kt_read, n - 1)
                pe.transpose(banks[4 + n % 2][:, 0:r], kb[0:r, n], ident[0:r, 0:r]).then_inc(kt_done, 1)
            pe.wait_ge(wmask, 1)
            for n in range(A_GROUPS + 1):
                if n >= 2:
                    pe.wait_ge(gate_read, n - 1)
                out = banks[n % 2 + 2]
                if n < A_GROUPS:
                    mm = pe.matmul(out[:], wsT[:, n], va[:, 0:NP_TILES, n * A_GD:(n + 1) * A_GD], start=True, stop=True)
                else:
                    for g in range(A_GROUPS):
                        mm = pe.matmul(out[0:DEC, g * A_GD:(g + 1) * A_GD], wsT[0:DEC, g, 0:DEC],
                                       va[0:DEC, SAMPLE, g * A_GD:(g + 1) * A_GD], start=True, stop=True)
                mm.then_inc(gate_done, 1)

            def q_transpose(t):
                r = rows(t)
                if t >= 1:
                    pe.wait_ge(qt_read, t)
                for b in range(4):
                    mm = pe.transpose(banks[7][:, b * P:b * P + r], A[0:r, t, A_WIDTH + b * P:A_WIDTH + (b + 1) * P],
                                      ident[0:r, 0:r])
                mm.then_inc(qt_done, 1)

            def scores(t):
                r, nk = rows(t), nkeys(t)
                pe.wait_ge(qt_read, t + 1)
                pe.wait_ge(kt_read, NT + 1)
                if t >= 1:
                    pe.wait_ge(s_read, B_HEADS * t)
                else:
                    pe.wait_ge(gate_read, A_GROUPS + 1)
                for b in range(4):
                    for half in range(2):
                        mm = pe.matmul(banks[2 * half + b // 2][0:r, (b % 2) * 2 * P:(b % 2) * 2 * P + nk],
                                       qT[half * HD:half * HD + HD, t % 2, b, 0:r], kT_keys(t, half), start=True, stop=True)
                mm.then_inc(s_done, 1)

            def p_transpose(t):
                r = rows(t)
                for n in range(4):
                    pe.wait_ge(e_done, B_HEADS * t + 2 * n + 2)
                    if 4 * t + n >= 2:
                        pe.wait_ge(pt_read, 4 * t + n - 1)
                    for hh in range(2):
                        for b in range(nblocks(t)):
                            w = kwidth(t, b)
                            at = (2 * hh + b) * P
                            mm = pe.transpose(banks[4 + n % 2][0:w, at:at + r], E[0:r, 2 * n + hh, b * P:b * P + w],
                                              ident[0:r, 0:r])
                    mm.then_inc(pt_done, 1)

            def values(t):
                r, nb = rows(t), nblocks(t)
                pe.wait_ge(pt_read, 4 * t + 4)
                if t >= 1:
                    pe.wait_ge(o_read, t)
                for h in range(B_HEADS):
                    kv = h // 4
                    for b in range(nb):
                        w = kwidth(t, b)
                        mm = pe.matmul(banks[6][0:r, h * HD:(h + 1) * HD], pT[0:w, h, b, 0:r],
                                       vb[0:w, first_slot(t) + b, kv * HD:(kv + 1) * HD], start=(b == 0), stop=(b == nb - 1))
                mm.then_inc(o_done, 1)

            q_transpose(0)
            scores(0)
            for t in range(NT):
                if t + 1 < NT:
                    q_transpose(t + 1)
                    scores(t + 1)
                p_transpose(t)
                values(t)


class Turn:

    def __init__(self, nc, c, tag, name, A, xt_hi, xt_lo, ident, bank_of):
        self.A, self.hi, self.lo, self.ident, self.bank_of = A, xt_hi, xt_lo, ident, bank_of
        self.turned = c(nc.semaphore(tag + f"{name}_turned"))
        self.hi_made = c(nc.semaphore(tag + f"{name}_hi_made"))

    def transpose(self, pe, n):
        t, h = divmod(n, 2)
        r = rows(t)
        for b in range(4):
            c0 = (4 * h + b) * P
            mm = pe.transpose(self.bank_of(n)[:, b * P:b * P + r], self.A[0:r, t, c0:c0 + P], self.ident[0:r, 0:r])
        mm.then_inc(self.turned, 1)

    def view(self, x, n):
        t, h = divmod(n, 2)
        a, b = tok(t)
        return x[:, 4 * h:4 * h + 4, a:b]

    def bank(self, n):
        return self.bank_of(n)[:].rearrange("p (b q) -> p b q", q=P)[:, :, 0:rows(n // 2)]

    def high(self, act, n):
        act.wait_ge(self.turned, n + 1)
        act.copy(self.view(self.hi, n), self.bank(n)).then_inc(self.hi_made, 1)

    def low(self, dve, n, freed):
        dve.wait_ge(self.hi_made, n + 1)
        dve.tensor_tensor(self.view(self.lo, n), self.bank(n), self.view(self.hi, n), ALU.subtract).then_inc(freed, 1)


def block_out(nc, aps, layer, resid, w_out, A, xt_hi, xt_lo, ident, mhalf, ps):
    tag = f"out{layer}_"
    banks = [ps[:, i] for i in range(8)]
    with ExitStack() as s:
        c = s.enter_context
        chunks = [(0, COLS), (COLS, COLS)]
        done = c(nc.semaphore(tag + "products_done"))
        st = Stream(nc, c, tag, w_out, chunks, done)
        ln = Norm(nc, c, tag, "ln1", D, aps["ln1_g"][layer:layer + 1], aps["ln1_b"][layer:layer + 1])
        NR = 4
        xr = c(nc.sbuf_tensor(tag + "resid", [P, NR, COLS], F32))
        r_arrived = [c(nc.semaphore(tag + f"resid_arrived{i}")) for i in range(NR)]
        freed = c(nc.semaphore(tag + "banks_freed"))
        scaled = c(nc.semaphore(tag + "alpha_scaled"))
        H2 = 2 * NT
        first = Turn(nc, c, tag, "mix", A, xt_hi, xt_lo, ident, lambda n: banks[n % 8])
        second = Turn(nc, c, tag, "x1", A, xt_hi, xt_lo, ident, lambda n: banks[(2 * H2 + n) % 8])
        block = c(nc.Block())

        @block.sync
        def _(sp):
            def load_resid(g):
                j, t = divmod(g, NT)
                a, b = tok(t)
                if g >= NR:
                    sp.wait_ge(freed, H2 + g - NR + 1)
                sp.dma_start(xr[0:b - a, g % NR], resid[a:b, j * COLS:(j + 1) * COLS]).then_inc(r_arrived[g % NR], 16)

            for n in range(W_SLOTS + 2):
                st.load(sp, n)
                if n == 2:
                    ln.load(sp)
            for g in range(NT + NR - 1):
                load_resid(g)
            for n in range(W_SLOTS + 2, st.n):
                st.load(sp, n)
            for g in range(NT + NR - 1, H2):
                load_resid(g)

        @block.gpsimd
        def _(pool):
            for t in range(NT + 1):
                if t < NT:
                    ln.rsqrt(pool, mhalf, t)
                if t >= 1:
                    ln.offset(pool, A[:, t - 1], t - 1)

        @block.scalar
        def _(act):
            for n in range(H2):
                first.high(act, n)
                if n % 4 == 3 and n // 4 < W_SLOTS:
                    st.split_hi(act, n // 4)
            for n in range(H2 // 4, W_SLOTS):
                st.split_hi(act, n)
            for n in st.next_pieces(0):
                st.split_hi(act, n)
            for t in range(NT):
                ln.normalise(act, A[:, t], t)
            act.wait_ge(done, H2)
            for n in range(H2):
                second.high(act, n)
                if n % 2:
                    t = n // 2
                    r = rows(t)
                    act.mul(A[0:r, t], A[0:r, t], ALPHA).then_inc(scaled, 1)

        @block.vector
        def _(dve):
            for n in range(H2):
                first.low(dve, n, freed)
                if n % 4 == 3 and n // 4 < W_SLOTS:
                    st.split_lo(dve, n // 4)
            for n in range(H2 // 4, W_SLOTS):
                st.split_lo(dve, n)
            for g in range(H2):
                j, t = divmod(g, NT)
                r = rows(t)
                if t == NT - 1:
                    for n in st.next_pieces(j):
                        st.split_lo(dve, n)
                dve.wait_ge(r_arrived[g % NR], 16 * (g // NR + 1))
                dve.wait_ge(done, g + 1)
                dve.scalar_tensor_tensor(out=A[0:r, t, j * COLS:(j + 1) * COLS], in0=xr[0:r, g % NR], scalar=ALPHA,
                                         in1=banks[(H2 + g) % 8][0:r], op0=ALU.mult, op1=ALU.add).then_inc(freed, 1)
                if j == 1:
                    dve.wait_ge(freed, H2 + g + 1)
                    ln.statistics(dve, A[:, t], t)
                    if t >= 1:
                        ln.scale(dve, A[:, t - 1], t - 1)
            ln.scale(dve, A[:, NT - 1], NT - 1)
            for n in range(H2):
                second.low(dve, n, freed)

        @block.tensor
        def _(pe):
            for n in range(H2):
                if n >= 8:
                    pe.wait_ge(freed, n - 7)
                first.transpose(pe, n)
            for g in range(H2):
                j, t = divmod(g, NT)
                pe.wait_ge(freed, max(H2 + g - 7, 2 * t + 2 if j == 0 else 0))
                st.product(pe, banks[(H2 + g) % 8], t, j, xt_hi, xt_lo)
            for n in range(H2):
                pe.wait_ge(freed, 2 * H2 + n - 7)
                pe.wait_ge(ln.done, n // 2 + 1)
                second.transpose(pe, n)


def block_mlp(nc, aps, layer, A, xt_hi, xt_lo, ident, mhalf, ps):
    w1 = aps["ff_w1"][layer].rearrange("(k p) (n f) -> p k n f", p=P, f=FC)
    w2 = aps["ff_w2"][layer].rearrange("(n f p) d -> p n f d", p=P, f=FT)
    NR = len(RANGES)
    G1 = FT * NR
    G2 = 2 * NT
    PAIRS = (N_FC - 4) // 2
    tag = f"mlp{layer}_"
    banks = [ps[:, i] for i in range(8)]
    with ExitStack() as s:
        c = s.enter_context
        sb = lambda name, shape, dt=F32: c(nc.sbuf_tensor(tag + name, shape, dt))
        sem = lambda name: c(nc.semaphore(tag + name))
        w1_raw, w1_hi, w1_lo = sb("w1_raw", [P, KT, FC]), sb("w1_hi", [P, KT, FC], F32R), sb("w1_lo", [P, KT, FC], F32R)
        w2_raw, w2_hi, w2_lo = sb("w2_raw", [P, FT, D]), sb("w2_hi", [P, FT, D], F32R), sb("w2_lo", [P, FT, D], F32R)
        h_hi, h_lo = sb("h_hi", [P, 2, FT, TOK], F32R), sb("h_lo", [P, 2, FT, TOK], F32R)
        h_raw = sb("h_raw", [P, 2, 384])
        ln = Norm(nc, c, tag, "ln2", D, aps["ln2_g"][layer:layer + 1], aps["ln2_b"][layer:layer + 1])
        w1_in, w2_in = sem("w1_arrived"), sem("w2_arrived")
        w1_hi_made, w1_lo_made = sem("w1_hi_made"), sem("w1_lo_made")
        w2_hi_made, w2_lo_made = sem("w2_hi_made"), sem("w2_lo_made")
        h_done, relu_done, square_done = sem("h_product_done"), sem("relu_done"), sem("square_done")
        h_hi_made, h_lo_made = sem("h_hi_made"), sem("h_lo_made")
        y_done, y_read = sem("y_product_done"), sem("y_banks_read")
        stored = sem("outputs_stored")
        turn = Turn(nc, c, tag, "x2", A, xt_hi, xt_lo, ident, lambda n: banks[4 + n % 4])
        reads_before = lambda g: g - 3 if g >= 4 else max(x for x in range(G2) if x % 4 == g % 4) + 1 - G2
        block = c(nc.Block())

        def load_w1(sp, i, wait):
            if wait:
                sp.wait_ge(w1_lo_made, i)
            sp.dma_start(w1_raw[:], w1[:, :, bass.ds(i, 1)].rearrange("p k n f -> p k (n f)")).then_inc(w1_in, 16)

        def load_w2(sp, i, wait):
            if wait:
                sp.wait_ge(w2_lo_made, i)
            sp.dma_start(w2_raw[:], w2[:, bass.ds(i, 1)].rearrange("p n f d -> p (n f) d")).then_inc(w2_in, 16)

        @block.sync
        def _(sp):
            load_w1(sp, 0, False)
            load_w2(sp, 0, False)
            ln.load(sp)
            with sp.Fori(1, N_FC) as i:
                load_w1(sp, i, True)
                load_w2(sp, i, True)
            for t in range(NT):
                a, b = tok(t)
                sp.wait_ge(ln.done, t + 1)
                if layer == 0:
                    dst = aps["x2"][a:b]
                else:
                    dst = aps["y_prompt"][a:b] if t < SAMPLE else aps["y_sample"]
                sp.dma_start(dst, A[0:b - a, t]).then_inc(stored, 16)
            sp.wait_ge(stored, 16 * NT)

        @block.gpsimd
        def _(pool):
            for t in range(NT + 1):
                if t < NT:
                    ln.rsqrt(pool, mhalf, t)
                if t >= 1:
                    ln.offset(pool, A[:, t - 1], t - 1)

        def w1_high(act, i, wait):
            act.wait_ge(w1_in, 16 * i + 16)
            if wait:
                act.wait_ge(h_done, G1 * i)
            act.copy(w1_hi[:], w1_raw[:]).then_inc(w1_hi_made, 1)

        def w2_high(act, i, wait):
            act.wait_ge(w2_in, 16 * i + 16)
            if wait:
                act.wait_ge(y_done, G2 * i)
            act.copy(w2_hi[:], w2_raw[:]).then_inc(w2_hi_made, 1)

        def h_high(act, i, buf, first):
            if not first:
                act.wait_ge(y_done, G2 * (i - 1))
            for g in range(G1):
                f, n = divmod(g, NR)
                a, b = RANGES[n]
                raw = h_raw[:, g % 2, 0:b - a]
                act.wait_ge(h_done, G1 * i + g + 1)
                if G1 * i + g >= 2 if first else True:
                    act.wait_ge(h_lo_made, G1 * i + g - 1)
                act.activation(raw, banks[g % 3][:, 0:b - a], ACT.Relu).then_inc(relu_done, 1)
                act.wait_ge(relu_done, G1 * i + g + 1)
                act.activation(raw, raw, ACT.Square).then_inc(square_done, 1)
                act.wait_ge(square_done, G1 * i + g + 1)
                act.copy(h_hi[:, buf, f, a:b], raw).then_inc(h_hi_made, 1)

        @block.scalar
        def _(act):
            w1_high(act, 0, False)
            w2_high(act, 0, False)
            h_high(act, 0, 0, True)
            w1_high(act, 1, True)
            h_high(act, 1, 1, True)
            w1_high(act, 2, True)
            w2_high(act, 1, True)
            with act.Fori(0, PAIRS) as m:
                for u in range(2):
                    i = 2 * m + (u + 2)
                    h_high(act, i, u, False)
                    w1_high(act, i + 1, True)
                    w2_high(act, i, True)
            h_high(act, N_FC - 2, 0, False)
            w1_high(act, N_FC - 1, True)
            w2_high(act, N_FC - 2, True)
            h_high(act, N_FC - 1, 1, False)
            w2_high(act, N_FC - 1, True)
            for t in range(NT):
                ln.normalise(act, A[:, t], t)
            if layer == 0:
                for n in range(G2):
                    turn.high(act, n)

        def w1_low(dve, i):
            dve.wait_ge(w1_hi_made, i + 1)
            dve.tensor_tensor(w1_lo[:], w1_raw[:], w1_hi[:], ALU.subtract).then_inc(w1_lo_made, 1)

        def w2_low(dve, i):
            dve.wait_ge(w2_hi_made, i + 1)
            dve.tensor_tensor(w2_lo[:], w2_raw[:], w2_hi[:], ALU.subtract).then_inc(w2_lo_made, 1)

        def h_low(dve, i, buf):
            for g in range(G1):
                f, n = divmod(g, NR)
                a, b = RANGES[n]
                dve.wait_ge(h_hi_made, G1 * i + g + 1)
                dve.tensor_tensor(h_lo[:, buf, f, a:b], h_raw[:, g % 2, 0:b - a], h_hi[:, buf, f, a:b],
                                  ALU.subtract).then_inc(h_lo_made, 1)

        def add_y(dve, i, g):
            t, j = divmod(g, 2)
            r = rows(t)
            dve.wait_ge(y_done, G2 * i + g + 1)
            acc = A[0:r, t, j * COLS:(j + 1) * COLS]
            dve.tensor_tensor(acc, banks[4 + g % 4][0:r], acc, ALU.add).then_inc(y_read, 1)

        @block.vector
        def _(dve):
            w1_low(dve, 0)
            w2_low(dve, 0)
            h_low(dve, 0, 0)
            w1_low(dve, 1)
            h_low(dve, 1, 1)
            w1_low(dve, 2)
            for g in range(G2):
                add_y(dve, 0, g)
            w2_low(dve, 1)
            with dve.Fori(0, PAIRS) as m:
                for u in range(2):
                    i = 2 * m + (u + 2)
                    h_low(dve, i, u)
                    w1_low(dve, i + 1)
                    for g in range(G2):
                        add_y(dve, i - 1, g)
                    w2_low(dve, i)
            h_low(dve, N_FC - 2, 0)
            w1_low(dve, N_FC - 1)
            for g in range(G2):
                add_y(dve, N_FC - 3, g)
            w2_low(dve, N_FC - 2)
            h_low(dve, N_FC - 1, 1)
            for g in range(G2):
                add_y(dve, N_FC - 2, g)
            w2_low(dve, N_FC - 1)
            for g in range(G2):
                add_y(dve, N_FC - 1, g)
                if g % 2:
                    t = g // 2
                    dve.wait_ge(y_read, G2 * (N_FC - 1) + g + 1)
                    ln.statistics(dve, A[:, t], t)
                    if t >= 1:
                        ln.scale(dve, A[:, t - 1], t - 1)
            ln.scale(dve, A[:, NT - 1], NT - 1)
            if layer == 0:
                for n in range(G2):
                    turn.low(dve, n, y_read)

        def first_product(pe, i, buf, prior):
            pe.wait_ge(w1_lo_made, i + 1)
            for g in range(G1):
                f, n = divmod(g, NR)
                a, b = RANGES[n]
                if prior or g >= 3:
                    pe.wait_ge(relu_done, G1 * i + g - 2)
                out = banks[g % 3][:, 0:b - a]
                for k in range(KT):
                    w = slice(f * P, (f + 1) * P)
                    pe.matmul(out, w1_hi[:, k, w], xt_hi[:, k, a:b], start=(k == 0), stop=False)
                    pe.matmul(out, w1_hi[:, k, w], xt_lo[:, k, a:b], start=False, stop=False)
                    mm = pe.matmul(out, w1_lo[:, k, w], xt_hi[:, k, a:b], start=False, stop=(k == KT - 1))
                mm.then_inc(h_done, 1)

        def second_product(pe, i, buf, prior):
            pe.wait_ge(w2_lo_made, i + 1)
            pe.wait_ge(h_lo_made, G1 * i + G1)
            for g in range(G2):
                t, j = divmod(g, 2)
                a, b = tok(t)
                if prior or g >= 4:
                    pe.wait_ge(y_read, G2 * i + reads_before(g))
                out = banks[4 + g % 4][0:b - a]
                d = slice(j * COLS, (j + 1) * COLS)
                for f in range(FT):
                    pe.matmul(out, h_hi[:, buf, f, a:b], w2_hi[:, f, d], start=(f == 0), stop=False)
                    pe.matmul(out, h_hi[:, buf, f, a:b], w2_lo[:, f, d], start=False, stop=False)
                    mm = pe.matmul(out, h_lo[:, buf, f, a:b], w2_hi[:, f, d], start=False, stop=(f == FT - 1))
                mm.then_inc(y_done, 1)

        @block.tensor
        def _(pe):
            first_product(pe, 0, 0, False)
            first_product(pe, 1, 1, True)
            second_product(pe, 0, 0, False)
            with pe.Fori(0, PAIRS + 1) as m:
                for u in range(2):
                    i = 2 * m + (u + 2)
                    first_product(pe, i, u, True)
                    second_product(pe, i - 1, (u + 1) % 2, True)
            second_product(pe, N_FC - 1, 1, True)
            if layer == 0:
                for n in range(G2):
                    pe.wait_ge(y_read, G2 * N_FC + reads_before(n))
                    pe.wait_ge(ln.done, n // 2 + 1)
                    turn.transpose(pe, n)


def ranges_of(numbers):
    found = []
    for n in sorted(numbers):
        if found and found[-1].stop == n:
            found[-1] = range(found[-1].start, n + 1)
        else:
            found.append(range(n, n + 1))
    return found


def block_c_in(nc, aps, A, xt_hi, xt_lo, kc, vc, ki, qi, wi, ps):
    tag = "c_in_"
    banks = [ps[:, i] for i in range(8)]
    with ExitStack() as s:
        c = s.enter_context
        chunks = [(IDX_COL, IDX_W), (0, COLS), (COLS, COLS), (C_Q, 2 * C_KVW)]
        done = c(nc.semaphore(tag + "products_done"))
        st = Stream(nc, c, tag, aps["c_w_in"], chunks, done)
        table = c(nc.sbuf_tensor(tag + "rope_table", [P, NT, P], F32))
        tmp = c(nc.sbuf_tensor(tag + "rope_tmp", [P, 2, 2, 8, HD], F32))
        loaded = c(nc.semaphore(tag + "table_and_caches_arrived"))
        read = c(nc.semaphore(tag + "banks_read"))
        chain = c(nc.semaphore(tag + "vector_chain"))
        stored = c(nc.semaphore(tag + "outputs_stored"))
        block = c(nc.Block())
        finished = ranges_of(nc.released_uncleared_semaphores)
        tiles = lambda x: x.rearrange("(t p) c -> p t c", p=P)
        CACHE = slice(NP_TILES, NP_TILES + 2)
        OWN = NT + 1

        @block.sync
        def _(sp):
            for n in range(W_SLOTS + 2):
                st.load(sp, n)
                if n == 2:
                    sp.dma_start(table[:, 0:NP_TILES], tiles(aps["rope"][0:SEQ])).then_inc(loaded, 16)
                    sp.dma_start(table[0:DEC, SAMPLE], aps["rope"][SEQ:TOK]).then_inc(loaded, 16)
            sp.dma_start(kc[:, CACHE], tiles(aps["cache_c_k"])).then_inc(loaded, 16)
            sp.dma_start(vc[:, CACHE], tiles(aps["cache_c_v"])).then_inc(loaded, 16)
            for h in range(2):
                sp.dma_start(ki[:, CACHE, h * HD:(h + 1) * HD], tiles(aps["cache_c_idx"])).then_inc(loaded, 16)
            for n in range(W_SLOTS + 2, st.n):
                st.load(sp, n)
            sp.wait_ge(read, 4 * NT)
            sp.dma_start(tiles(aps["p_c_k"]), kc[:, 0:NP_TILES]).then_inc(stored, 16)
            sp.dma_start(tiles(aps["p_c_v"]), vc[:, 0:NP_TILES]).then_inc(stored, 16)
            sp.dma_start(tiles(aps["p_c_idx"]), ki[:, 0:NP_TILES, 0:HD]).then_inc(stored, 16)
            sp.dma_start(aps["s_c_k"], kc[0:DEC, OWN]).then_inc(stored, 16)
            sp.dma_start(aps["s_c_v"], vc[0:DEC, OWN]).then_inc(stored, 16)
            sp.dma_start(aps["s_c_idx"], ki[0:DEC, OWN, 0:HD]).then_inc(stored, 16)
            sp.wait_ge(stored, 96)
            sp.wait_ge(loaded, 96)

        @block.gpsimd
        def _(pool):
            for sem_range in finished:
                pool.sem_clear(sem_range)

        @block.scalar
        def _(act):
            for n in range(W_SLOTS):
                st.split_hi(act, n)
            for j in range(len(chunks)):
                for n in st.next_pieces(j):
                    st.split_hi(act, n)

        @block.vector
        def _(dve):
            links = [0]

            def link(ins):
                links[0] += 1
                ins.then_inc(chain, 1)
                dve.wait_ge(chain, links[0])

            for n in range(W_SLOTS):
                st.split_lo(dve, n)
            dve.wait_ge(loaded, 96)
            for j in range(len(chunks)):
                for t in range(NT):
                    g, r = j * NT + t, rows(t)
                    turn = tmp[0:r, g % 2]
                    slot = t if t < SAMPLE else OWN
                    bank = banks[g % 8][0:r]
                    if t == NT - 1:
                        for n in st.next_pieces(j):
                            st.split_lo(dve, n)
                    dve.wait_ge(done, g + 1)
                    if g >= 2:
                        dve.wait_ge(read, g - 1)
                    if j == 0:
                        n = IDX_HEADS + 1
                        rope(dve, link, bank[:, 0:n * HD].rearrange("p (h d) -> p h d", d=HD), table[0:r, t], turn, n)
                        dve.tensor_tensor(qi[0:r, t].rearrange("p (h d) -> p h d", d=HD), turn[:, 0, 0:IDX_HEADS],
                                          turn[:, 1, 0:IDX_HEADS], ALU.add)
                        twice = lambda i: turn[:, i, IDX_HEADS:IDX_HEADS + 1].to_broadcast([r, 2, HD])
                        dve.tensor_tensor(ki[0:r, slot].rearrange("p (h d) -> p h d", d=HD), twice(0), twice(1), ALU.add)
                        dve.tensor_copy(wi[0:r, t], bank[:, n * HD:IDX_W]).then_inc(read, 1)
                    elif j < 3:
                        rope(dve, link, bank.rearrange("p (h d) -> p h d", d=HD), table[0:r, t], turn, 8)
                        out = A[0:r, t, (j - 1) * COLS:j * COLS].rearrange("p (g kv d) -> p kv g d", kv=2, d=HD)
                        two = lambda i: turn[:, i].rearrange("p (kv g) d -> p kv g d", kv=2)
                        dve.tensor_tensor(out, two(0), two(1), ALU.add).then_inc(read, 1)
                    else:
                        rope(dve, link, bank[:, 0:C_KVW].rearrange("p (h d) -> p h d", d=HD), table[0:r, t], turn, C_KV)
                        dve.tensor_tensor(kc[0:r, slot].rearrange("p (h d) -> p h d", d=HD), turn[:, 0, 0:C_KV],
                                          turn[:, 1, 0:C_KV], ALU.add)
                        dve.tensor_copy(vc[0:r, slot], bank[:, C_KVW:2 * C_KVW]).then_inc(read, 1)

        @block.tensor
        def _(pe):
            for j in range(len(chunks)):
                for t in range(NT):
                    g = j * NT + t
                    if g >= 8:
                        pe.wait_ge(read, g - 7)
                    st.product(pe, banks[g % 8], t, j, xt_hi, xt_lo)


def block_c_mixer(nc, aps, A, kc, vc, ki, qi, wi, ident, ps):
    tag = "c_mix_"
    NS = NT + 2
    OWN = NT + 1
    HP = C_HEADS
    with ExitStack() as s:
        c = s.enter_context
        sb = lambda name, shape: c(nc.sbuf_tensor(tag + name, shape, F32))
        sem = lambda name: c(nc.semaphore(tag + name))
        kT = sb("kT", [P, 2, NS * P])
        kiT = sb("kiT", [P, NS * P])
        qT = sb("qT", [P, 8, P])
        qiT = sb("qiT", [P, 2, P])
        idx = sb("idx_scores", [P, 2, SEQ])
        early = sb("early_mask", [P, 2 * P])
        rel = sb("relu", [P, 2, SEQ])
        S = sb("scores", [P, 2, SEQ])
        E = sb("probs", [P, 2, SEQ])
        pT = sb("probs_T", [P, 2, 8, P])
        top8 = sb("top8", [P, 8])
        nm = sb("minus_max", [P, 2, HP])
        rs = sb("row_sum", [P, 2, HP])
        rden = sb("rden", [P, 2, HP])
        masks = sem("masks_made")
        turned, copied = sem("transposed"), sem("transposes_copied")
        i_done, relu_done, mixed = sem("idx_product_done"), sem("relu_done"), sem("idx_head_added")
        chain = sem("vector_chain")
        s_done, s_read, e_done = sem("scores_done"), sem("scores_read"), sem("probs_ready")
        o_done, o_read, rden_made = sem("outputs_done"), sem("outputs_read"), sem("rden_made")
        block = c(nc.Block())
        banks = [ps[:, i] for i in range(8)]

        nkeys = lambda t: (t + 1) * P if t < SAMPLE else PAST + DEC
        key0 = lambda t: 0 if t < SAMPLE else NP_TILES * P
        slot0 = lambda t: 0 if t < SAMPLE else NP_TILES
        blocks = lambda t: -(-nkeys(t) // P)
        width = lambda t, b: min(P, nkeys(t) - b * P)
        groups = lambda t: -(-blocks(t) // 4)
        rounds = lambda t: (TOPK if t < SAMPLE else TOPK_SAMPLE) // 8
        ranked = lambda t: 2 <= t < NT
        wide = lambda half, r, n: ps[0:r, 2 * half:2 * half + 2].rearrange("p b c -> p (b c)")[:, 0:n]
        head = lambda m: (m // 8, (m % 8) // 2, m % 2)
        place = lambda m: head(m)[0] * 8 + head(m)[2] * 4 + head(m)[1]
        KSETS = [(kc, kT[:, 0], 0), (kc, kT[:, 1], P), (ki, kiT, 0)]
        KGROUPS = [(x, g) for x in range(3) for g in range(3)]

        @block.gpsimd
        def _(pool):
            pool.memset(early[:], 0.0).then_inc(masks, 1)
            pool.wait_ge(masks, 1)
            pool.memset(early[0:CHUNK, 3 * CHUNK:], MASKED).then_inc(masks, 1)

        def each_slot(g):
            return [(sl, DEC if sl == OWN else P) for sl in range(4 * g, min(4 * g + 4, NS))]

        @block.scalar
        def _(act):
            n = [0]

            def copy(out, bank):
                act.wait_ge(turned, n[0] + 1)
                act.copy(out, bank).then_inc(copied, 1)
                n[0] += 1

            for x, g in KGROUPS:
                w = sum(r for _, r in each_slot(g))
                copy(KSETS[x][1][:, 4 * g * P:4 * g * P + w], banks[4 + n[0] % 2][:, 0:w])

            def quads(bank, r):
                return bank.rearrange("p (b q) -> p b q", q=P)[:, :, 0:r]

            def queries(t):
                r = rows(t)
                if t >= 1:
                    act.wait_ge(s_done, HP * t)
                for h in range(2):
                    copy(qT[:, 4 * h:4 * h + 4, 0:r], quads(banks[4 + n[0] % 2], r))

            def rank(t):
                r, nk = rows(t), nkeys(t)
                copy(qiT[:, :, 0:r], quads(banks[4 + n[0] % 2], r)[:, 0:2])
                for h in range(IDX_HEADS):
                    x = IDX_HEADS * (t - 2) + h
                    act.wait_ge(i_done, x + 1)
                    if x >= 2:
                        act.wait_ge(mixed, x - 1)
                    act.activation(rel[0:r, h % 2, 0:nk], wide(h % 2, r, nk), ACT.Relu,
                                   scale=(HD * IDX_HEADS) ** -0.5).then_inc(relu_done, 1)

            def exp(t, m):
                r, nk, x = rows(t), nkeys(t), HP * t + m
                act.wait_ge(s_read, x + 1)
                act.activation(E[0:r, x % 2, 0:nk], S[0:r, x % 2, 0:nk], ACT.Exp, bias=nm[0:r, t % 2, place(m):place(m) + 1],
                               scale=-1.0, accum_out=rs[0:r, t % 2, place(m):place(m) + 1]).then_inc(e_done, 1)

            def copy_probs(t, m):
                r, x = rows(t), HP * t + m
                if x >= 2:
                    act.wait_ge(o_done, x - 1)
                for g in range(groups(t)):
                    nb = min(4, blocks(t) - 4 * g)
                    bank = quads(banks[4 + n[0] % 2], r)
                    last = width(t, 4 * g + nb - 1)
                    if last == P:
                        copy(pT[:, x % 2, 4 * g:4 * g + nb, 0:r], bank[:, 0:nb])
                    else:
                        act.wait_ge(turned, n[0] + 1)
                        act.copy(pT[:, x % 2, 4 * g:4 * g + nb - 1, 0:r], bank[:, 0:nb - 1])
                        copy(pT[0:last, x % 2, 4 * g + nb - 1, 0:r], bank[0:last, nb - 1])

            for t in range(NT):
                queries(t)
                if ranked(t + 1):
                    rank(t + 1)
                exp(t, 0)
                for m in range(HP):
                    if m + 1 < HP:
                        exp(t, m + 1)
                    copy_probs(t, m)

        @block.vector
        def _(dve):
            links = [0]

            def link(ins):
                links[0] += 1
                ins.then_inc(chain, 1)
                dve.wait_ge(chain, links[0])

            def mix(t):
                r, nk = rows(t), nkeys(t)
                out = idx[0:r, t % 2, 0:nk]
                if ranked(t - 2):
                    dve.wait_ge(s_read, HP * (t - 1))
                for h in range(IDX_HEADS):
                    x = IDX_HEADS * (t - 2) + h
                    dve.wait_ge(relu_done, x + 1)
                    src, w = rel[0:r, h % 2, 0:nk], wi[0:r, t, h:h + 1]
                    if h == 0:
                        dve.tensor_scalar(out, src, w, None, ALU.mult).then_inc(mixed, 1)
                    else:
                        dve.scalar_tensor_tensor(out=out, in0=src, scalar=w, in1=out, op0=ALU.mult, op1=ALU.add).then_inc(mixed, 1)
                    dve.wait_ge(mixed, x + 1)
                if t < SAMPLE:
                    link(dve.memset(idx[0:CHUNK, t % 2, nk - CHUNK:nk], BARRED))

            def take(t):
                r, v = rows(t), idx[0:rows(t), t % 2, 0:nkeys(t)]
                link(dve.max(top8[0:r], v))
                link(dve.match_replace(v, top8[0:r], v, TAKEN))

            def close(t):
                v = idx[0:rows(t), t % 2, 0:nkeys(t)]
                link(dve.tensor_scalar(v, v, TAKEN, MASKED, ALU.not_equal, ALU.mult))

            def scores(t, m):
                r, nk, x = rows(t), nkeys(t), HP * t + m
                mask = idx[0:r, t % 2, 0:nk] if ranked(t) else early[0:r, 2 * P - nk:2 * P]
                dve.wait_ge(s_done, x + 1)
                if x >= 2:
                    dve.wait_ge(e_done, x - 1)
                dve.tensor_tensor_reduce(S[0:r, x % 2, 0:nk], wide(m % 2, r, nk), mask, -HD ** -0.5, LARGE,
                                         ALU.add, ALU.min, nm[0:r, t % 2, place(m):place(m) + 1]).then_inc(s_read, 1)

            def outputs(t, b):
                r = rows(t)
                dve.wait_ge(e_done, HP * t + 8 * b + 8)
                if t >= 2:
                    dve.wait_ge(o_read, 2 * (t - 2) + b + 1)
                dve.reciprocal(rden[0:r, t % 2, 8 * b:8 * b + 8], rs[0:r, t % 2, 8 * b:8 * b + 8]).then_inc(rden_made, 1)
                dve.wait_ge(rden_made, 2 * t + b + 1)
                dve.wait_ge(o_done, HP * t + 8 * b + 8)
                dve.tensor_tensor(A[0:r, t, b * COLS:(b + 1) * COLS].rearrange("p (h d) -> p h d", d=HD),
                                  banks[6 + b][0:r].rearrange("p (h d) -> p h d", d=HD),
                                  rden[0:r, t % 2, 8 * b:8 * b + 8].unsqueeze(2).to_broadcast([r, 8, HD]),
                                  ALU.mult).then_inc(o_read, 1)

            dve.wait_ge(masks, 2)
            for t in range(NT):
                ahead = t + 1
                if ranked(ahead):
                    mix(ahead)
                left = rounds(ahead) if ranked(ahead) else 0
                for m in range(HP):
                    scores(t, m)
                    for _ in range(-(-left // (HP - m)) if left else 0):
                        take(ahead)
                        left -= 1
                    if m == 3 and t >= 1:
                        outputs(t - 1, 1)
                    if m == 11:
                        outputs(t, 0)
                if ranked(ahead):
                    close(ahead)
            outputs(NT - 1, 1)

        @block.tensor
        def _(pe):
            n = [0]

            def group(pairs):
                bank = banks[4 + n[0] % 2]
                if n[0] >= 2:
                    pe.wait_ge(copied, n[0] - 1)
                for at, src, r in pairs:
                    mm = pe.transpose(bank[0:src.shape[1], at:at + r], src, ident[0:r, 0:r])
                mm.then_inc(turned, 1)
                n[0] += 1

            for x, g in KGROUPS:
                src, _, c0 = KSETS[x]
                group([((sl % 4) * P, src[0:r, sl, c0:c0 + P], r) for sl, r in each_slot(g)])

            def queries(t):
                r = rows(t)
                for h in range(2):
                    group([(b * P, A[0:r, t, (4 * h + b) * P:(4 * h + b + 1) * P], r) for b in range(4)])

            def product(half, r, nk, q, k, done):
                for c0 in range(0, nk, COLS):
                    w = min(COLS, nk - c0)
                    mm = pe.matmul(ps[0:r, 2 * half + c0 // COLS, 0:w], q, k[:, c0:c0 + w], start=True, stop=True)
                mm.then_inc(done, 1)

            def rank(t):
                r, nk = rows(t), nkeys(t)
                group([(b * P, qi[0:r, t, b * P:(b + 1) * P], r) for b in range(2)])
                pe.wait_ge(copied, n[0])
                for h in range(IDX_HEADS):
                    half = h % 2
                    p0 = half * HD
                    x = IDX_HEADS * (t - 2) + h
                    if h < 2:
                        pe.wait_ge(s_read, HP * (t - 1))
                    else:
                        pe.wait_ge(relu_done, x - 1)
                    product(half, r, nk, qiT[p0:p0 + HD, h // 2, 0:r], kiT[p0:p0 + HD, key0(t):key0(t) + nk], i_done)

            def scores(t, m):
                r, nk, x = rows(t), nkeys(t), HP * t + m
                b, g, half = head(m)
                p0 = half * HD
                if m < 2 and ranked(t + 1):
                    pe.wait_ge(relu_done, IDX_HEADS * (t - 1) + 4)
                elif x >= 2:
                    pe.wait_ge(s_read, x - 1)
                product(half, r, nk, qT[p0:p0 + HD, 4 * b + g, 0:r], kT[p0:p0 + HD, b, key0(t):key0(t) + nk], s_done)

            def transposes(t, m):
                r, x = rows(t), HP * t + m
                pe.wait_ge(e_done, x + 1)
                for g in range(groups(t)):
                    group([(b % 4 * P, E[0:r, x % 2, b * P:b * P + width(t, b)], r)
                           for b in range(4 * g, min(4 * g + 4, blocks(t)))])

            def values(t, m, at):
                r, x = rows(t), HP * t + m
                b, g, half = head(m)
                kv = 2 * b + half
                pe.wait_ge(copied, at)
                if m % 8 == 0 and t >= 1:
                    pe.wait_ge(o_read, 2 * t + b - 1)
                o = (half * 4 + g) * HD
                for kb in range(blocks(t)):
                    w = width(t, kb)
                    mm = pe.matmul(banks[6 + b][0:r, o:o + HD], pT[0:w, x % 2, kb, 0:r],
                                   vc[0:w, slot0(t) + kb, kv * HD:(kv + 1) * HD], start=(kb == 0), stop=(kb == blocks(t) - 1))
                mm.then_inc(o_done, 1)

            for t in range(NT):
                queries(t)
                here = n[0]
                if ranked(t + 1):
                    rank(t + 1)
                pe.wait_ge(copied, here)
                scores(t, 0)
                ready = [0] * HP
                for m in range(HP):
                    if m + 1 < HP:
                        scores(t, m + 1)
                    transposes(t, m)
                    ready[m] = n[0]
                    if m >= 1:
                        values(t, m - 1, ready[m - 1])
                values(t, HP - 1, ready[HP - 1])


def rope_table():
    inv = np.exp(-np.float32(np.log(THETA)) * np.arange(HALF, dtype=np.float32) / np.float32(HALF)).astype(np.float32)
    pos = np.concatenate([np.arange(SEQ), PAST + np.arange(DEC)]).astype(np.float32)
    ang = (pos[:, None] * inv[None, :]).astype(np.float32)
    cos, sin = np.cos(ang), np.sin(ang)
    return np.concatenate([cos, cos, -sin, sin], axis=1).astype(np.float32)


OUTPUTS = [
    ("y_prompt", (SEQ, D), (1, SEQ, D)),
    ("y_sample", (DEC, D), (1, DEC, D)),
    ("p_b_k", (B_WIN, B_KV * HD), (1, 1, B_WIN, B_KV, HD)),
    ("p_b_v", (B_WIN, B_KV * HD), (1, 1, B_WIN, B_KV, HD)),
    ("p_c_k", (SEQ, C_KVW), (1, 1, SEQ, C_KV, HD)),
    ("p_c_v", (SEQ, C_KVW), (1, 1, SEQ, C_KV, HD)),
    ("p_c_idx", (SEQ, HD), (1, 1, SEQ, HD)),
    ("s_a_v", (DEC, A_WIDTH), (1, 1, DEC, A_WIDTH)),
    ("s_b_k", (DEC, B_KV * HD), (1, 1, DEC, B_KV, HD)),
    ("s_b_v", (DEC, B_KV * HD), (1, 1, DEC, B_KV, HD)),
    ("s_c_k", (DEC, C_KVW), (1, 1, DEC, C_KV, HD)),
    ("s_c_v", (DEC, C_KVW), (1, 1, DEC, C_KV, HD)),
    ("s_c_idx", (DEC, HD), (1, 1, DEC, HD)),
]


def kernel(x_prompt, x_sample, cache_b_k, cache_b_v, cache_c_k, cache_c_v, cache_c_idx,
           ab_w_in, a_ln_g, a_ln_b, a_ws, a_bs, b_sinks, ab_w_out, c_w_in, c_w_out,
           ln1_g, ln1_b, ln2_g, ln2_b, ff_w1, ff_w2):
    import concourse.bacc as bacc
    from concourse.bass_utils import run_bass_kernel_spmd

    x = np.concatenate([np.asarray(x_prompt)[0], np.asarray(x_sample)[0]], axis=0)
    ins = {
        "x": x,
        "xT": x.T,
        "cache_b_k": np.asarray(cache_b_k).reshape(B_WIN, B_KV * HD),
        "cache_b_v": np.asarray(cache_b_v).reshape(B_WIN, B_KV * HD),
        "cache_c_k": np.asarray(cache_c_k).reshape(PAST, C_KVW),
        "cache_c_v": np.asarray(cache_c_v).reshape(PAST, C_KVW),
        "cache_c_idx": np.asarray(cache_c_idx).reshape(PAST, HD),
        "ab_w_in": np.asarray(ab_w_in)[0],
        "a_ln_g": np.asarray(a_ln_g),
        "a_ln_b": np.asarray(a_ln_b),
        "ws_T": np.asarray(a_ws)[0].transpose(2, 0, 1),
        "bs_T": np.asarray(a_bs)[0].T,
        "sinks": np.asarray(b_sinks),
        "ab_w_out": np.asarray(ab_w_out)[0],
        "c_w_in": np.asarray(c_w_in)[0],
        "c_w_out": np.asarray(c_w_out)[0],
        "ln1_g": np.asarray(ln1_g), "ln1_b": np.asarray(ln1_b),
        "ln2_g": np.asarray(ln2_g), "ln2_b": np.asarray(ln2_b),
        "ff_w1": np.asarray(ff_w1), "ff_w2": np.asarray(ff_w2),
        "rope": rope_table(),
    }
    ins = {k: np.ascontiguousarray(v) for k, v in ins.items()}
    nc = bacc.Bacc("TRN2", target_bir_lowering=False, num_devices=1)
    aps, arrays = {}, {}
    for k, v in ins.items():
        arrays[f"in_{k}"] = v
        aps[k] = nc.dram_tensor(f"in_{k}", v.shape, mybir.dt.from_np(v.dtype), kind="ExternalInput").ap()
    for k, shape, _ in OUTPUTS:
        aps[k] = nc.dram_tensor(f"out_{k}", shape, F32, kind="ExternalOutput").ap()
    encoder(nc, aps)
    got = run_bass_kernel_spmd(nc, [arrays], core_ids=[0]).results[0]
    return tuple(np.asarray(got[f"out_{k}"]).reshape(shape) for k, _, shape in OUTPUTS)
```

```python
from contextlib import ExitStack

import numpy as np

import concourse.bass as bass
from concourse import mybir

ALU = mybir.AluOpType
ACT = mybir.ActivationFunctionType
F32 = mybir.dt.float32
F32R = mybir.dt.float32r

P = 128
D = 1024
KT = D // P
SEQ = 1024
DEC = 64
TOK = SEQ + DEC
NP_TILES = SEQ // P
NT = NP_TILES + 1
SAMPLE = NP_TILES
CHUNK = 64
HD = 64
HALF = HD // 2
D_FF = 4 * D
DEPTH = 2
ALPHA = (2.0 * DEPTH) ** 0.25
EPS = 1e-5
THETA = 10000.0
PAST = 256

A_WIDTH = D // 2
A_GROUPS = 8
A_GD = A_WIDTH // A_GROUPS
B_HEADS = 8
B_KV = 2
B_WIN = 128
AB_IN = 2 * A_WIDTH + B_HEADS * HD + 2 * B_KV * HD

C_HEADS = 16
C_KV = 4
IDX_HEADS = 4
C_Q = C_HEADS * HD
C_KVW = C_KV * HD
C_QI = IDX_HEADS * HD
C_IN = C_Q + 2 * C_KVW + C_QI + HD + IDX_HEADS
TOPK = 256
TOPK_SAMPLE = min(TOPK, (PAST + DEC) // 4)

COLS = 512
QUARTER = 2
W_SLOTS = 5
FC = 256
N_FC = D_FF // FC
FT = FC // P

MASKED = -1e30
BARRED = -3.0e38
TAKEN = -3.3e38
LARGE = 3.0e38

IDX_COL = C_Q + 2 * C_KVW
IDX_W = C_QI + HD + IDX_HEADS


def rows(t):
    return P if t < SAMPLE else DEC


def tok(t):
    return t * P, t * P + rows(t)


RANGES = [(0, 384), (384, 768), (768, TOK)]


class Room:

    def __init__(self, nc, tag, at, end=None):
        self.nc, self.tag, self.at, self.end = nc, tag, at, end or nc.sbuf_usable_end

    def take(self, name, shape, dtype=F32):
        size = 4 * int(np.prod(shape[1:]))
        x = self.nc.alloc_sbuf_tensor_at(self.tag + name, shape, dtype, offset=self.at)
        self.at += -(-size // 32) * 32
        assert self.at <= self.end, (self.tag, name, self.at - self.end)
        return x

    def from_here(self, tag):
        return Room(self.nc, tag, self.at, self.end)


def encoder(nc, aps):
    with ExitStack() as ctx:
        base = Room(nc, "", -(-nc.sbuf_base // 64) * 64)
        A = base.take("act", [P, NT, D])
        ident = base.take("ident", [P, P])
        ident_r = base.take("ident_r", [P, P], F32R)
        mhalf = base.take("minus_half", [P, 1])
        ps = ctx.enter_context(nc.psum_tensor("psum", [P, 8, COLS], F32))
        x2_dram = nc.dram_tensor("x2_scratch", (TOK, D), F32, kind="Internal").ap()
        aps = dict(aps, x2=x2_dram)
        keep_b = base.from_here("b_")
        va = keep_b.take("va", [P, NT, A_WIDTH])
        kb = keep_b.take("k", [P, NT + 1, P])
        vb = keep_b.take("v", [P, NT + 1, P])
        keep_c = base.from_here("c_")
        kc = keep_c.take("k", [P, NT + 2, C_KVW])
        vc = keep_c.take("v", [P, NT + 2, C_KVW])
        ki = keep_c.take("k_idx", [P, NT + 2, 2 * HD])
        qi = keep_c.take("q_idx", [P, NT, C_QI])
        wi = keep_c.take("w_idx", [P, NT, IDX_HEADS])
        split = Room(nc, "", max(keep_b.at, keep_c.at))
        xt_hi = split.take("xt_hi", [P, KT, TOK], F32R)
        xt_lo = split.take("xt_lo", [P, KT, TOK], F32R)

        block_ab_in(nc, aps, split.from_here("ab_in_"), keep_b.from_here("ab_in_"), A, xt_hi, xt_lo, va, kb, vb, ident, ident_r, mhalf, ps)
        block_ab_mixer(nc, aps, split.from_here("ab_mix_"), A, va, kb, vb, ident, ps)
        block_layer(nc, aps, base.from_here("layer0_"), split.from_here("layer0w_"), 0, aps["x"], aps["ab_w_out"], A,
                    xt_hi, xt_lo, ident, mhalf, ps)
        block_c_in(nc, aps, split.from_here("c_in_"), A, xt_hi, xt_lo, kc, vc, ki, qi, wi, ps)
        block_c_mixer(nc, aps, Room(nc, "c_mix_", max(keep_b.at, keep_c.at)), A, kc, vc, ki, qi, wi, ident, ident_r, ps)
        block_layer(nc, aps, base.from_here("layer1_"), split.from_here("layer1w_"), 1, aps["x2"], aps["c_w_out"], A,
                    xt_hi, xt_lo, ident, mhalf, ps)


class Stream:

    def __init__(self, nc, c, tag, room, w, chunks, done):
        self.w = w.rearrange("(k p) n -> p k n", p=P)
        self.chunks = chunks
        self.n = 4 * len(chunks)
        self.raw = room.take("w_raw", [P, 2, QUARTER, COLS], F32)
        self.hi = room.take("w_hi", [P, W_SLOTS, QUARTER, COLS], F32R)
        self.lo = room.take("w_lo", [P, W_SLOTS, QUARTER, COLS], F32R)
        self.arrived = [c(nc.semaphore(tag + f"w_arrived{i}")) for i in range(2)]
        self.hi_made = c(nc.semaphore(tag + "w_hi_made"))
        self.lo_made = c(nc.semaphore(tag + "w_lo_made"))
        self.used = c(nc.semaphore(tag + "w_used"))
        self.done = done

    def load(self, eng, n):
        j, q = divmod(n, 4)
        c0, w = self.chunks[j]
        if n >= 2:
            eng.wait_ge(self.lo_made, n - 1)
        eng.dma_start(self.raw[:, n % 2, :, 0:w],
                      self.w[:, QUARTER * q:QUARTER * q + QUARTER, c0:c0 + w]).then_inc(self.arrived[n % 2], 16)

    def split_hi(self, act, n):
        w = self.chunks[n // 4][1]
        act.wait_ge(self.arrived[n % 2], 16 * (n // 2 + 1))
        if n >= W_SLOTS:
            j, q = divmod(n - W_SLOTS, 4)
            if q < 3:
                act.wait_ge(self.used, 3 * j + q + 1)
            else:
                act.wait_ge(self.done, NT * (j + 1))
        act.copy(self.hi[:, n % W_SLOTS, :, 0:w], self.raw[:, n % 2, :, 0:w]).then_inc(self.hi_made, 1)

    def split_lo(self, dve, n):
        w = self.chunks[n // 4][1]
        dve.wait_ge(self.hi_made, n + 1)
        dve.tensor_tensor(self.lo[:, n % W_SLOTS, :, 0:w], self.raw[:, n % 2, :, 0:w],
                          self.hi[:, n % W_SLOTS, :, 0:w], ALU.subtract).then_inc(self.lo_made, 1)

    def next_pieces(self, j):
        return range(4 * j + W_SLOTS, min(4 * j + 4 + W_SLOTS, self.n))

    def product(self, pe, out, t, j, xt_hi, xt_lo):
        a, b = tok(t)
        w = self.chunks[j][1]
        for q in range(4):
            n = 4 * j + q
            if t == 0:
                pe.wait_ge(self.lo_made, n + 1)
            s = n % W_SLOTS
            for k in range(QUARTER):
                kk = QUARTER * q + k
                first, last = kk == 0, kk == KT - 1
                pe.matmul(out[0:b - a, 0:w], xt_hi[:, kk, a:b], self.hi[:, s, k, 0:w], start=first, stop=False)
                pe.matmul(out[0:b - a, 0:w], xt_hi[:, kk, a:b], self.lo[:, s, k, 0:w], start=False, stop=False)
                mm = pe.matmul(out[0:b - a, 0:w], xt_lo[:, kk, a:b], self.hi[:, s, k, 0:w], start=False, stop=last)
            if t == NT - 1 and q < 3:
                mm.then_inc(self.used, 1)
        mm.then_inc(self.done, 1)


class Norm:

    def __init__(self, nc, c, tag, room, name, width, g_row, b_row):
        self.width, self.g_row, self.b_row = width, g_row, b_row
        self.g = room.take(f"{name}_g", [P, width], F32)
        self.b = room.take(f"{name}_b", [P, width], F32)
        self.stats = room.take(f"{name}_stats", [P, 2, 6 * (width // COLS)], F32)
        self.mv = room.take(f"{name}_mv", [P, NT, 2], F32)
        self.var = room.take(f"{name}_var", [P, NT], F32)
        self.rstd = room.take(f"{name}_rstd", [P, NT], F32)
        self.shift = room.take(f"{name}_shift", [P, NT], F32)
        s = lambda what: c(nc.semaphore(tag + f"{name}_{what}"))
        self.loaded, self.chain, self.var_ready, self.rstd_ready = s("loaded"), s("chain"), s("var_ready"), s("rstd_ready")
        self.shift_ready, self.normalised, self.scaled, self.done = s("shift_ready"), s("normalised"), s("scaled"), s("done")
        self.links = 0

    def load(self, eng):
        eng.dma_start(self.g[:], self.g_row.to_broadcast([P, self.width])).then_inc(self.loaded, 16)
        eng.dma_start(self.b[:], self.b_row.to_broadcast([P, self.width])).then_inc(self.loaded, 16)

    def link(self, dve, ins):
        self.links += 1
        ins.then_inc(self.chain, 1)
        dve.wait_ge(self.chain, self.links)

    def statistics(self, dve, x, t):
        r, st = rows(t), self.stats[:, t % 2]
        for h in range(self.width // COLS):
            ins = dve.bn_stats(st[0:r, 6 * h:6 * h + 6], x[0:r, COLS * h:COLS * h + COLS])
        self.link(dve, ins)
        self.link(dve, dve.bn_aggr(self.mv[0:r, t], st[0:r]))
        dve.tensor_scalar(self.var[0:r, t:t + 1], self.mv[0:r, t, 1:2], EPS, None, ALU.add).then_inc(self.var_ready, 1)

    def rsqrt(self, pool, mhalf, t):
        r = rows(t)
        pool.wait_ge(self.var_ready, t + 1)
        pool.tensor_tensor(self.rstd[0:r, t:t + 1], self.var[0:r, t:t + 1], mhalf[0:r], ALU.pow).then_inc(self.rstd_ready, 1)
        pool.wait_ge(self.rstd_ready, t + 1)
        pool.tensor_scalar(self.shift[0:r, t:t + 1], self.mv[0:r, t, 0:1], self.rstd[0:r, t:t + 1], -1.0,
                           ALU.mult, ALU.mult).then_inc(self.shift_ready, 1)

    def normalise(self, act, x, t):
        r = rows(t)
        act.wait_ge(self.shift_ready, t + 1)
        act.activation(x[0:r], x[0:r], ACT.Identity, bias=self.shift[0:r, t:t + 1],
                       scale=self.rstd[0:r, t:t + 1]).then_inc(self.normalised, 1)

    def scale(self, dve, x, t):
        r = rows(t)
        if t == 0:
            dve.wait_ge(self.loaded, 32)
        dve.wait_ge(self.normalised, t + 1)
        dve.tensor_tensor(x[0:r], x[0:r], self.g[0:r], ALU.mult).then_inc(self.scaled, 1)

    def offset(self, pool, x, t):
        r = rows(t)
        if t == 0:
            pool.wait_ge(self.loaded, 32)
        pool.wait_ge(self.scaled, t + 1)
        pool.tensor_tensor(x[0:r], x[0:r], self.b[0:r], ALU.add).then_inc(self.done, 1)


def rope(dve, link, src, table, tmp, heads):
    r = src.shape[0]
    both = lambda c0, w: table[:, c0:c0 + w].unsqueeze(1).to_broadcast([r, heads, w])
    dve.tensor_tensor(tmp[:, 0, 0:heads], src, both(0, HD), ALU.mult)
    dve.tensor_tensor(tmp[:, 1, 0:heads, 0:HALF], src[:, :, HALF:HD], both(HD, HALF), ALU.mult)
    link(dve.tensor_tensor(tmp[:, 1, 0:heads, HALF:HD], src[:, :, 0:HALF], both(HD + HALF, HALF), ALU.mult))


def block_ab_in(nc, aps, room, x_room, A, xt_hi, xt_lo, va, kb, vb, ident, ident_r, mhalf, ps):
    tag = "ab_in_"
    banks = [ps[:, i] for i in range(8)]
    with ExitStack() as s:
        c = s.enter_context
        chunks = [(0, COLS), (COLS, COLS), (2 * COLS, COLS), (3 * COLS, 2 * P)]
        done = c(nc.semaphore(tag + "products_done"))
        st = Stream(nc, c, tag, room, aps["ab_w_in"], chunks, done)
        ln = Norm(nc, c, tag, room, "a_ln", A_WIDTH, aps["a_ln_g"], aps["a_ln_b"])
        xr = x_room.take("xt_raw", [P, 2, KT, P], F32)
        table = room.take("rope_table", [P, NT, P], F32)
        tmp = room.take("rope_tmp", [P, 2, 2, 8, HD], F32)
        x_arrived = [c(nc.semaphore(tag + f"x_arrived{i}")) for i in range(2)]
        table_arrived = c(nc.semaphore(tag + "table_arrived"))
        x_hi = c(nc.semaphore(tag + "x_hi_made"))
        x_lo = c(nc.semaphore(tag + "x_lo_made"))
        evac_act = c(nc.semaphore(tag + "banks_read_by_scalar"))
        evac_dve = c(nc.semaphore(tag + "banks_read_by_vector"))
        chain = c(nc.semaphore(tag + "vector_chain"))
        consts = c(nc.semaphore(tag + "constants"))
        ident_copied = c(nc.semaphore(tag + "ident_copied"))
        ready = c(nc.semaphore(tag + "outputs_ready"))
        stored = c(nc.semaphore(tag + "outputs_stored"))
        block = c(nc.Block())
        xT = aps["xT"].rearrange("(k p) t -> p k t", p=P)

        @block.sync
        def _(sp):
            def load_x(t):
                a, b = tok(t)
                if t >= 2:
                    sp.wait_ge(x_lo, t - 1)
                sp.dma_start(xr[:, t % 2, :, 0:b - a], xT[:, :, a:b]).then_inc(x_arrived[t % 2], 16)

            load_x(0)
            for n in range(4):
                st.load(sp, n)
            sp.dma_start(table[:, 0:NP_TILES], aps["rope"][0:SEQ].rearrange("(t p) c -> p t c", p=P)).then_inc(table_arrived, 16)
            sp.dma_start(table[0:DEC, SAMPLE], aps["rope"][SEQ:TOK]).then_inc(table_arrived, 16)
            ln.load(sp)
            for t in range(1, NT):
                load_x(t)
            for n in range(4, st.n):
                st.load(sp, n)
            sp.wait_ge(ready, NT)
            sp.wait_ge(evac_dve, 2 * NT)
            sp.dma_start(aps["p_b_k"], kb[:, NP_TILES - 1]).then_inc(stored, 16)
            sp.dma_start(aps["p_b_v"], vb[:, NP_TILES - 1]).then_inc(stored, 16)
            sp.dma_start(aps["s_b_k"], kb[0:DEC, NT]).then_inc(stored, 16)
            sp.dma_start(aps["s_b_v"], vb[0:DEC, NT]).then_inc(stored, 16)
            sp.wait_ge(ln.done, NT)
            sp.dma_start(aps["s_a_v"], va[0:DEC, SAMPLE]).then_inc(stored, 16)
            sp.wait_ge(stored, 80)

        @block.gpsimd
        def _(pool):
            pool.memset(mhalf[:], -0.5).then_inc(consts, 1)
            pool.memset(ident[:], 0.0).then_inc(consts, 1)
            pool.wait_ge(consts, 2)
            pool.affine_select(out=ident[:], in_=ident[:], compare_op=ALU.not_equal, fill=1.0, base=0,
                               pattern=[[-1, P]], channel_multiplier=1).then_inc(consts, 1)
            for t in range(NT + 1):
                if t < NT:
                    ln.rsqrt(pool, mhalf, t)
                if t >= 1:
                    ln.offset(pool, va[:, t - 1], t - 1)

        @block.scalar
        def _(act):
            act.wait_ge(consts, 3)
            act.copy(ident_r[:], ident[:]).then_inc(ident_copied, 1)

            def x_high(t):
                a, b = tok(t)
                act.wait_ge(x_arrived[t % 2], 16 * (t // 2 + 1))
                act.copy(xt_hi[:, :, a:b], xr[:, t % 2, :, 0:b - a]).then_inc(x_hi, 1)

            x_high(0)
            for n in range(4):
                st.split_hi(act, n)
            x_high(1)
            for j in range(len(chunks)):
                for t in range(NT):
                    if j == 0 and t + 2 < NT:
                        x_high(t + 2)
                    if j == 0 and t == NT - 2:
                        st.split_hi(act, 4)
                    if t == NT - 1:
                        for n in st.next_pieces(j):
                            st.split_hi(act, n)
                    if j < 2:
                        g, r = j * NT + t, rows(t)
                        act.wait_ge(done, g + 1)
                        out = A[0:r, t, 0:A_WIDTH] if j == 0 else va[0:r, t]
                        act.activation(out, banks[g % 8][0:r], ACT.Gelu_apprx_tanh).then_inc(evac_act, 1)
                    if j == 1 and t >= 1:
                        ln.normalise(act, va[:, t - 1], t - 1)
                if j == 1:
                    ln.normalise(act, va[:, NT - 1], NT - 1)

        @block.vector
        def _(dve):
            links = [0]

            def link(ins):
                links[0] += 1
                ins.then_inc(chain, 1)
                dve.wait_ge(chain, links[0])

            def x_low(t):
                a, b = tok(t)
                dve.wait_ge(x_hi, t + 1)
                dve.tensor_tensor(xt_lo[:, :, a:b], xr[:, t % 2, :, 0:b - a], xt_hi[:, :, a:b],
                                  ALU.subtract).then_inc(x_lo, 1)

            x_low(0)
            for n in range(4):
                st.split_lo(dve, n)
            for t in range(1, NT):
                x_low(t)
            st.split_lo(dve, 4)
            dve.wait_ge(table_arrived, 32)
            for j in range(len(chunks)):
                for t in range(NT):
                    g, r = j * NT + t, rows(t)
                    turn = tmp[0:r, g % 2]
                    if t == NT - 1:
                        for n in st.next_pieces(j):
                            st.split_lo(dve, n)
                    if j == 1:
                        dve.wait_ge(evac_act, g + 1)
                        ln.statistics(dve, va[:, t], t)
                        if t >= 1:
                            ln.scale(dve, va[:, t - 1], t - 1)
                    if j == 2:
                        dve.wait_ge(done, g + 1)
                        if t >= 2:
                            dve.wait_ge(evac_dve, t - 1)
                        src = banks[g % 8][0:r].rearrange("p (h d) -> p h d", d=HD)
                        rope(dve, link, src, table[0:r, t], turn, 8)
                        out = A[0:r, t, A_WIDTH:D].rearrange("p (g kv d) -> p kv g d", kv=B_KV, d=HD)
                        two = lambda i: turn[:, i].rearrange("p (kv g) d -> p kv g d", kv=B_KV)
                        dve.tensor_tensor(out, two(0), two(1), ALU.add).then_inc(evac_dve, 1)
                    if j == 3:
                        slot = t if t < SAMPLE else NT
                        dve.wait_ge(done, g + 1)
                        dve.wait_ge(evac_dve, g - 1 - 2 * NT)
                        src = banks[g % 8][0:r, 0:P].rearrange("p (h d) -> p h d", d=HD)
                        rope(dve, link, src, table[0:r, t], turn, 2)
                        dve.tensor_tensor(kb[0:r, slot].rearrange("p (h d) -> p h d", d=HD),
                                          turn[:, 0, 0:2], turn[:, 1, 0:2], ALU.add).then_inc(ready, 1)
                        dve.tensor_copy(vb[0:r, slot], banks[g % 8][0:r, P:2 * P]).then_inc(evac_dve, 1)
                if j == 1:
                    ln.scale(dve, va[:, NT - 1], NT - 1)

        @block.tensor
        def _(pe):
            for j in range(len(chunks)):
                for t in range(NT):
                    g = j * NT + t
                    if j == 0:
                        pe.wait_ge(x_lo, t + 1)
                    before = g - 8
                    if before >= 0:
                        if before < 2 * NT:
                            pe.wait_ge(evac_act, before + 1)
                        else:
                            pe.wait_ge(evac_dve, before + 1 - 2 * NT)
                    st.product(pe, banks[g % 8], t, j, xt_hi, xt_lo)


def block_ab_mixer(nc, aps, room, A, va, kb, vb, ident, ps):
    CACHE, OWN = SAMPLE, NT
    tag = "ab_mix_"
    banks = [ps[:, i] for i in range(8)]
    with ExitStack() as s:
        c = s.enter_context
        sb = lambda name, shape: room.take(name, shape)
        sem = lambda name: c(nc.semaphore(tag + name))
        wsT = sb("ws_T", [P, A_GROUPS, P])
        bs = sb("bs", [P, A_GROUPS])
        sinks = sb("sinks", [P, B_HEADS])
        nsinks = sb("minus_sinks", [P, B_HEADS])
        mask = sb("mask", [P, 3, 2 * P])
        kT = sb("kT", [P, NT + 1, P])
        qT = sb("qT", [P, 2, 4, P])
        S = sb("scores", [P, B_HEADS, 2 * P])
        E = sb("probs", [P, B_HEADS, 2 * P])
        pT = sb("probs_T", [P, B_HEADS, 2, P])
        nm = sb("minus_max", [P, 2, B_HEADS])
        rs = sb("row_sum", [P, 2, B_HEADS])
        es = sb("sink_shifted", [P, 2, B_HEADS])
        ee = sb("sink_exp", [P, 2, B_HEADS])
        den = sb("den", [P, 2, B_HEADS])
        rden = sb("rden", [P, 2, B_HEADS])
        loaded, wmask, masks = sem("loaded"), sem("ws_masked"), sem("masks_made")
        gate_done, gate_read, ns_made = sem("gate_done"), sem("gate_read"), sem("minus_sinks_made")
        kt_done, kt_read = sem("k_transposed"), sem("k_T_ready")
        qt_done, qt_read = sem("q_transposed"), sem("q_T_ready")
        s_done, s_read = sem("scores_done"), sem("scores_read")
        e_done, ee_done, es_done = sem("probs_ready"), sem("sink_exp_ready"), sem("sink_shifted_ready")
        pt_done, pt_read = sem("p_transposed"), sem("p_T_ready")
        o_done, o_read = sem("out_done"), sem("out_read")
        den_made, rden_made = sem("den_made"), sem("rden_made")
        block = c(nc.Block())
        nkeys = lambda t: P if t == 0 else (2 * P if t < SAMPLE else P + DEC)
        first_slot = lambda t: max(t - 1, 0) if t < SAMPLE else CACHE
        nblocks = lambda t: 1 if t == 0 else 2
        kwidth = lambda t, b: DEC if (t == SAMPLE and b == 1) else P

        def kT_keys(t, half):
            flat = kT[half * HD:half * HD + HD].rearrange("p s k -> p (s k)")
            s0 = first_slot(t) * P
            return flat[:, s0:s0 + nkeys(t)]

        @block.sync
        def _(sp):
            sp.dma_start(wsT[:], aps["ws_T"]).then_inc(loaded, 16)
            sp.dma_start(bs[:], aps["bs_T"]).then_inc(loaded, 16)
            sp.dma_start(sinks[:], aps["sinks"].to_broadcast([P, B_HEADS])).then_inc(loaded, 16)
            sp.dma_start(kb[:, CACHE], aps["cache_b_k"]).then_inc(loaded, 16)
            sp.dma_start(vb[:, CACHE], aps["cache_b_v"]).then_inc(loaded, 16)

        @block.gpsimd
        def _(pool):
            pool.wait_ge(loaded, 80)
            pool.affine_select(out=wsT[:], in_=wsT[:], compare_op=ALU.is_ge, fill=0.0, base=0,
                               pattern=[[0, A_GROUPS], [1, P]], channel_multiplier=-1).then_inc(wmask, 1)

        @block.scalar
        def _(act):
            for n in range(NT + 1):
                w = DEC if n == OWN else P
                act.wait_ge(kt_done, n + 1)
                act.copy(kT[:, n, 0:w], banks[4 + n % 2][:, 0:w]).then_inc(kt_read, 1)

            def q_copy(t):
                r = rows(t)
                act.wait_ge(qt_done, t + 1)
                if t >= 2:
                    act.wait_ge(s_done, 4 * (t - 1))
                act.copy(qT[:, t % 2, :, 0:r], banks[7][:].rearrange("p (b q) -> p b q", q=P)[:, :, 0:r]).then_inc(qt_read, 1)

            def softmax(t):
                r, nk = rows(t), nkeys(t)
                for h in range(B_HEADS):
                    act.wait_ge(s_read, B_HEADS * t + h + 1)
                    if t >= 1 and h == 0:
                        act.wait_ge(pt_done, 4 * t)
                    act.activation(E[0:r, h, 0:nk], S[0:r, h, 0:nk], ACT.Exp, bias=nm[0:r, t % 2, h:h + 1], scale=-1.0,
                                   accum_out=rs[0:r, t % 2, h:h + 1]).then_inc(e_done, 1)
                act.wait_ge(es_done, t + 1)
                act.activation(ee[0:r, t % 2], es[0:r, t % 2], ACT.Exp).then_inc(ee_done, 1)

            def p_copy(t):
                r = rows(t)
                for n in range(4):
                    act.wait_ge(pt_done, 4 * t + n + 1)
                    if t >= 1 and n == 0:
                        act.wait_ge(o_done, t)
                    bank = banks[4 + n % 2][:].rearrange("p (h b q) -> p h b q", h=2, b=2)
                    if t == SAMPLE:
                        act.copy(pT[:, 2 * n:2 * n + 2, 0, 0:r], bank[:, :, 0, 0:r])
                        act.copy(pT[0:DEC, 2 * n:2 * n + 2, 1, 0:r], bank[0:DEC, :, 1, 0:r]).then_inc(pt_read, 1)
                    else:
                        nb = nblocks(t)
                        act.copy(pT[:, 2 * n:2 * n + 2, 0:nb, 0:r], bank[:, :, 0:nb, 0:r]).then_inc(pt_read, 1)

            q_copy(0)
            softmax(0)
            for t in range(NT):
                if t + 1 < NT:
                    q_copy(t + 1)
                p_copy(t)
                if t + 1 < NT:
                    softmax(t + 1)

        @block.vector
        def _(dve):
            dve.memset(mask[:], 0.0).then_inc(masks, 1)
            dve.wait_ge(masks, 1)
            dve.memset(mask[0:CHUNK, 0, CHUNK:P], MASKED)
            dve.memset(mask[0:CHUNK, 1, 3 * CHUNK:], MASKED)
            dve.memset(mask[CHUNK:P, 1, 0:CHUNK], MASKED).then_inc(masks, 1)
            dve.wait_ge(loaded, 80)
            dve.tensor_scalar(nsinks[:], sinks[:], -1.0, None, ALU.mult).then_inc(ns_made, 1)
            dve.wait_ge(masks, 2)
            dve.wait_ge(ns_made, 1)

            def gate(n):
                dve.wait_ge(gate_done, n + 1)
                if n < A_GROUPS:
                    u = A[:, 0:NP_TILES, n * A_GD:(n + 1) * A_GD]
                    dve.scalar_tensor_tensor(out=u, in0=banks[n % 2 + 2][:].rearrange("p (t c) -> p t c", c=A_GD),
                                             scalar=bs[:, n:n + 1], in1=u, op0=ALU.add, op1=ALU.mult).then_inc(gate_read, 1)
                else:
                    for g in range(A_GROUPS):
                        u = A[0:DEC, SAMPLE, g * A_GD:(g + 1) * A_GD]
                        ins = dve.scalar_tensor_tensor(out=u, in0=banks[n % 2 + 2][0:DEC, g * A_GD:(g + 1) * A_GD],
                                                       scalar=bs[0:DEC, g:g + 1], in1=u, op0=ALU.add, op1=ALU.mult)
                    ins.then_inc(gate_read, 1)

            def scores(t):
                r, nk = rows(t), nkeys(t)
                m = mask[0:r, min(t, 1) if t < SAMPLE else 2, 0:nk]
                if t >= 1:
                    dve.wait_ge(e_done, B_HEADS * t)
                for h in range(B_HEADS):
                    kv, g = divmod(h, 4)
                    if h % 2 == 0:
                        dve.wait_ge(s_done, 4 * t + h // 2 + 1)
                    src = banks[2 * kv + g // 2][0:r, (g % 2) * 2 * P:(g % 2) * 2 * P + nk]
                    dve.tensor_tensor_reduce(S[0:r, h, 0:nk], src, m, -HD ** -0.5, nsinks[0:r, h:h + 1],
                                             ALU.add, ALU.min, nm[0:r, t % 2, h:h + 1]).then_inc(s_read, 1)
                dve.wait_ge(s_read, B_HEADS * t + B_HEADS)
                dve.tensor_tensor(es[0:r, t % 2], sinks[0:r], nm[0:r, t % 2], ALU.add).then_inc(es_done, 1)

            def outputs(t):
                r = rows(t)
                dve.wait_ge(ee_done, t + 1)
                dve.wait_ge(e_done, B_HEADS * (t + 1))
                dve.tensor_tensor(den[0:r, t % 2], rs[0:r, t % 2], ee[0:r, t % 2], ALU.add).then_inc(den_made, 1)
                dve.wait_ge(den_made, t + 1)
                if t >= 2:
                    dve.wait_ge(o_read, t - 1)
                dve.reciprocal(rden[0:r, t % 2], den[0:r, t % 2]).then_inc(rden_made, 1)
                dve.wait_ge(rden_made, t + 1)
                dve.wait_ge(o_done, t + 1)
                dve.tensor_tensor(A[0:r, t, A_WIDTH:D].rearrange("p (h d) -> p h d", d=HD),
                                  banks[6][0:r].rearrange("p (h d) -> p h d", d=HD),
                                  rden[0:r, t % 2].unsqueeze(2).to_broadcast([r, B_HEADS, HD]), ALU.mult).then_inc(o_read, 1)

            for n in range(A_GROUPS + 1):
                gate(n)
            scores(0)
            for t in range(NT):
                if t + 1 < NT:
                    scores(t + 1)
                outputs(t)

        @block.tensor
        def _(pe):
            pe.wait_ge(loaded, 80)
            for n in range(NT + 1):
                r = DEC if n == OWN else P
                if n >= 2:
                    pe.wait_ge(kt_read, n - 1)
                pe.transpose(banks[4 + n % 2][:, 0:r], kb[0:r, n], ident[0:r, 0:r]).then_inc(kt_done, 1)
            pe.wait_ge(wmask, 1)
            for n in range(A_GROUPS + 1):
                if n >= 2:
                    pe.wait_ge(gate_read, n - 1)
                out = banks[n % 2 + 2]
                if n < A_GROUPS:
                    mm = pe.matmul(out[:], wsT[:, n], va[:, 0:NP_TILES, n * A_GD:(n + 1) * A_GD], start=True, stop=True)
                else:
                    for g in range(A_GROUPS):
                        mm = pe.matmul(out[0:DEC, g * A_GD:(g + 1) * A_GD], wsT[0:DEC, g, 0:DEC],
                                       va[0:DEC, SAMPLE, g * A_GD:(g + 1) * A_GD], start=True, stop=True)
                mm.then_inc(gate_done, 1)

            def q_transpose(t):
                r = rows(t)
                if t >= 1:
                    pe.wait_ge(qt_read, t)
                for b in range(4):
                    mm = pe.transpose(banks[7][:, b * P:b * P + r], A[0:r, t, A_WIDTH + b * P:A_WIDTH + (b + 1) * P],
                                      ident[0:r, 0:r])
                mm.then_inc(qt_done, 1)

            def scores(t):
                r, nk = rows(t), nkeys(t)
                pe.wait_ge(qt_read, t + 1)
                pe.wait_ge(kt_read, NT + 1)
                if t == 0:
                    pe.wait_ge(gate_read, A_GROUPS + 1)
                for half in range(2):
                    for b in range(4):
                        if t >= 1 and b % 2 == 0:
                            pe.wait_ge(s_read, B_HEADS * (t - 1) + 4 * half + b + 2)
                        mm = pe.matmul(banks[2 * half + b // 2][0:r, (b % 2) * 2 * P:(b % 2) * 2 * P + nk],
                                       qT[half * HD:half * HD + HD, t % 2, b, 0:r], kT_keys(t, half), start=True, stop=True)
                        if b % 2:
                            mm.then_inc(s_done, 1)

            def p_transpose(t):
                r = rows(t)
                for n in range(4):
                    pe.wait_ge(e_done, B_HEADS * t + 2 * n + 2)
                    if 4 * t + n >= 2:
                        pe.wait_ge(pt_read, 4 * t + n - 1)
                    for hh in range(2):
                        for b in range(nblocks(t)):
                            w = kwidth(t, b)
                            at = (2 * hh + b) * P
                            mm = pe.transpose(banks[4 + n % 2][0:w, at:at + r], E[0:r, 2 * n + hh, b * P:b * P + w],
                                              ident[0:r, 0:r])
                    mm.then_inc(pt_done, 1)

            def values(t):
                r, nb = rows(t), nblocks(t)
                pe.wait_ge(pt_read, 4 * t + 4)
                if t >= 1:
                    pe.wait_ge(o_read, t)
                for h in range(B_HEADS):
                    kv = h // 4
                    for b in range(nb):
                        w = kwidth(t, b)
                        mm = pe.matmul(banks[6][0:r, h * HD:(h + 1) * HD], pT[0:w, h, b, 0:r],
                                       vb[0:w, first_slot(t) + b, kv * HD:(kv + 1) * HD], start=(b == 0), stop=(b == nb - 1))
                mm.then_inc(o_done, 1)

            q_transpose(0)
            scores(0)
            for t in range(NT):
                if t + 1 < NT:
                    q_transpose(t + 1)
                    scores(t + 1)
                p_transpose(t)
                values(t)


class Turn:

    def __init__(self, nc, c, tag, name, A, xt_hi, xt_lo, ident, bank_of):
        self.A, self.hi, self.lo, self.ident, self.bank_of = A, xt_hi, xt_lo, ident, bank_of
        self.turned = c(nc.semaphore(tag + f"{name}_turned"))
        self.hi_made = c(nc.semaphore(tag + f"{name}_hi_made"))

    def transpose(self, pe, n):
        t, h = divmod(n, 2)
        r = rows(t)
        for b in range(4):
            c0 = (4 * h + b) * P
            mm = pe.transpose(self.bank_of(n)[:, b * P:b * P + r], self.A[0:r, t, c0:c0 + P], self.ident[0:r, 0:r])
        mm.then_inc(self.turned, 1)

    def view(self, x, n):
        t, h = divmod(n, 2)
        a, b = tok(t)
        return x[:, 4 * h:4 * h + 4, a:b]

    def bank(self, n):
        return self.bank_of(n)[:].rearrange("p (b q) -> p b q", q=P)[:, :, 0:rows(n // 2)]

    def high(self, act, n):
        act.wait_ge(self.turned, n + 1)
        act.copy(self.view(self.hi, n), self.bank(n)).then_inc(self.hi_made, 1)

    def low(self, dve, n, freed):
        dve.wait_ge(self.hi_made, n + 1)
        dve.tensor_tensor(self.view(self.lo, n), self.bank(n), self.view(self.hi, n), ALU.subtract).then_inc(freed, 1)


def block_layer(nc, aps, room, w_room, layer, resid, w_out, A, xt_hi, xt_lo, ident, mhalf, ps):
    w1 = aps["ff_w1"][layer].rearrange("(k p) (n f) -> p k n f", p=P, f=FC)
    w2 = aps["ff_w2"][layer].rearrange("(n f p) d -> p n f d", p=P, f=FT)
    NR = len(RANGES)
    G1 = FT * NR
    G2 = 2 * NT
    PAIRS = (N_FC - 4) // 2
    LAST = N_FC - 1
    LAG = 2
    RESID = 4
    tag = f"layer{layer}_"
    banks = [ps[:, i] for i in range(8)]

    both = lambda kind, t: [(kind, 2 * t), (kind, 2 * t + 1)]
    GROUPS = both("mix", 0) + both("mix", 1)
    for t in range(NT):
        GROUPS += [("out", 0, t)] + (both("mix", t + 2) if t + 2 < NT else [])
    for t in range(NT):
        GROUPS += [("out", 1, t)] + (both("x1", t - LAG) if t >= LAG else [])
    TAIL = [both("x1", t) for t in range(NT - LAG, NT)]
    for pair in TAIL:
        GROUPS += pair
    number = {group: k for k, group in enumerate(GROUPS)}
    SHIFT = (4 - number[TAIL[0][0]]) % 8
    bank_number = lambda group: (number[group] + SHIFT) % 8
    emptied = lambda bank: max(k for k, group in enumerate(GROUPS) if bank_number(group) == bank) + 1

    with ExitStack() as s:
        c = s.enter_context
        sb = lambda name, shape, dt=F32: room.take(name, shape, dt)
        sem = lambda name: c(nc.semaphore(tag + name))
        chunks = [(0, COLS), (COLS, COLS)]
        done = sem("products_done")
        h_room = w_room.from_here(tag)
        st = Stream(nc, c, tag, w_room, w_out, chunks, done)
        w1_at = (w_room.end - 2 * 4 * KT * FC) // 32 * 32
        top = Room(nc, tag, w1_at)
        assert w_room.at <= top.at
        w1_hi, w1_lo = [top.take(n, [P, KT, FC], F32R) for n in ("w1_hi", "w1_lo")]
        w2_hi, w2_lo = [h_room.take(n, [P, FT, D], F32R) for n in ("w2_hi", "w2_lo")]
        h_hi, h_lo = [h_room.take(n, [P, 2, FT, TOK], F32R) for n in ("h_hi", "h_lo")]
        assert h_room.at <= w1_at
        ln1 = Norm(nc, c, tag, room, "ln1", D, aps["ln1_g"][layer:layer + 1], aps["ln1_b"][layer:layer + 1])
        w1_raw, w2_raw = sb("w1_raw", [P, KT, FC]), sb("w2_raw", [P, FT, D])
        h_raw = sb("h_raw", [P, 2, 384])
        xr = room.from_here(tag).take("resid", [P, RESID, COLS], F32)
        ln2 = Norm(nc, c, tag, room, "ln2", D, aps["ln2_g"][layer:layer + 1], aps["ln2_b"][layer:layer + 1])
        r_arrived = [sem(f"resid_arrived{i}") for i in range(RESID)]
        freed, scaled = sem("banks_freed"), sem("alpha_scaled")
        turns = {"mix": Turn(nc, c, tag, "mix", A, xt_hi, xt_lo, ident, lambda n: banks[bank_number(("mix", n))]),
                 "x1": Turn(nc, c, tag, "x1", A, xt_hi, xt_lo, ident, lambda n: banks[bank_number(("x1", n))])}
        w1_in, w2_in = sem("w1_arrived"), sem("w2_arrived")
        w1_hi_made, w1_lo_made = sem("w1_hi_made"), sem("w1_lo_made")
        w2_hi_made, w2_lo_made = sem("w2_hi_made"), sem("w2_lo_made")
        h_done, relu_done, square_done = sem("h_product_done"), sem("relu_done"), sem("square_done")
        h_hi_made, h_lo_made = sem("h_hi_made"), sem("h_lo_made")
        y_done, y_read = sem("y_product_done"), sem("y_banks_read")
        x2_freed = sem("x2_banks_freed")
        stored = sem("outputs_stored")
        turn2 = Turn(nc, c, tag, "x2", A, xt_hi, xt_lo, ident, lambda n: banks[n % 4])
        reads_before = lambda g: g - 3 if g >= 4 else max(x for x in range(G2) if x % 4 == g % 4) + 1 - G2
        block = c(nc.Block())

        def load_w1(sp, i, wait):
            if wait:
                sp.wait_ge(w1_lo_made, FT * i)
            sp.dma_start(w1_raw[:], w1[:, :, bass.ds(i, 1)].rearrange("p k n f -> p k (n f)")).then_inc(w1_in, 16)

        def load_w2(sp, i, wait):
            if wait:
                sp.wait_ge(w2_lo_made, i)
            sp.dma_start(w2_raw[:], w2[:, bass.ds(i, 1)].rearrange("p n f d -> p (n f) d")).then_inc(w2_in, 16)

        @block.sync
        def _(sp):
            def load_resid(g):
                j, t = divmod(g, NT)
                a, b = tok(t)
                if g >= RESID:
                    before = divmod(g - RESID, NT)
                    sp.wait_ge(freed, number[("out",) + before] + 1)
                sp.dma_start(xr[0:b - a, g % RESID], resid[a:b, j * COLS:(j + 1) * COLS]).then_inc(r_arrived[g % RESID], 16)

            for n in range(W_SLOTS + 2):
                st.load(sp, n)
                if n == 1:
                    ln1.load(sp)
                    load_resid(0)
                    load_resid(1)
            load_w1(sp, 0, False)
            load_w2(sp, 0, False)
            for g in range(2, NT + RESID - 1):
                load_resid(g)
            for n in range(W_SLOTS + 2, st.n):
                st.load(sp, n)
            for g in range(NT + RESID - 1, G2):
                load_resid(g)
            sp.wait_ge(freed, number[("out", 1, NT - 1)] + 1)
            ln2.load(sp)
            with sp.Fori(1, N_FC) as i:
                load_w1(sp, i, True)
                load_w2(sp, i, True)
            for t in range(NT):
                a, b = tok(t)
                sp.wait_ge(ln2.done, t + 1)
                if layer == 0:
                    dst = aps["x2"][a:b]
                else:
                    dst = aps["y_prompt"][a:b] if t < SAMPLE else aps["y_sample"]
                sp.dma_start(dst, A[0:b - a, t]).then_inc(stored, 16)
            sp.wait_ge(stored, 16 * NT)

        @block.gpsimd
        def _(pool):
            for ln in (ln1, ln2):
                ln.rsqrt(pool, mhalf, 0)
                for t in range(1, NT):
                    ln.offset(pool, A[:, t - 1], t - 1)
                    ln.rsqrt(pool, mhalf, t)
                ln.offset(pool, A[:, NT - 1], NT - 1)

        def w1_high(act, i, f, wait):
            if f == 0:
                act.wait_ge(w1_in, 16 * i + 16)
            if wait:
                act.wait_ge(h_done, G1 * i - G1 + NR * (f + 1))
            part = slice(f * P, (f + 1) * P)
            act.copy(w1_hi[:, :, part], w1_raw[:, :, part]).then_inc(w1_hi_made, 1)

        def w2_high(act, i, wait):
            act.wait_ge(w2_in, 16 * i + 16)
            if wait:
                act.wait_ge(y_done, G2 * i)
            act.copy(w2_hi[:], w2_raw[:]).then_inc(w2_hi_made, 1)

        w2_place = lambda x, f: x[:, :, f * P:(f + 1) * P]
        w2_part = lambda f: w2_raw[:, f].rearrange("p (k q) -> p k q", q=P)

        def w2_high_last(act, f):
            if f == 0:
                act.wait_ge(w2_in, 16 * N_FC)
            act.wait_ge(h_done, G1 * LAST + NR * (f + 1))
            act.copy(w2_place(w1_hi, f), w2_part(f)).then_inc(w2_hi_made, 1)

        def h_high(act, i, buf, f, settled=True):
            for n in range(NR):
                g = NR * f + n
                a, b = RANGES[n]
                raw = h_raw[:, g % 2, 0:b - a]
                act.wait_ge(h_done, G1 * i + g + 1)
                if settled or g >= 2:
                    act.wait_ge(h_lo_made, G1 * i + g - 1)
                act.activation(raw, banks[g % 3][:, 0:b - a], ACT.Relu).then_inc(relu_done, 1)
                act.wait_ge(relu_done, G1 * i + g + 1)
                act.activation(raw, raw, ACT.Square).then_inc(square_done, 1)
                act.wait_ge(square_done, G1 * i + g + 1)
                act.copy(h_hi[:, buf, f, a:b], raw).then_inc(h_hi_made, 1)

        def normalised_x1(act, t):
            for n in (2 * t, 2 * t + 1):
                turns["x1"].high(act, n)
            r = rows(t)
            act.mul(A[0:r, t], A[0:r, t], ALPHA).then_inc(scaled, 1)

        @block.scalar
        def _(act):
            for t in range(2):
                for n in (2 * t, 2 * t + 1):
                    turns["mix"].high(act, n)
                st.split_hi(act, t)
            for n in range(2, W_SLOTS):
                st.split_hi(act, n)
            for t in range(2, NT):
                for n in (2 * t, 2 * t + 1):
                    turns["mix"].high(act, n)
            for n in st.next_pieces(0):
                st.split_hi(act, n)
            w1_high(act, 0, 0, False)
            w1_high(act, 0, 1, False)
            for t in range(NT):
                if t >= LAG:
                    normalised_x1(act, t - LAG)
                ln1.normalise(act, A[:, t], t)
            normalised_x1(act, NT - 2)
            act.wait_ge(done, G2)
            w2_high(act, 0, False)
            normalised_x1(act, NT - 1)
            for i in range(2):
                if i == 1:
                    act.wait_ge(h_lo_made, G1)
                h_high(act, i, i, 0, settled=i > 0)
                w1_high(act, i + 1, 0, True)
                h_high(act, i, i, 1)
                w1_high(act, i + 1, 1, True)
            w2_high(act, 1, True)
            with act.Fori(0, PAIRS) as m:
                for u in range(2):
                    i = 2 * m + (u + 2)
                    act.wait_ge(y_done, G2 * (i - 1))
                    h_high(act, i, u, 0)
                    w1_high(act, i + 1, 0, True)
                    h_high(act, i, u, 1)
                    w1_high(act, i + 1, 1, True)
                    w2_high(act, i, True)
            act.wait_ge(y_done, G2 * (N_FC - 3))
            h_high(act, N_FC - 2, 0, 0)
            w1_high(act, LAST, 0, True)
            h_high(act, N_FC - 2, 0, 1)
            w1_high(act, LAST, 1, True)
            w2_high(act, N_FC - 2, True)
            h_high(act, LAST, 1, 0)
            w2_high_last(act, 0)
            h_high(act, LAST, 1, 1)
            w2_high_last(act, 1)
            for t in range(NT + LAG):
                if layer == 0 and t >= LAG:
                    for n in (2 * (t - LAG), 2 * (t - LAG) + 1):
                        turn2.high(act, n)
                if t < NT:
                    ln2.normalise(act, A[:, t], t)

        def w1_low(dve, i, f):
            part = slice(f * P, (f + 1) * P)
            dve.wait_ge(w1_hi_made, FT * i + f + 1)
            dve.tensor_tensor(w1_lo[:, :, part], w1_raw[:, :, part], w1_hi[:, :, part], ALU.subtract).then_inc(w1_lo_made, 1)

        def w2_low(dve, i):
            dve.wait_ge(w2_hi_made, i + 1)
            dve.tensor_tensor(w2_lo[:], w2_raw[:], w2_hi[:], ALU.subtract).then_inc(w2_lo_made, 1)

        def w2_low_last(dve, f):
            dve.wait_ge(w2_hi_made, LAST + f + 1)
            dve.tensor_tensor(w2_place(w1_lo, f), w2_part(f), w2_place(w1_hi, f), ALU.subtract).then_inc(w2_lo_made, 1)

        def h_low(dve, i, buf, f):
            for n in range(NR):
                g = NR * f + n
                a, b = RANGES[n]
                dve.wait_ge(h_hi_made, G1 * i + g + 1)
                dve.tensor_tensor(h_lo[:, buf, f, a:b], h_raw[:, g % 2, 0:b - a], h_hi[:, buf, f, a:b],
                                  ALU.subtract).then_inc(h_lo_made, 1)

        def add_y(dve, i, g):
            t, j = divmod(g, 2)
            r = rows(t)
            if g % 2 == 0 and isinstance(i, int) and i == 0:
                dve.wait_ge(scaled, t + 1)
            dve.wait_ge(y_done, G2 * i + g + 1)
            acc = A[0:r, t, j * COLS:(j + 1) * COLS]
            dve.tensor_tensor(acc, banks[4 + g % 4][0:r], acc, ALU.add).then_inc(y_read, 1)

        @block.vector
        def _(dve):
            def empty(kind, n):
                turns[kind].low(dve, n, freed)

            def add_resid(j, t):
                g, r = j * NT + t, rows(t)
                if t == NT - 1:
                    for n in st.next_pieces(j):
                        st.split_lo(dve, n)
                dve.wait_ge(r_arrived[g % RESID], 16 * (g // RESID + 1))
                dve.wait_ge(done, g + 1)
                dve.scalar_tensor_tensor(out=A[0:r, t, j * COLS:(j + 1) * COLS], in0=xr[0:r, g % RESID], scalar=ALPHA,
                                         in1=banks[bank_number(("out", j, t))][0:r], op0=ALU.mult, op1=ALU.add).then_inc(freed, 1)

            for k, group in enumerate(GROUPS):
                if group[0] != "out":
                    empty(*group)
                    if group in (("mix", 1), ("mix", 3)):
                        st.split_lo(dve, group[1] // 2)
                    if group == ("mix", 3):
                        for n in range(2, W_SLOTS):
                            st.split_lo(dve, n)
                    if group == ("x1", 2 * (NT - 1 - LAG) + 1):
                        ln1.scale(dve, A[:, NT - 1], NT - 1)
                    if group == ("x1", 2 * (NT - 2) + 1):
                        w2_low(dve, 0)
                else:
                    _, j, t = group
                    if j == 1 and t >= 1:
                        ln1.scale(dve, A[:, t - 1], t - 1)
                    add_resid(j, t)
                    if j == 1:
                        dve.wait_ge(freed, k + 1)
                        ln1.statistics(dve, A[:, t], t)
                        if t < FT:
                            w1_low(dve, 0, t)
            for i in range(2):
                for f in range(FT):
                    h_low(dve, i, i, f)
                    w1_low(dve, i + 1, f)
            for g in range(G2):
                add_y(dve, 0, g)
            w2_low(dve, 1)
            with dve.Fori(0, PAIRS) as m:
                for u in range(2):
                    i = 2 * m + (u + 2)
                    for f in range(FT):
                        h_low(dve, i, u, f)
                        w1_low(dve, i + 1, f)
                    for g in range(G2):
                        add_y(dve, i - 1, g)
                    w2_low(dve, i)
            for f in range(FT):
                h_low(dve, N_FC - 2, 0, f)
                w1_low(dve, LAST, f)
            for g in range(G2):
                add_y(dve, N_FC - 3, g)
            w2_low(dve, N_FC - 2)
            for f in range(FT):
                h_low(dve, LAST, 1, f)
                w2_low_last(dve, f)
            for t in range(NT + LAG):
                if 1 <= t <= NT:
                    ln2.scale(dve, A[:, t - 1], t - 1)
                if t < NT:
                    add_y(dve, N_FC - 2, 2 * t)
                    add_y(dve, N_FC - 2, 2 * t + 1)
                    dve.wait_ge(y_read, G2 * (N_FC - 2) + 2 * t + 2)
                    ln2.statistics(dve, A[:, t], t)
                if layer == 0 and t >= LAG:
                    for n in (2 * (t - LAG), 2 * (t - LAG) + 1):
                        turn2.low(dve, n, x2_freed)

        def first_group(pe, i, g):
            f, n = divmod(g, NR)
            a, b = RANGES[n]
            if n == 0:
                pe.wait_ge(w1_lo_made, FT * i + f + 1)
            out = banks[g % 3][:, 0:b - a]
            for k in range(KT):
                w = slice(f * P, (f + 1) * P)
                pe.matmul(out, w1_hi[:, k, w], xt_hi[:, k, a:b], start=(k == 0), stop=False)
                pe.matmul(out, w1_hi[:, k, w], xt_lo[:, k, a:b], start=False, stop=False)
                mm = pe.matmul(out, w1_lo[:, k, w], xt_hi[:, k, a:b], start=False, stop=(k == KT - 1))
            mm.then_inc(h_done, 1)

        def first_product(pe, i):
            for g in range(G1):
                pe.wait_ge(relu_done, G1 * i + g - 2)
                first_group(pe, i, g)

        def second_product(pe, i, buf, prior, last=False):
            pe.wait_ge(w2_lo_made, i + 1)
            pe.wait_ge(h_lo_made, G1 * i + G1)
            for g in range(G2):
                t, j = divmod(g, 2)
                a, b = tok(t)
                if prior or g >= 4:
                    pe.wait_ge(y_read, G2 * i + reads_before(g))
                else:
                    pe.wait_ge(freed, emptied(4 + g % 4))
                out = banks[4 + g % 4][0:b - a]
                d = slice(j * COLS, (j + 1) * COLS)
                parts = [(buf, f, w2_hi[:, f, d], w2_lo[:, f, d]) for f in range(FT)]
                if last:
                    k = slice(j * COLS // P, (j + 1) * COLS // P)
                    parts += [(1 - buf, f, w2_place(w1_hi, f)[:, k], w2_place(w1_lo, f)[:, k]) for f in range(FT)]
                for n, (hb, f, high, low) in enumerate(parts):
                    if g == 0 and n >= FT:
                        pe.wait_ge(w2_lo_made, i + 1 + n - FT + 1)
                        pe.wait_ge(h_lo_made, G1 * N_FC)
                    pe.matmul(out, h_hi[:, hb, f, a:b], high, start=(n == 0), stop=False)
                    pe.matmul(out, h_hi[:, hb, f, a:b], low, start=False, stop=False)
                    mm = pe.matmul(out, h_lo[:, hb, f, a:b], high, start=False, stop=(n == len(parts) - 1))
                mm.then_inc(y_done, 1)
                if last and layer == 0 and j == 1 and t >= LAG:
                    turn_x2(pe, t - LAG)

        def turn_x2(pe, t):
            pe.wait_ge(ln2.done, t + 1)
            for n in (2 * t, 2 * t + 1):
                if n >= 4:
                    pe.wait_ge(x2_freed, n - 3)
                else:
                    pe.wait_ge(relu_done, G1 * N_FC)
                turn2.transpose(pe, n)

        @block.tensor
        def _(pe):
            def turn_group(kind, n):
                k = number[(kind, n)]
                if k >= 8:
                    pe.wait_ge(freed, k - 7)
                if kind == "x1":
                    pe.wait_ge(ln1.done, n // 2 + 1)
                turns[kind].transpose(pe, n)

            for k, group in enumerate(GROUPS[:number[TAIL[0][0]]]):
                if group[0] == "out":
                    _, j, t = group
                    pe.wait_ge(freed, max(k - 7, number[("mix", 2 * t + 1)] + 1 if j == 0 else 0))
                    st.product(pe, banks[bank_number(group)], t, j, xt_hi, xt_lo)
                else:
                    turn_group(*group)
            for n in range(NR):
                pe.wait_ge(freed, max(emptied(n), number[("x1", 2 * (-(-RANGES[n][1] // P) - 1) + 1)] + 1))
                first_group(pe, 0, n)
                if n < len(TAIL):
                    for group in TAIL[n]:
                        turn_group(*group)
            for g in range(NR, G1):
                pe.wait_ge(relu_done, g - 2)
                first_group(pe, 0, g)
            first_product(pe, 1)
            second_product(pe, 0, 0, False)
            with pe.Fori(0, PAIRS) as m:
                for u in range(2):
                    i = 2 * m + (u + 2)
                    first_product(pe, i)
                    second_product(pe, i - 1, (u + 1) % 2, True)
            first_product(pe, N_FC - 2)
            second_product(pe, N_FC - 3, 1, True)
            first_product(pe, LAST)
            second_product(pe, N_FC - 2, 0, True, last=True)
            if layer == 0:
                for t in range(NT - LAG, NT):
                    turn_x2(pe, t)


def ranges_of(numbers):
    found = []
    for n in sorted(numbers):
        if found and found[-1].stop == n:
            found[-1] = range(found[-1].start, n + 1)
        else:
            found.append(range(n, n + 1))
    return found


def block_c_in(nc, aps, room, A, xt_hi, xt_lo, kc, vc, ki, qi, wi, ps):
    tag = "c_in_"
    banks = [ps[:, i] for i in range(8)]
    with ExitStack() as s:
        c = s.enter_context
        chunks = [(IDX_COL, IDX_W), (0, COLS), (COLS, COLS), (C_Q, 2 * C_KVW)]
        done = c(nc.semaphore(tag + "products_done"))
        st = Stream(nc, c, tag, room, aps["c_w_in"], chunks, done)
        table = room.take("rope_table", [P, NT, P], F32)
        tmp = room.take("rope_tmp", [P, 2, 2, 8, HD], F32)
        loaded = c(nc.semaphore(tag + "table_and_caches_arrived"))
        read = c(nc.semaphore(tag + "banks_read"))
        chain = c(nc.semaphore(tag + "vector_chain"))
        stored = c(nc.semaphore(tag + "outputs_stored"))
        block = c(nc.Block())
        finished = ranges_of(nc.released_uncleared_semaphores)
        tiles = lambda x: x.rearrange("(t p) c -> p t c", p=P)
        CACHE = slice(NP_TILES, NP_TILES + 2)
        OWN = NT + 1

        @block.sync
        def _(sp):
            for n in range(W_SLOTS + 2):
                st.load(sp, n)
                if n == 2:
                    sp.dma_start(table[:, 0:NP_TILES], tiles(aps["rope"][0:SEQ])).then_inc(loaded, 16)
                    sp.dma_start(table[0:DEC, SAMPLE], aps["rope"][SEQ:TOK]).then_inc(loaded, 16)
            sp.dma_start(kc[:, CACHE], tiles(aps["cache_c_k"])).then_inc(loaded, 16)
            sp.dma_start(vc[:, CACHE], tiles(aps["cache_c_v"])).then_inc(loaded, 16)
            for h in range(2):
                sp.dma_start(ki[:, CACHE, h * HD:(h + 1) * HD], tiles(aps["cache_c_idx"])).then_inc(loaded, 16)
            for n in range(W_SLOTS + 2, st.n):
                st.load(sp, n)
            sp.wait_ge(read, 4 * NT)
            sp.dma_start(tiles(aps["p_c_k"]), kc[:, 0:NP_TILES]).then_inc(stored, 16)
            sp.dma_start(tiles(aps["p_c_v"]), vc[:, 0:NP_TILES]).then_inc(stored, 16)
            sp.dma_start(tiles(aps["p_c_idx"]), ki[:, 0:NP_TILES, 0:HD]).then_inc(stored, 16)
            sp.dma_start(aps["s_c_k"], kc[0:DEC, OWN]).then_inc(stored, 16)
            sp.dma_start(aps["s_c_v"], vc[0:DEC, OWN]).then_inc(stored, 16)
            sp.dma_start(aps["s_c_idx"], ki[0:DEC, OWN, 0:HD]).then_inc(stored, 16)
            sp.wait_ge(stored, 96)
            sp.wait_ge(loaded, 96)

        @block.gpsimd
        def _(pool):
            for sem_range in finished:
                pool.sem_clear(sem_range)

        @block.scalar
        def _(act):
            for n in range(W_SLOTS):
                st.split_hi(act, n)
            for j in range(len(chunks)):
                for n in st.next_pieces(j):
                    st.split_hi(act, n)

        @block.vector
        def _(dve):
            links = [0]

            def link(ins):
                links[0] += 1
                ins.then_inc(chain, 1)
                dve.wait_ge(chain, links[0])

            for n in range(W_SLOTS):
                st.split_lo(dve, n)
            dve.wait_ge(loaded, 96)
            for j in range(len(chunks)):
                for t in range(NT):
                    g, r = j * NT + t, rows(t)
                    turn = tmp[0:r, g % 2]
                    slot = t if t < SAMPLE else OWN
                    bank = banks[g % 8][0:r]
                    if t == NT - 1:
                        for n in st.next_pieces(j):
                            st.split_lo(dve, n)
                    dve.wait_ge(done, g + 1)
                    if g >= 2:
                        dve.wait_ge(read, g - 1)
                    if j == 0:
                        n = IDX_HEADS + 1
                        rope(dve, link, bank[:, 0:n * HD].rearrange("p (h d) -> p h d", d=HD), table[0:r, t], turn, n)
                        dve.tensor_tensor(qi[0:r, t].rearrange("p (h d) -> p h d", d=HD), turn[:, 0, 0:IDX_HEADS],
                                          turn[:, 1, 0:IDX_HEADS], ALU.add)
                        twice = lambda i: turn[:, i, IDX_HEADS:IDX_HEADS + 1].to_broadcast([r, 2, HD])
                        dve.tensor_tensor(ki[0:r, slot].rearrange("p (h d) -> p h d", d=HD), twice(0), twice(1), ALU.add)
                        dve.tensor_copy(wi[0:r, t], bank[:, n * HD:IDX_W]).then_inc(read, 1)
                    elif j < 3:
                        rope(dve, link, bank.rearrange("p (h d) -> p h d", d=HD), table[0:r, t], turn, 8)
                        out = A[0:r, t, (j - 1) * COLS:j * COLS].rearrange("p (h d) -> p h d", d=HD)
                        dve.tensor_tensor(out, turn[:, 0], turn[:, 1], ALU.add).then_inc(read, 1)
                    else:
                        rope(dve, link, bank[:, 0:C_KVW].rearrange("p (h d) -> p h d", d=HD), table[0:r, t], turn, C_KV)
                        dve.tensor_tensor(kc[0:r, slot].rearrange("p (h d) -> p h d", d=HD), turn[:, 0, 0:C_KV],
                                          turn[:, 1, 0:C_KV], ALU.add)
                        dve.tensor_copy(vc[0:r, slot], bank[:, C_KVW:2 * C_KVW]).then_inc(read, 1)

        @block.tensor
        def _(pe):
            for j in range(len(chunks)):
                for t in range(NT):
                    g = j * NT + t
                    if g >= 8:
                        pe.wait_ge(read, g - 7)
                    st.product(pe, banks[g % 8], t, j, xt_hi, xt_lo)


def block_c_mixer(nc, aps, room, A, kc, vc, ki, qi, wi, ident, ident_r, ps):
    tag = "c_mix_"
    NS = NT + 2
    OWN = NT + 1
    HP = C_HEADS
    ORDER = [0, 1, SAMPLE, 7, 6, 5, 4, 3, 2]
    RANKED = ORDER[2:]
    NR = len(RANKED)
    RING = 3

    nkeys = lambda t: (t + 1) * P if t < SAMPLE else PAST + DEC
    key0 = lambda t: 0 if t < SAMPLE else NP_TILES * P
    slot0 = lambda t: 0 if t < SAMPLE else NP_TILES
    blocks = lambda t: -(-nkeys(t) // P)
    width = lambda t, b: min(P, nkeys(t) - b * P)
    groups = lambda t: -(-blocks(t) // 4)
    rounds = lambda t: (TOPK if t < SAMPLE else TOPK_SAMPLE) // 8

    FIRST = 2
    FIRST_RANKED = 3
    items_at = [[] for _ in range(HP * NT)]
    mixes_at = [[] for _ in range(HP * NT)]
    rounds_at = [[] for _ in range(HP * NT)]
    for m in range(FIRST, NR):
        start = HP * m if m >= RING else 3
        for i, (x_item, x_mix) in enumerate([(-2, 0), (-1, 1), (2, 3), (3, 4)]):
            items_at[start + x_item].append((m, i))
            mixes_at[start + x_mix].append((m, i))

    def spread(m, count, lo, hi):
        for j in range(count):
            rounds_at[lo + j * (hi - lo) // count].append(m)

    AHEAD = rounds(RANKED[0])
    half = [rounds(t) // 2 for t in RANKED]
    spread(1, 5, 0, 7)
    spread(1, rounds(RANKED[1]) - AHEAD - 5, 7, FIRST_RANKED * HP)
    spread(2, half[2], 7, FIRST_RANKED * HP)
    for m in range(FIRST, NR):
        lo, hi = HP * (m + 1), HP * (m + 2)
        alone = 5 if m + 1 < NR else 5 * half[m] // HP
        spread(m, alone, lo, lo + 5)
        spread(m, half[m] - alone, lo + 5, hi)
        if m + 1 < NR:
            spread(m + 1, half[m + 1], lo + 5, hi)
    uses = [("item", m, i) for m in range(FIRST) for i in range(IDX_HEADS)]
    for x in range(HP * NT):
        uses += [("head", x)] + [("item",) + item for item in items_at[x]]
    number = {use: k for k, use in enumerate(uses)}
    QUERY_AT = [10, 11, 12, 13]

    with ExitStack() as s:
        c = s.enter_context
        sb = lambda name, shape, dt=F32: room.take(name, shape, dt)
        sem = lambda name: c(nc.semaphore(tag + name))
        k_hh = sb("k_hi_hi", [P, C_KV, NS * P], F32R)
        k_ll = sb("k_lo_lo", [P, C_KV, NS * P], F32R)
        ki_hh = sb("k_idx_hi_hi", [P, NS * P], F32R)
        ki_ll = sb("k_idx_lo_lo", [P, NS * P], F32R)
        q_tok = sb("q_split", [P, HP, 2, HD], F32R)
        qS = sb("q_stacked", [P, 2, HP, P], F32R)
        qi_tok = sb("q_idx_split", [P, 2, IDX_HEADS, 2, HD], F32R)
        qiS = sb("q_idx_stacked", [P, IDX_HEADS, P], F32R)
        idx = sb("idx_scores", [P, RING, SEQ])
        early = sb("early_mask", [P, 2 * P])
        top8 = sb("top8", [P, RING, 8])
        nm = sb("minus_max", [P, 2, HP])
        rs = sb("row_sum", [P, 2, HP])
        rden = sb("rden", [P, 2, HP])
        rel = sb("relu", [P, 2, SEQ])
        prep = room.from_here(tag)
        S = sb("scores", [P, 2, SEQ])
        E = sb("probs", [P, 2, SEQ])
        pT = sb("probs_T", [P, 2, 8, P])
        ih = prep.take("k_idx_split_hi", [P, NS, P], F32R)
        il = prep.take("k_idx_split_lo", [P, NS, P], F32R)
        KRING = 3
        kh = prep.take("k_split_hi", [P, KRING, C_KV, 2, HD], F32R)
        kl = prep.take("k_split_lo", [P, KRING, C_KV, 2, HD], F32R)
        ih_made, il_made = sem("k_idx_hi_made"), sem("k_idx_lo_made")
        ihi_turned, ilo_turned = sem("k_idx_hi_turned"), sem("k_idx_lo_turned")
        ihi_copied, ilo_copied = sem("k_idx_hi_copied"), sem("k_idx_lo_copied")
        kh_made, kl_made = sem("k_hi_made"), sem("k_lo_made")
        k_turned, k_copied = sem("keys_turned"), sem("keys_copied")
        q_hi_made, q_lo_made = sem("q_hi_made"), sem("q_lo_made")
        qi_hi_made, qi_lo_made = sem("q_idx_hi_made"), sem("q_idx_lo_made")
        masks = sem("masks_made")
        turned, copied = sem("transposed"), sem("transposes_copied")
        i_done, relu_done, mixed = sem("idx_product_done"), sem("relu_done"), sem("idx_head_added")
        chain = sem("ranking_steps")
        s_done, s_read, e_done = sem("scores_done"), sem("scores_read"), sem("probs_ready")
        o_done, o_read, rden_made = sem("outputs_done"), sem("outputs_read"), sem("rden_made")
        block = c(nc.Block())
        banks = [ps[:, i] for i in range(8)]
        srows = lambda sl: DEC if sl == OWN else P
        wide = lambda use, r, n: ps[0:r, number[use] % 2 * 2:number[use] % 2 * 2 + 2].rearrange("p b c -> p (b c)")[:, 0:n]
        heads_of = lambda x, r: x[0:r].rearrange("p (h d) -> p h d", d=HD)
        quads = lambda bank, r: bank.rearrange("p (b q) -> p b q", q=P)[:, :, 0:r]
        idx_parts = [(slice(0, OWN), P), (slice(OWN, NS), DEC)]
        idx_quads = [range(s0, min(s0 + 4, NS)) for s0 in range(0, NS, 4)]

        def copy_idx_quad(copy, out, bank, quad):
            full = [sl for sl in quad if sl != OWN]
            last = copy(out[:, full[0] * P:(full[-1] + 1) * P], bank[:, 0:len(full) * P])
            if OWN in quad:
                last = copy(out[:, OWN * P:OWN * P + DEC], bank[:, len(full) * P:len(full) * P + DEC])
            return last

        @block.gpsimd
        def _(pool):
            pool.memset(early[:], 0.0).then_inc(masks, 1)
            pool.wait_ge(masks, 1)
            pool.memset(early[0:CHUNK, 3 * CHUNK:], MASKED).then_inc(masks, 1)

            def q_idx_low(m):
                r = rows(RANKED[m])
                pool.wait_ge(qi_hi_made, m + 1)
                pool.tensor_tensor(qi_tok[0:r, m % 2, :, 1], heads_of(qi[:, RANKED[m]], r), qi_tok[0:r, m % 2, :, 0],
                                   ALU.subtract).then_inc(qi_lo_made, 1)

            def q_low(p):
                r = rows(ORDER[p])
                pool.wait_ge(q_hi_made, p + 1)
                pool.tensor_tensor(q_tok[0:r, :, 1], heads_of(A[:, ORDER[p]], r), q_tok[0:r, :, 0],
                                   ALU.subtract).then_inc(q_lo_made, 1)

            for m in range(FIRST):
                q_idx_low(m)
            for sl in range(NS):
                r = srows(sl)
                pool.wait_ge(kh_made, sl + 1)
                pool.tensor_tensor(kl[0:r, sl % KRING], heads_of(kc[:, sl], r).unsqueeze(2).to_broadcast([r, C_KV, 2, HD]),
                                   kh[0:r, sl % KRING], ALU.subtract).then_inc(kl_made, 1)
                if sl == 0:
                    q_low(0)
            q_idx_low(FIRST)
            for p in range(NT - 1):
                if p + 1 >= RING and p + 1 < NR:
                    q_idx_low(p + 1)
                q_low(p + 1)

        @block.scalar
        def _(act):
            n = [0]

            def copy(out, bank):
                act.wait_ge(turned, n[0] + 1)
                act.copy(out, bank).then_inc(copied, 1)
                n[0] += 1

            def q_idx_high(m):
                r = rows(RANKED[m])
                if m >= 2:
                    act.wait_ge(i_done, IDX_HEADS * (m - 1))
                act.copy(qi_tok[0:r, m % 2, :, 0], heads_of(qi[:, RANKED[m]], r)).then_inc(qi_hi_made, 1)

            def q_high(p):
                r = rows(ORDER[p])
                if p >= 1:
                    act.wait_ge(s_done, HP * (p - 1) + 1)
                act.copy(q_tok[0:r, :, 0], heads_of(A[:, ORDER[p]], r)).then_inc(q_hi_made, 1)

            def idx_queries(m):
                r = rows(RANKED[m])
                if m >= 1:
                    act.wait_ge(i_done, IDX_HEADS * m)
                copy(qiS[:, :, 0:r], quads(banks[4 + n[0] % 2], r))

            def item(m, i):
                t = RANKED[m]
                r, nk, y = rows(t), nkeys(t), IDX_HEADS * m + i
                act.wait_ge(i_done, y + 1)
                if y >= 2:
                    act.wait_ge(mixed, y - 1)
                act.activation(rel[0:r, i % 2, 0:nk], wide(("item", m, i), r, nk), ACT.Relu,
                               scale=(HD * IDX_HEADS) ** -0.5).then_inc(relu_done, 1)

            def k_high(sl):
                r = srows(sl)
                if sl >= KRING:
                    act.wait_ge(k_turned, 2 * (sl - KRING) + 2)
                act.copy(kh[0:r, sl % KRING], heads_of(kc[:, sl], r).unsqueeze(2).to_broadcast([r, C_KV, 2, HD])).then_inc(kh_made, 1)

            def queries(p, g):
                r = rows(ORDER[p])
                if p >= 2 and g == 0:
                    act.wait_ge(s_done, HP * (p - 1))
                copy(qS[:, p % 2, 4 * g:4 * g + 4, 0:r], quads(banks[4 + n[0] % 2], r))

            def exp(x):
                p, h = divmod(x, HP)
                r, nk = rows(ORDER[p]), nkeys(ORDER[p])
                act.wait_ge(s_read, x + 1)
                act.activation(E[0:r, x % 2, 0:nk], S[0:r, x % 2, 0:nk], ACT.Exp, bias=nm[0:r, p % 2, h:h + 1],
                               scale=-1.0, accum_out=rs[0:r, p % 2, h:h + 1]).then_inc(e_done, 1)

            def copy_probs(x):
                t = ORDER[x // HP]
                r = rows(t)
                if x >= 2:
                    act.wait_ge(o_done, x - 1)
                for g in range(groups(t)):
                    nb = min(4, blocks(t) - 4 * g)
                    bank = quads(banks[4 + n[0] % 2], r)
                    last = width(t, 4 * g + nb - 1)
                    if last == P:
                        copy(pT[:, x % 2, 4 * g:4 * g + nb, 0:r], bank[:, 0:nb])
                    else:
                        act.wait_ge(turned, n[0] + 1)
                        act.copy(pT[:, x % 2, 4 * g:4 * g + nb - 1, 0:r], bank[:, 0:nb - 1])
                        copy(pT[0:last, x % 2, 4 * g + nb - 1, 0:r], bank[0:last, nb - 1])

            for part, r in idx_parts:
                act.copy(ih[0:r, part], ki[0:r, part]).then_inc(ih_made, 1)
            for m in range(FIRST):
                q_idx_high(m)
            for g, quad in enumerate(idx_quads):
                act.wait_ge(ihi_turned, g + 1)
                copy_idx_quad(act.copy, ki_hh, banks[g], quad).then_inc(ihi_copied, 1)
            q_high(0)
            k_high(0)
            for m in range(FIRST):
                idx_queries(m)
                for i in range(IDX_HEADS):
                    item(m, i)
            for sl in range(NS):
                r = srows(sl)
                if sl + 1 < NS:
                    k_high(sl + 1)
                for part, keys in enumerate((k_hh, k_ll)):
                    act.wait_ge(k_turned, 2 * sl + part + 1)
                    act.copy(keys[:, :, sl * P:sl * P + r], quads(banks[2 * part + sl % 2], r)).then_inc(k_copied, 1)
            q_idx_high(FIRST)
            for g in range(4):
                queries(0, g)
            idx_queries(FIRST)
            for x in range(-1, HP * NT):
                p, h = divmod(x, HP)
                if x >= 0:
                    copy_probs(x)
                    if p + 1 < NT:
                        if h == 2 and RING <= p + 1 < NR:
                            q_idx_high(p + 1)
                        if h == 5:
                            q_high(p + 1)
                        if h == 7 and RING <= p + 1 < NR:
                            idx_queries(p + 1)
                        if h in QUERY_AT:
                            queries(p + 1, QUERY_AT.index(h))
                if x + 1 < HP * NT:
                    exp(x + 1)
                    for m, i in items_at[x + 1]:
                        item(m, i)

        @block.vector
        def _(dve):
            steps = [0]
            last = {}

            def step(m, ins):
                steps[0] += 1
                last[m] = steps[0]
                ins.then_inc(chain, 1)

            for part, r in idx_parts:
                dve.wait_ge(ih_made, 1 if r == P else 2)
                dve.tensor_tensor(il[0:r, part], ki[0:r, part], ih[0:r, part], ALU.subtract).then_inc(il_made, 1)
            for g, quad in enumerate(idx_quads):
                dve.wait_ge(ilo_turned, g + 1)
                copy_idx_quad(dve.tensor_copy, ki_ll, banks[len(idx_quads) + g], quad).then_inc(ilo_copied, 1)

            def mix(m, i):
                t = RANKED[m]
                r, nk, y = rows(t), nkeys(t), IDX_HEADS * m + i
                out = idx[0:r, m % RING, 0:nk]
                dve.wait_ge(relu_done, y + 1)
                src, w = rel[0:r, i % 2, 0:nk], wi[0:r, t, i:i + 1]
                if i == 0:
                    if m >= RING:
                        dve.wait_ge(s_read, HP * m)
                    dve.tensor_scalar(out, src, w, None, ALU.mult).then_inc(mixed, 1)
                else:
                    dve.wait_ge(mixed, y)
                    dve.scalar_tensor_tensor(out=out, in0=src, scalar=w, in1=out, op0=ALU.mult, op1=ALU.add).then_inc(mixed, 1)
                if i == IDX_HEADS - 1:
                    dve.wait_ge(mixed, y + 1)
                    if t < SAMPLE:
                        step(m, dve.memset(idx[0:CHUNK, m % RING, nk - CHUNK:nk], BARRED))

            def scored(m):
                return idx[0:rows(RANKED[m]), m % RING, 0:nkeys(RANKED[m])]

            def take(ranks):
                for m in ranks:
                    if m in last:
                        dve.wait_ge(chain, last[m])
                    step(m, dve.max(top8[0:rows(RANKED[m]), m % RING], scored(m)))
                for m in ranks:
                    dve.wait_ge(chain, last[m])
                    step(m, dve.match_replace(scored(m), top8[0:rows(RANKED[m]), m % RING], scored(m), TAKEN))

            def close(m):
                dve.wait_ge(chain, last[m])
                step(m, dve.tensor_scalar(scored(m), scored(m), TAKEN, MASKED, ALU.not_equal, ALU.mult))

            def scores(x):
                p, h = divmod(x, HP)
                t = ORDER[p]
                r, nk = rows(t), nkeys(t)
                mask = scored(p - FIRST) if p >= FIRST else early[0:r, 2 * P - nk:2 * P]
                if h == 0 and p >= FIRST:
                    dve.wait_ge(chain, last[p - FIRST])
                dve.wait_ge(s_done, x + 1)
                if x >= 2:
                    dve.wait_ge(e_done, x - 1)
                dve.tensor_tensor_reduce(S[0:r, x % 2, 0:nk], wide(("head", x), r, nk), mask, -HD ** -0.5, LARGE,
                                         ALU.add, ALU.min, nm[0:r, p % 2, h:h + 1]).then_inc(s_read, 1)

            def outputs(p, b):
                t, r = ORDER[p], rows(ORDER[p])
                dve.wait_ge(e_done, HP * p + 8 * b + 8)
                if p >= 2:
                    dve.wait_ge(o_read, 2 * (p - 2) + b + 1)
                dve.reciprocal(rden[0:r, p % 2, 8 * b:8 * b + 8], rs[0:r, p % 2, 8 * b:8 * b + 8]).then_inc(rden_made, 1)
                dve.wait_ge(rden_made, 2 * p + b + 1)
                dve.wait_ge(o_done, HP * p + 8 * b + 8)
                dve.tensor_tensor(A[0:r, t, b * COLS:(b + 1) * COLS].rearrange("p (h d) -> p h d", d=HD),
                                  heads_of(banks[6 + b], r), rden[0:r, p % 2, 8 * b:8 * b + 8].unsqueeze(2).to_broadcast([r, 8, HD]),
                                  ALU.mult).then_inc(o_read, 1)

            for m in range(FIRST):
                for i in range(IDX_HEADS):
                    mix(m, i)
            for _ in range(AHEAD):
                take(range(FIRST))
            close(0)
            dve.wait_ge(masks, 2)
            for x in range(HP * NT):
                p, h = divmod(x, HP)
                scores(x)
                for m, i in mixes_at[x]:
                    mix(m, i)
                left = list(rounds_at[x])
                while left:
                    together = sorted(set(left))
                    take(together)
                    for m in together:
                        left.remove(m)
                if h == 3 and p >= 1:
                    outputs(p - 1, 1)
                if h == 11:
                    outputs(p, 0)
                if h == HP - 1 and 2 <= p < NT - 1:
                    close(p - 1)
            outputs(NT - 1, 1)

        @block.tensor
        def _(pe):
            n = [0]

            def group(pairs, unit):
                bank = banks[4 + n[0] % 2]
                if n[0] >= 2:
                    pe.wait_ge(copied, n[0] - 1)
                for at, src, r in pairs:
                    out = bank[0:src.shape[1], at:at + r]
                    mm = pe.transpose(out if unit is ident else out.bitcast(F32R), src, unit[0:r, 0:r])
                mm.then_inc(turned, 1)
                n[0] += 1

            flat = lambda x: x.rearrange("p two d -> p (two d)")
            turn = lambda bank, at, src: pe.transpose(bank[:, at:at + src.shape[0]].bitcast(F32R), src,
                                                      ident_r[0:src.shape[0], 0:src.shape[0]])

            def queries(p, g):
                r = rows(ORDER[p])
                if g == 0:
                    pe.wait_ge(q_lo_made, p + 1)
                group([(i * P, flat(q_tok[0:r, 4 * g + i]), r) for i in range(4)], ident_r)

            def product(use, r, nk, q, k_hi, k_lo, done):
                k = number[use]
                if k >= 2:
                    before = uses[k - 2]
                    if before[0] == "item":
                        pe.wait_ge(relu_done, IDX_HEADS * before[1] + before[2] + 1)
                    else:
                        pe.wait_ge(s_read, before[1] + 1)
                for c0 in range(0, nk, COLS):
                    w = min(COLS, nk - c0)
                    out = ps[0:r, k % 2 * 2 + c0 // COLS, 0:w]
                    pe.matmul(out, q, k_hi[:, c0:c0 + w], start=True, stop=False)
                    mm = pe.matmul(out, q, k_lo[:, c0:c0 + w], start=False, stop=True)
                mm.then_inc(done, 1)

            idx_group = {}

            def idx_queries(m):
                r = rows(RANKED[m])
                pe.wait_ge(qi_lo_made, m + 1)
                group([(h * P, flat(qi_tok[0:r, m % 2, h]), r) for h in range(IDX_HEADS)], ident_r)
                idx_group[m] = n[0]

            def item(m, i):
                t = RANKED[m]
                r, nk, k0 = rows(t), nkeys(t), key0(t)
                if i == 0:
                    pe.wait_ge(copied, idx_group[m])
                product(("item", m, i), r, nk, qiS[:, i, 0:r], ki_hh[:, k0:k0 + nk], ki_ll[:, k0:k0 + nk], i_done)

            query_groups = {}

            def scores(x):
                p, h = divmod(x, HP)
                t = ORDER[p]
                r, nk, k0 = rows(t), nkeys(t), key0(t)
                kv = h // (C_HEADS // C_KV)
                if h == 0:
                    pe.wait_ge(copied, query_groups[p])
                product(("head", x), r, nk, qS[:, p % 2, h, 0:r], k_hh[:, kv, k0:k0 + nk], k_ll[:, kv, k0:k0 + nk], s_done)

            def transposes(x):
                t = ORDER[x // HP]
                r = rows(t)
                pe.wait_ge(e_done, x + 1)
                for g in range(groups(t)):
                    group([(b % 4 * P, E[0:r, x % 2, b * P:b * P + width(t, b)], r)
                           for b in range(4 * g, min(4 * g + 4, blocks(t)))], ident)

            def values(x, at):
                p, h = divmod(x, HP)
                t = ORDER[p]
                r = rows(t)
                kv, b = h // (C_HEADS // C_KV), h // 8
                pe.wait_ge(copied, at)
                if h % 8 == 0 and p >= 1:
                    pe.wait_ge(o_read, 2 * p + b - 1)
                o = h % 8 * HD
                for kb in range(blocks(t)):
                    w = width(t, kb)
                    mm = pe.matmul(banks[6 + b][0:r, o:o + HD], pT[0:w, x % 2, kb, 0:r],
                                   vc[0:w, slot0(t) + kb, kv * HD:(kv + 1) * HD], start=(kb == 0), stop=(kb == blocks(t) - 1))
                mm.then_inc(o_done, 1)

            for part, (split, made, done) in enumerate(((ih, ih_made, ihi_turned), (il, il_made, ilo_turned))):
                for g, quad in enumerate(idx_quads):
                    if g == 0:
                        pe.wait_ge(made, 2)
                    for b, sl in enumerate(quad):
                        mm = turn(banks[part * len(idx_quads) + g], b * P, split[0:srows(sl), sl])
                    mm.then_inc(done, 1)
            pe.wait_ge(ihi_copied, len(idx_quads))
            pe.wait_ge(ilo_copied, len(idx_quads))
            for m in range(FIRST):
                idx_queries(m)
                for i in range(IDX_HEADS):
                    item(m, i)
            pe.wait_ge(relu_done, FIRST * IDX_HEADS)
            for sl in range(NS):
                r = srows(sl)
                for part, (split, made) in enumerate(((kh, kh_made), (kl, kl_made))):
                    pe.wait_ge(made, sl + 1)
                    if sl >= 2:
                        pe.wait_ge(k_copied, 2 * (sl - 2) + part + 1)
                    for kv in range(C_KV):
                        mm = turn(banks[2 * part + sl % 2], kv * P, flat(split[0:r, sl % KRING, kv]))
                    mm.then_inc(k_turned, 1)
            for g in range(4):
                queries(0, g)
            query_groups[0] = n[0]
            idx_queries(FIRST)
            pe.wait_ge(k_copied, 2 * NS)
            ready = {}
            for x in range(-1, HP * NT):
                p, h = divmod(x, HP)
                if x + 1 < HP * NT:
                    scores(x + 1)
                    for m, i in items_at[x + 1]:
                        item(m, i)
                if x >= 0:
                    transposes(x)
                    ready[x] = n[0]
                    if h == 7 and RING <= p + 1 < NR:
                        idx_queries(p + 1)
                    if h in QUERY_AT and p + 1 < NT:
                        queries(p + 1, QUERY_AT.index(h))
                        query_groups[p + 1] = n[0]
                    if x >= 1:
                        values(x - 1, ready[x - 1])
            values(HP * NT - 1, ready[HP * NT - 1])


def rope_table():
    inv = np.exp(-np.float32(np.log(THETA)) * np.arange(HALF, dtype=np.float32) / np.float32(HALF)).astype(np.float32)
    pos = np.concatenate([np.arange(SEQ), PAST + np.arange(DEC)]).astype(np.float32)
    ang = (pos[:, None] * inv[None, :]).astype(np.float32)
    cos, sin = np.cos(ang), np.sin(ang)
    return np.concatenate([cos, cos, -sin, sin], axis=1).astype(np.float32)


OUTPUTS = [
    ("y_prompt", (SEQ, D), (1, SEQ, D)),
    ("y_sample", (DEC, D), (1, DEC, D)),
    ("p_b_k", (B_WIN, B_KV * HD), (1, 1, B_WIN, B_KV, HD)),
    ("p_b_v", (B_WIN, B_KV * HD), (1, 1, B_WIN, B_KV, HD)),
    ("p_c_k", (SEQ, C_KVW), (1, 1, SEQ, C_KV, HD)),
    ("p_c_v", (SEQ, C_KVW), (1, 1, SEQ, C_KV, HD)),
    ("p_c_idx", (SEQ, HD), (1, 1, SEQ, HD)),
    ("s_a_v", (DEC, A_WIDTH), (1, 1, DEC, A_WIDTH)),
    ("s_b_k", (DEC, B_KV * HD), (1, 1, DEC, B_KV, HD)),
    ("s_b_v", (DEC, B_KV * HD), (1, 1, DEC, B_KV, HD)),
    ("s_c_k", (DEC, C_KVW), (1, 1, DEC, C_KV, HD)),
    ("s_c_v", (DEC, C_KVW), (1, 1, DEC, C_KV, HD)),
    ("s_c_idx", (DEC, HD), (1, 1, DEC, HD)),
]


def kernel(x_prompt, x_sample, cache_b_k, cache_b_v, cache_c_k, cache_c_v, cache_c_idx,
           ab_w_in, a_ln_g, a_ln_b, a_ws, a_bs, b_sinks, ab_w_out, c_w_in, c_w_out,
           ln1_g, ln1_b, ln2_g, ln2_b, ff_w1, ff_w2):
    import concourse.bacc as bacc
    from concourse.bass_utils import run_bass_kernel_spmd

    x = np.concatenate([np.asarray(x_prompt)[0], np.asarray(x_sample)[0]], axis=0)
    ins = {
        "x": x,
        "xT": x.T,
        "cache_b_k": np.asarray(cache_b_k).reshape(B_WIN, B_KV * HD),
        "cache_b_v": np.asarray(cache_b_v).reshape(B_WIN, B_KV * HD),
        "cache_c_k": np.asarray(cache_c_k).reshape(PAST, C_KVW),
        "cache_c_v": np.asarray(cache_c_v).reshape(PAST, C_KVW),
        "cache_c_idx": np.asarray(cache_c_idx).reshape(PAST, HD),
        "ab_w_in": np.asarray(ab_w_in)[0],
        "a_ln_g": np.asarray(a_ln_g),
        "a_ln_b": np.asarray(a_ln_b),
        "ws_T": np.asarray(a_ws)[0].transpose(2, 0, 1),
        "bs_T": np.asarray(a_bs)[0].T,
        "sinks": np.asarray(b_sinks),
        "ab_w_out": np.asarray(ab_w_out)[0],
        "c_w_in": np.asarray(c_w_in)[0],
        "c_w_out": np.asarray(c_w_out)[0],
        "ln1_g": np.asarray(ln1_g), "ln1_b": np.asarray(ln1_b),
        "ln2_g": np.asarray(ln2_g), "ln2_b": np.asarray(ln2_b),
        "ff_w1": np.asarray(ff_w1), "ff_w2": np.asarray(ff_w2),
        "rope": rope_table(),
    }
    ins = {k: np.ascontiguousarray(v) for k, v in ins.items()}
    nc = bacc.Bacc("TRN2", target_bir_lowering=False, num_devices=1)
    aps, arrays = {}, {}
    for k, v in ins.items():
        arrays[f"in_{k}"] = v
        aps[k] = nc.dram_tensor(f"in_{k}", v.shape, mybir.dt.from_np(v.dtype), kind="ExternalInput").ap()
    for k, shape, _ in OUTPUTS:
        aps[k] = nc.dram_tensor(f"out_{k}", shape, F32, kind="ExternalOutput").ap()
    encoder(nc, aps)
    got = run_bass_kernel_spmd(nc, [arrays], core_ids=[0]).results[0]
    return tuple(np.asarray(got[f"out_{k}"]).reshape(shape) for k, _, shape in OUTPUTS)
```

```python
from contextlib import ExitStack

import numpy as np

import concourse.bass as bass
from concourse import mybir

ALU = mybir.AluOpType
ACT = mybir.ActivationFunctionType
F32 = mybir.dt.float32
F32R = mybir.dt.float32r

P = 128
D = 1024
KT = D // P
SEQ = 1024
DEC = 64
TOK = SEQ + DEC
NP_TILES = SEQ // P
NT = NP_TILES + 1
SAMPLE = NP_TILES
CHUNK = 64
HD = 64
HALF = HD // 2
D_FF = 4 * D
DEPTH = 2
ALPHA = (2.0 * DEPTH) ** 0.25
EPS = 1e-5
THETA = 10000.0
PAST = 256

A_WIDTH = D // 2
A_GROUPS = 8
A_GD = A_WIDTH // A_GROUPS
B_HEADS = 8
B_KV = 2
B_WIN = 128
AB_IN = 2 * A_WIDTH + B_HEADS * HD + 2 * B_KV * HD

C_HEADS = 16
C_KV = 4
IDX_HEADS = 4
C_Q = C_HEADS * HD
C_KVW = C_KV * HD
C_QI = IDX_HEADS * HD
C_IN = C_Q + 2 * C_KVW + C_QI + HD + IDX_HEADS
TOPK = 256
TOPK_SAMPLE = min(TOPK, (PAST + DEC) // 4)

COLS = 512
QUARTER = KT // 4
W_SLOTS = 5
FC = 256
N_FC = D_FF // FC
FT = FC // P

MASKED = -1e30
BARRED = -3.0e38
TAKEN = -3.3e38
LARGE = 3.0e38

IDX_COL = C_Q + 2 * C_KVW
IDX_W = C_QI + HD + IDX_HEADS

C_ORDER = [0, 1, SAMPLE, 7, 6, 5, 4, 3, 2]
UNRANKED = 2
C_RANKED = C_ORDER[UNRANKED:]
KEY_SLOTS = NT + 2
OWN = NT + 1


def rows(t):
    return P if t < SAMPLE else DEC


def nkeys(t):
    return (t + 1) * P if t < SAMPLE else PAST + DEC


def key0(t):
    return 0 if t < SAMPLE else NP_TILES * P


def rounds(m):
    return (TOPK if C_RANKED[m] < SAMPLE else TOPK_SAMPLE) // 8


ROUND_TILES = 7
ROUNDS_BEFORE = 2 * ROUND_TILES
ROUNDS_AHEAD = 5
RING = 3
IDX_WIDTH = [max(nkeys(t) for t in C_RANKED[n::RING]) for n in range(RING)]
rows_of_slot = lambda sl: DEC if sl == OWN else P
KEY_QUADS = [range(s0, min(s0 + 4, KEY_SLOTS)) for s0 in range(0, KEY_SLOTS, 4)]


def tok(t):
    return t * P, t * P + rows(t)


RANGES = [(0, 384), (384, 768), (768, TOK)]


class Room:

    def __init__(self, nc, tag, at, end=None):
        self.nc, self.tag, self.at, self.end = nc, tag, at, end or nc.sbuf_usable_end

    def take(self, name, shape, dtype=F32):
        size = 4 * int(np.prod(shape[1:]))
        x = self.nc.alloc_sbuf_tensor_at(self.tag + name, shape, dtype, offset=self.at)
        self.at += -(-size // 32) * 32
        assert self.at <= self.end, (self.tag, name, self.at - self.end)
        return x

    def from_here(self, tag):
        return Room(self.nc, tag, self.at, self.end)


def encoder(nc, aps):
    with ExitStack() as ctx:
        base = Room(nc, "", -(-nc.sbuf_base // 64) * 64)
        act_at = base.at
        A = base.take("act", [P, NT, D])
        ident = base.take("ident", [P, P])
        ident_r = base.take("ident_r", [P, P], F32R)
        mhalf = base.take("minus_half", [P, 1])
        ps = ctx.enter_context(nc.psum_tensor("psum", [P, 8, COLS], F32))
        x2_stored, y_stored = [ctx.enter_context(nc.semaphore(n)) for n in ("x2_stored", "y_stored")]
        x2_dram = nc.dram_tensor("x2_scratch", (TOK, D), F32, kind="Internal").ap()
        aps = dict(aps, x2=x2_dram)
        keep_b = base.from_here("b_")
        va = keep_b.take("va", [P, NT, A_WIDTH])
        kb = keep_b.take("k", [P, NT + 1, P])
        vb = keep_b.take("v", [P, NT + 1, P])
        keep_c = base.from_here("c_")
        kc = keep_c.take("k", [P, NT + 2, C_KVW])
        vc = keep_c.take("v", [P, NT + 2, C_KVW])
        ki = keep_c.take("k_idx", [P, NT + 2, 2 * HD])
        qi = keep_c.take("q_idx", [P, NT, C_QI])
        wi = keep_c.take("w_idx", [P, NT, IDX_HEADS])
        split = Room(nc, "", max(keep_b.at, keep_c.at))
        xt_hi = split.take("xt_hi", [P, KT, TOK], F32R)
        xt_lo = split.take("xt_lo", [P, KT, TOK], F32R)
        top_at = (nc.sbuf_usable_end - 4 * (sum(IDX_WIDTH) + 8 * RING)) // 32 * 32
        top = Room(nc, "c_", top_at)
        rank0_at = top_at + 4 * (IDX_WIDTH[0] - nkeys(C_RANKED[0]))
        idx = [top.take(f"idx_scores{n}", [P, w]) for n, w in enumerate(IDX_WIDTH)]
        top8 = top.take("top8", [P, RING, 8])

        w1_at = (split.end - 2 * 4 * KT * FC) // 32 * 32
        piece = 4 * QUARTER * COLS
        early_c = EarlyPieces(nc, ctx, "c_in_", [base.at + n * 4 * QUARTER * IDX_W for n in range(3)],
                              aps["c_w_in"], IDX_COL, IDX_W)
        early_0 = EarlyPieces(nc, ctx, "out0_", [w1_at + n * piece for n in range(3)], aps["ab_w_out"], 0, COLS)
        early_1 = EarlyPieces(nc, ctx, "out1_", [top_at - piece, top_at + 4 * IDX_WIDTH[0]], aps["c_w_out"], 0, COLS)

        block_ab_in(nc, aps, split.from_here("ab_in_"), keep_b.from_here("ab_in_"), A, xt_hi, xt_lo, va, kb, vb, ident, ident_r, mhalf, ps)
        block_ab_mixer(nc, aps, split.from_here("ab_mix_"), A, va, kb, vb, ident, early_0, ps)
        block_layer(nc, aps, base.from_here("layer0_"), split.from_here("layer0w_"), 0, aps["x"], aps["ab_w_out"], A,
                    xt_hi, xt_lo, ident, mhalf, x2_stored, early_0, ps, early_c)
        block_c_in(nc, aps, Room(nc, "c_in_", split.at, rank0_at), Room(nc, "c_in_scratch_", act_at, act_at + 4 * NT * D),
                   A, xt_hi, xt_lo, kc, vc, ki, qi, wi, idx, top8, ident_r, x2_stored, early_c, ps)
        block_c_mixer(nc, Room(nc, "c_mix_", max(keep_b.at, keep_c.at), top_at - piece), A, kc, vc, ki, qi, wi, idx, top8,
                      ident, ident_r, early_1, ps)
        block_layer(nc, aps, base.from_here("layer1_"), split.from_here("layer1w_"), 1, aps["x2"], aps["c_w_out"], A,
                    xt_hi, xt_lo, ident, mhalf, y_stored, early_1, ps)


class EarlyPieces:

    def __init__(self, nc, ctx, tag, places, w, c0, width):
        self.arrived = ctx.enter_context(nc.semaphore(tag + "early_arrived"))
        self.pieces = [nc.alloc_sbuf_tensor_at(tag + f"w_early{n}", [P, QUARTER, width], F32, offset=at)
                       for n, at in enumerate(places)]
        self.w, self.columns = w.rearrange("(k p) n -> p k n", p=P), slice(c0, c0 + width)

    def load(self, eng, n):
        eng.dma_start(self.pieces[n][:], self.w[:, QUARTER * n:QUARTER * (n + 1), self.columns]).then_inc(self.arrived, 16)


class Stream:

    def __init__(self, nc, c, tag, room, w, chunks, done, early=(), early_arrived=None):
        self.early, self.early_arrived = early, early_arrived
        self.n_early = len(early)
        self.w = w.rearrange("(k p) n -> p k n", p=P)
        self.chunks = chunks
        self.n = 4 * len(chunks)
        self.raw = room.take("w_raw", [P, 2, QUARTER, COLS], F32)
        self.hi = room.take("w_hi", [P, W_SLOTS, QUARTER, COLS], F32R)
        self.lo = room.take("w_lo", [P, W_SLOTS, QUARTER, COLS], F32R)
        self.arrived = [c(nc.semaphore(tag + f"w_arrived{i}")) for i in range(2)]
        self.hi_made = c(nc.semaphore(tag + "w_hi_made"))
        self.lo_made = c(nc.semaphore(tag + "w_lo_made"))
        self.used = c(nc.semaphore(tag + "w_used"))
        self.done = done

    def raw_piece(self, n):
        w = self.chunks[n // 4][1]
        return self.early[n][:] if n < self.n_early else self.raw[:, (n - self.n_early) % 2, :, 0:w]

    def load(self, eng, n):
        if n < self.n_early:
            return
        j, q = divmod(n, 4)
        c0, w = self.chunks[j]
        if n >= self.n_early + 2:
            eng.wait_ge(self.lo_made, n - 1)
        eng.dma_start(self.raw_piece(n), self.w[:, QUARTER * q:QUARTER * q + QUARTER, c0:c0 + w]).then_inc(
            self.arrived[(n - self.n_early) % 2], 16)

    def split_hi(self, act, n):
        w = self.chunks[n // 4][1]
        if n < self.n_early:
            act.wait_ge(self.early_arrived, 16 * self.n_early)
        else:
            act.wait_ge(self.arrived[(n - self.n_early) % 2], 16 * ((n - self.n_early) // 2 + 1))
        if n >= W_SLOTS:
            j, q = divmod(n - W_SLOTS, 4)
            if q < 3:
                act.wait_ge(self.used, 3 * j + q + 1)
            else:
                act.wait_ge(self.done, NT * (j + 1))
        act.copy(self.hi[:, n % W_SLOTS, :, 0:w], self.raw_piece(n)).then_inc(self.hi_made, 1)

    def split_lo(self, dve, n):
        w = self.chunks[n // 4][1]
        dve.wait_ge(self.hi_made, n + 1)
        dve.tensor_tensor(self.lo[:, n % W_SLOTS, :, 0:w], self.raw_piece(n),
                          self.hi[:, n % W_SLOTS, :, 0:w], ALU.subtract).then_inc(self.lo_made, 1)

    def next_pieces(self, j):
        return range(4 * j + W_SLOTS, min(4 * j + 4 + W_SLOTS, self.n))

    def product(self, pe, out, t, j, xt_hi, xt_lo):
        a, b = tok(t)
        w = self.chunks[j][1]
        for q in range(4):
            n = 4 * j + q
            if t == 0:
                pe.wait_ge(self.lo_made, n + 1)
            s = n % W_SLOTS
            for k in range(QUARTER):
                kk = QUARTER * q + k
                first, last = kk == 0, kk == KT - 1
                pe.matmul(out[0:b - a, 0:w], xt_hi[:, kk, a:b], self.hi[:, s, k, 0:w], start=first, stop=False)
                pe.matmul(out[0:b - a, 0:w], xt_hi[:, kk, a:b], self.lo[:, s, k, 0:w], start=False, stop=False)
                mm = pe.matmul(out[0:b - a, 0:w], xt_lo[:, kk, a:b], self.hi[:, s, k, 0:w], start=False, stop=last)
            if t == NT - 1 and q < 3:
                mm.then_inc(self.used, 1)
        mm.then_inc(self.done, 1)


class Norm:

    def __init__(self, nc, c, tag, room, name, width, g_row, b_row, tail=0):
        self.width, self.g_row, self.b_row = width, g_row, b_row
        self.pool_tiles = NT - tail
        self.g = room.take(f"{name}_g", [P, width], F32)
        self.b = room.take(f"{name}_b", [P, width], F32)
        self.stats = room.take(f"{name}_stats", [P, 2, 6 * (width // COLS)], F32)
        self.mv = room.take(f"{name}_mv", [P, NT, 2], F32)
        self.var = room.take(f"{name}_var", [P, NT], F32)
        self.rstd = room.take(f"{name}_rstd", [P, NT], F32)
        self.shift = room.take(f"{name}_shift", [P, NT], F32)
        s = lambda what: c(nc.semaphore(tag + f"{name}_{what}"))
        self.loaded, self.chain, self.var_ready, self.rstd_ready = s("loaded"), s("chain"), s("var_ready"), s("rstd_ready")
        self.shift_ready, self.normalised, self.scaled, self.done = s("shift_ready"), s("normalised"), s("scaled"), s("done")
        self.tail_done = s("tail_done")
        self.links = 0

    def load(self, eng):
        eng.dma_start(self.g[:], self.g_row.to_broadcast([P, self.width])).then_inc(self.loaded, 16)
        eng.dma_start(self.b[:], self.b_row.to_broadcast([P, self.width])).then_inc(self.loaded, 16)

    def link(self, dve, ins):
        self.links += 1
        ins.then_inc(self.chain, 1)
        dve.wait_ge(self.chain, self.links)

    def statistics(self, dve, x, t):
        r, st = rows(t), self.stats[:, t % 2]
        for h in range(self.width // COLS):
            ins = dve.bn_stats(st[0:r, 6 * h:6 * h + 6], x[0:r, COLS * h:COLS * h + COLS])
        self.link(dve, ins)
        self.link(dve, dve.bn_aggr(self.mv[0:r, t], st[0:r]))
        dve.tensor_scalar(self.var[0:r, t:t + 1], self.mv[0:r, t, 1:2], EPS, None, ALU.add).then_inc(self.var_ready, 1)

    def rsqrt(self, pool, mhalf, t):
        r = rows(t)
        pool.wait_ge(self.var_ready, t + 1)
        pool.tensor_tensor(self.rstd[0:r, t:t + 1], self.var[0:r, t:t + 1], mhalf[0:r], ALU.pow).then_inc(self.rstd_ready, 1)
        pool.wait_ge(self.rstd_ready, t + 1)
        pool.tensor_scalar(self.shift[0:r, t:t + 1], self.mv[0:r, t, 0:1], self.rstd[0:r, t:t + 1], -1.0,
                           ALU.mult, ALU.mult).then_inc(self.shift_ready, 1)

    def normalise(self, act, x, t):
        r = rows(t)
        act.wait_ge(self.shift_ready, t + 1)
        act.activation(x[0:r], x[0:r], ACT.Identity, bias=self.shift[0:r, t:t + 1],
                       scale=self.rstd[0:r, t:t + 1]).then_inc(self.normalised, 1)

    def scale(self, dve, x, t):
        r = rows(t)
        if t == 0:
            dve.wait_ge(self.loaded, 32)
        dve.wait_ge(self.normalised, t + 1)
        dve.tensor_tensor(x[0:r], x[0:r], self.g[0:r], ALU.mult).then_inc(self.scaled, 1)

    def offset(self, pool, x, t):
        r = rows(t)
        if t == 0:
            pool.wait_ge(self.loaded, 32)
        pool.wait_ge(self.scaled, t + 1)
        pool.tensor_tensor(x[0:r], x[0:r], self.b[0:r], ALU.add).then_inc(self.done if t < self.pool_tiles else self.tail_done, 1)

    def wait_done(self, eng, t):
        if t < self.pool_tiles:
            eng.wait_ge(self.done, t + 1)
        else:
            eng.wait_ge(self.tail_done, t - self.pool_tiles + 1)


def rope(dve, link, src, table, tmp, heads):
    r = src.shape[0]
    both = lambda c0, w: table[:, c0:c0 + w].unsqueeze(1).to_broadcast([r, heads, w])
    dve.tensor_tensor(tmp[:, 0, 0:heads], src, both(0, HD), ALU.mult)
    dve.tensor_tensor(tmp[:, 1, 0:heads, 0:HALF], src[:, :, HALF:HD], both(HD, HALF), ALU.mult)
    link(dve.tensor_tensor(tmp[:, 1, 0:heads, HALF:HD], src[:, :, 0:HALF], both(HD + HALF, HALF), ALU.mult))


def block_ab_in(nc, aps, room, x_room, A, xt_hi, xt_lo, va, kb, vb, ident, ident_r, mhalf, ps):
    tag = "ab_in_"
    banks = [ps[:, i] for i in range(8)]
    with ExitStack() as s:
        c = s.enter_context
        chunks = [(0, COLS), (COLS, COLS), (2 * COLS, COLS), (3 * COLS, 2 * P)]
        done = c(nc.semaphore(tag + "products_done"))
        st = Stream(nc, c, tag, room, aps["ab_w_in"], chunks, done)
        ln = Norm(nc, c, tag, room, "a_ln", A_WIDTH, aps["a_ln_g"], aps["a_ln_b"])
        xr = x_room.take("xt_raw", [P, 2, KT, P], F32)
        table = room.take("rope_table", [P, NT, P], F32)
        tmp = room.take("rope_tmp", [P, 2, 2, 8, HD], F32)
        x_arrived = [c(nc.semaphore(tag + f"x_arrived{i}")) for i in range(2)]
        table_arrived = c(nc.semaphore(tag + "table_arrived"))
        x_hi = c(nc.semaphore(tag + "x_hi_made"))
        x_lo = c(nc.semaphore(tag + "x_lo_made"))
        evac_act = c(nc.semaphore(tag + "banks_read_by_scalar"))
        evac_dve = c(nc.semaphore(tag + "banks_read_by_vector"))
        chain = c(nc.semaphore(tag + "vector_chain"))
        consts = c(nc.semaphore(tag + "constants"))
        ident_copied = c(nc.semaphore(tag + "ident_copied"))
        ready = c(nc.semaphore(tag + "outputs_ready"))
        block = c(nc.Block())
        xT = aps["xT"].rearrange("(k p) t -> p k t", p=P)

        @block.sync
        def _(sp):
            def load_x(t):
                a, b = tok(t)
                if t >= 2:
                    sp.wait_ge(x_lo, t - 1)
                sp.dma_start(xr[:, t % 2, :, 0:b - a], xT[:, :, a:b]).then_inc(x_arrived[t % 2], 16)

            load_x(0)
            for n in range(4):
                st.load(sp, n)
            sp.dma_start(table[:, 0:NP_TILES], aps["rope"][0:SEQ].rearrange("(t p) c -> p t c", p=P)).then_inc(table_arrived, 16)
            sp.dma_start(table[0:DEC, SAMPLE], aps["rope"][SEQ:TOK]).then_inc(table_arrived, 16)
            ln.load(sp)
            for t in range(1, NT):
                load_x(t)
            for n in range(4, st.n):
                st.load(sp, n)

        @block.gpsimd
        def _(pool):
            pool.memset(mhalf[:], -0.5).then_inc(consts, 1)
            pool.memset(ident[:], 0.0).then_inc(consts, 1)
            pool.wait_ge(consts, 2)
            pool.affine_select(out=ident[:], in_=ident[:], compare_op=ALU.not_equal, fill=1.0, base=0,
                               pattern=[[-1, P]], channel_multiplier=1).then_inc(consts, 1)
            for t in range(NT + 1):
                if t < NT:
                    ln.rsqrt(pool, mhalf, t)
                if t >= 1:
                    ln.offset(pool, va[:, t - 1], t - 1)

        @block.scalar
        def _(act):
            act.wait_ge(consts, 3)
            act.copy(ident_r[:], ident[:]).then_inc(ident_copied, 1)

            def x_high(t):
                a, b = tok(t)
                act.wait_ge(x_arrived[t % 2], 16 * (t // 2 + 1))
                act.copy(xt_hi[:, :, a:b], xr[:, t % 2, :, 0:b - a]).then_inc(x_hi, 1)

            x_high(0)
            for n in range(4):
                st.split_hi(act, n)
            x_high(1)
            for j in range(len(chunks)):
                for t in range(NT):
                    if j == 0 and t + 2 < NT:
                        x_high(t + 2)
                    if j == 0 and t == NT - 2:
                        st.split_hi(act, 4)
                    if t == NT - 1:
                        for n in st.next_pieces(j):
                            st.split_hi(act, n)
                    if j < 2:
                        g, r = j * NT + t, rows(t)
                        act.wait_ge(done, g + 1)
                        out = A[0:r, t, 0:A_WIDTH] if j == 0 else va[0:r, t]
                        act.activation(out, banks[g % 8][0:r], ACT.Gelu_apprx_tanh).then_inc(evac_act, 1)
                    if j == 1 and t >= 1:
                        ln.normalise(act, va[:, t - 1], t - 1)
                if j == 1:
                    ln.normalise(act, va[:, NT - 1], NT - 1)

        @block.vector
        def _(dve):
            links = [0]

            def link(ins):
                links[0] += 1
                ins.then_inc(chain, 1)
                dve.wait_ge(chain, links[0])

            def x_low(t):
                a, b = tok(t)
                dve.wait_ge(x_hi, t + 1)
                dve.tensor_tensor(xt_lo[:, :, a:b], xr[:, t % 2, :, 0:b - a], xt_hi[:, :, a:b],
                                  ALU.subtract).then_inc(x_lo, 1)

            x_low(0)
            for n in range(4):
                st.split_lo(dve, n)
            for t in range(1, NT):
                x_low(t)
            st.split_lo(dve, 4)
            dve.wait_ge(table_arrived, 32)
            for j in range(len(chunks)):
                for t in range(NT):
                    g, r = j * NT + t, rows(t)
                    turn = tmp[0:r, g % 2]
                    if t == NT - 1:
                        for n in st.next_pieces(j):
                            st.split_lo(dve, n)
                    if j == 1:
                        dve.wait_ge(evac_act, g + 1)
                        ln.statistics(dve, va[:, t], t)
                        if t >= 1:
                            ln.scale(dve, va[:, t - 1], t - 1)
                    if j == 2:
                        dve.wait_ge(done, g + 1)
                        if t >= 2:
                            dve.wait_ge(evac_dve, t - 1)
                        src = banks[g % 8][0:r].rearrange("p (h d) -> p h d", d=HD)
                        rope(dve, link, src, table[0:r, t], turn, 8)
                        out = A[0:r, t, A_WIDTH:D].rearrange("p (g kv d) -> p kv g d", kv=B_KV, d=HD)
                        two = lambda i: turn[:, i].rearrange("p (kv g) d -> p kv g d", kv=B_KV)
                        dve.tensor_tensor(out, two(0), two(1), ALU.add).then_inc(evac_dve, 1)
                    if j == 3:
                        slot = t if t < SAMPLE else NT
                        dve.wait_ge(done, g + 1)
                        dve.wait_ge(evac_dve, g - 1 - 2 * NT)
                        src = banks[g % 8][0:r, 0:P].rearrange("p (h d) -> p h d", d=HD)
                        rope(dve, link, src, table[0:r, t], turn, 2)
                        dve.tensor_tensor(kb[0:r, slot].rearrange("p (h d) -> p h d", d=HD),
                                          turn[:, 0, 0:2], turn[:, 1, 0:2], ALU.add).then_inc(ready, 1)
                        dve.tensor_copy(vb[0:r, slot], banks[g % 8][0:r, P:2 * P]).then_inc(evac_dve, 1)
                if j == 1:
                    ln.scale(dve, va[:, NT - 1], NT - 1)

        @block.tensor
        def _(pe):
            for j in range(len(chunks)):
                for t in range(NT):
                    g = j * NT + t
                    if j == 0:
                        pe.wait_ge(x_lo, t + 1)
                    before = g - 8
                    if before >= 0:
                        if before < 2 * NT:
                            pe.wait_ge(evac_act, before + 1)
                        else:
                            pe.wait_ge(evac_dve, before + 1 - 2 * NT)
                    st.product(pe, banks[g % 8], t, j, xt_hi, xt_lo)


def block_ab_mixer(nc, aps, room, A, va, kb, vb, ident, early, ps):
    CACHE, OWN = SAMPLE, NT
    KEY_ORDER = [*range(NP_TILES), OWN, CACHE]
    tag = "ab_mix_"
    banks = [ps[:, i] for i in range(8)]
    with ExitStack() as s:
        c = s.enter_context
        sb = lambda name, shape: room.take(name, shape)
        sem = lambda name: c(nc.semaphore(tag + name))
        wsT = sb("ws_T", [P, A_GROUPS, P])
        bs = sb("bs", [P, A_GROUPS])
        sinks = sb("sinks", [P, B_HEADS])
        nsinks = sb("minus_sinks", [P, B_HEADS])
        mask = sb("mask", [P, 3, 2 * P])
        kT = sb("kT", [P, NT + 1, P])
        qT = sb("qT", [P, 2, 4, P])
        S = sb("scores", [P, B_HEADS, 2 * P])
        E = sb("probs", [P, B_HEADS, 2 * P])
        pT = sb("probs_T", [P, B_HEADS, 2, P])
        nm = sb("minus_max", [P, 2, B_HEADS])
        rs = sb("row_sum", [P, 2, B_HEADS])
        es = sb("sink_shifted", [P, 2, B_HEADS])
        ee = sb("sink_exp", [P, 2, B_HEADS])
        den = sb("den", [P, 2, B_HEADS])
        rden = sb("rden", [P, 2, B_HEADS])
        loaded, cache_arrived, stored = sem("loaded"), sem("cached_keys_arrived"), sem("outputs_stored")
        wmask, masks = sem("ws_masked"), sem("masks_made")
        gate_done, gate_read, ns_made = sem("gate_done"), sem("gate_read"), sem("minus_sinks_made")
        kt_done, kt_read = sem("k_transposed"), sem("k_T_ready")
        qt_done, qt_read = sem("q_transposed"), sem("q_T_ready")
        s_done, s_read = sem("scores_done"), sem("scores_read")
        e_done, ee_done, es_done = sem("probs_ready"), sem("sink_exp_ready"), sem("sink_shifted_ready")
        pt_done, pt_read = sem("p_transposed"), sem("p_T_ready")
        o_done, o_read = sem("out_done"), sem("out_read")
        den_made, rden_made = sem("den_made"), sem("rden_made")
        block = c(nc.Block())
        nkeys = lambda t: P if t == 0 else (2 * P if t < SAMPLE else P + DEC)
        first_slot = lambda t: max(t - 1, 0) if t < SAMPLE else CACHE
        nblocks = lambda t: 1 if t == 0 else 2
        kwidth = lambda t, b: DEC if (t == SAMPLE and b == 1) else P

        def kT_keys(t, half):
            flat = kT[half * HD:half * HD + HD].rearrange("p s k -> p (s k)")
            s0 = first_slot(t) * P
            return flat[:, s0:s0 + nkeys(t)]

        @block.sync
        def _(sp):
            sp.dma_start(wsT[:], aps["ws_T"]).then_inc(loaded, 16)
            sp.dma_start(kb[:, CACHE], aps["cache_b_k"]).then_inc(cache_arrived, 16)
            sp.dma_start(sinks[:], aps["sinks"].to_broadcast([P, B_HEADS])).then_inc(loaded, 16)
            sp.dma_start(bs[:], aps["bs_T"]).then_inc(loaded, 16)
            sp.dma_start(vb[:, CACHE], aps["cache_b_v"]).then_inc(loaded, 16)
            sp.dma_start(aps["p_b_k"], kb[:, NP_TILES - 1]).then_inc(stored, 16)
            sp.dma_start(aps["p_b_v"], vb[:, NP_TILES - 1]).then_inc(stored, 16)
            sp.dma_start(aps["s_b_k"], kb[0:DEC, OWN]).then_inc(stored, 16)
            sp.dma_start(aps["s_b_v"], vb[0:DEC, OWN]).then_inc(stored, 16)
            sp.dma_start(aps["s_a_v"], va[0:DEC, SAMPLE]).then_inc(stored, 16)
            for n in range(len(early.pieces)):
                early.load(sp, n)
            sp.wait_ge(stored, 80)

        @block.gpsimd
        def _(pool):
            pool.wait_ge(loaded, 64)
            pool.affine_select(out=wsT[:], in_=wsT[:], compare_op=ALU.is_ge, fill=0.0, base=0,
                               pattern=[[0, A_GROUPS], [1, P]], channel_multiplier=-1).then_inc(wmask, 1)

        @block.scalar
        def _(act):
            for n, slot in enumerate(KEY_ORDER):
                w = DEC if slot == OWN else P
                act.wait_ge(kt_done, n + 1)
                act.copy(kT[:, slot, 0:w], banks[4 + n % 2][:, 0:w]).then_inc(kt_read, 1)

            def q_copy(t):
                r = rows(t)
                act.wait_ge(qt_done, t + 1)
                if t >= 2:
                    act.wait_ge(s_done, 4 * (t - 1))
                act.copy(qT[:, t % 2, :, 0:r], banks[7][:].rearrange("p (b q) -> p b q", q=P)[:, :, 0:r]).then_inc(qt_read, 1)

            def softmax(t):
                r, nk = rows(t), nkeys(t)
                for h in range(B_HEADS):
                    act.wait_ge(s_read, B_HEADS * t + h + 1)
                    if t >= 1 and h == 0:
                        act.wait_ge(pt_done, 4 * t)
                    act.activation(E[0:r, h, 0:nk], S[0:r, h, 0:nk], ACT.Exp, bias=nm[0:r, t % 2, h:h + 1], scale=-1.0,
                                   accum_out=rs[0:r, t % 2, h:h + 1]).then_inc(e_done, 1)
                act.wait_ge(es_done, t + 1)
                act.activation(ee[0:r, t % 2], es[0:r, t % 2], ACT.Exp).then_inc(ee_done, 1)

            def p_copy(t):
                r = rows(t)
                for n in range(4):
                    act.wait_ge(pt_done, 4 * t + n + 1)
                    if t >= 1 and n == 0:
                        act.wait_ge(o_done, t)
                    bank = banks[4 + n % 2][:].rearrange("p (h b q) -> p h b q", h=2, b=2)
                    if t == SAMPLE:
                        act.copy(pT[:, 2 * n:2 * n + 2, 0, 0:r], bank[:, :, 0, 0:r])
                        act.copy(pT[0:DEC, 2 * n:2 * n + 2, 1, 0:r], bank[0:DEC, :, 1, 0:r]).then_inc(pt_read, 1)
                    else:
                        nb = nblocks(t)
                        act.copy(pT[:, 2 * n:2 * n + 2, 0:nb, 0:r], bank[:, :, 0:nb, 0:r]).then_inc(pt_read, 1)

            q_copy(0)
            q_copy(1)
            softmax(0)
            for t in range(NT):
                p_copy(t)
                if t + 2 < NT:
                    q_copy(t + 2)
                if t + 1 < NT:
                    softmax(t + 1)

        @block.vector
        def _(dve):
            dve.memset(mask[:], 0.0).then_inc(masks, 1)
            dve.wait_ge(masks, 1)
            dve.memset(mask[0:CHUNK, 0, CHUNK:P], MASKED)
            dve.memset(mask[0:CHUNK, 1, 3 * CHUNK:], MASKED)
            dve.memset(mask[CHUNK:P, 1, 0:CHUNK], MASKED).then_inc(masks, 1)
            dve.wait_ge(loaded, 64)
            dve.tensor_scalar(nsinks[:], sinks[:], -1.0, None, ALU.mult).then_inc(ns_made, 1)
            dve.wait_ge(masks, 2)
            dve.wait_ge(ns_made, 1)

            def gate(n):
                dve.wait_ge(gate_done, n + 1)
                if n < A_GROUPS:
                    u = A[:, 0:NP_TILES, n * A_GD:(n + 1) * A_GD]
                    dve.scalar_tensor_tensor(out=u, in0=banks[n % 2 + 2][:].rearrange("p (t c) -> p t c", c=A_GD),
                                             scalar=bs[:, n:n + 1], in1=u, op0=ALU.add, op1=ALU.mult).then_inc(gate_read, 1)
                else:
                    for g in range(A_GROUPS):
                        u = A[0:DEC, SAMPLE, g * A_GD:(g + 1) * A_GD]
                        ins = dve.scalar_tensor_tensor(out=u, in0=banks[n % 2 + 2][0:DEC, g * A_GD:(g + 1) * A_GD],
                                                       scalar=bs[0:DEC, g:g + 1], in1=u, op0=ALU.add, op1=ALU.mult)
                    ins.then_inc(gate_read, 1)

            def scores(t):
                r, nk = rows(t), nkeys(t)
                m = mask[0:r, min(t, 1) if t < SAMPLE else 2, 0:nk]
                if t >= 1:
                    dve.wait_ge(e_done, B_HEADS * t)
                for h in range(B_HEADS):
                    kv, g = divmod(h, 4)
                    if h % 2 == 0:
                        dve.wait_ge(s_done, 4 * t + h // 2 + 1)
                    src = banks[2 * kv + g // 2][0:r, (g % 2) * 2 * P:(g % 2) * 2 * P + nk]
                    dve.tensor_tensor_reduce(S[0:r, h, 0:nk], src, m, -HD ** -0.5, nsinks[0:r, h:h + 1],
                                             ALU.add, ALU.min, nm[0:r, t % 2, h:h + 1]).then_inc(s_read, 1)
                dve.wait_ge(s_read, B_HEADS * t + B_HEADS)
                dve.tensor_tensor(es[0:r, t % 2], sinks[0:r], nm[0:r, t % 2], ALU.add).then_inc(es_done, 1)

            def outputs(t):
                r = rows(t)
                dve.wait_ge(ee_done, t + 1)
                dve.wait_ge(e_done, B_HEADS * (t + 1))
                dve.tensor_tensor(den[0:r, t % 2], rs[0:r, t % 2], ee[0:r, t % 2], ALU.add).then_inc(den_made, 1)
                dve.wait_ge(den_made, t + 1)
                if t >= 2:
                    dve.wait_ge(o_read, t - 1)
                dve.reciprocal(rden[0:r, t % 2], den[0:r, t % 2]).then_inc(rden_made, 1)
                dve.wait_ge(rden_made, t + 1)
                dve.wait_ge(o_done, t + 1)
                dve.tensor_tensor(A[0:r, t, A_WIDTH:D].rearrange("p (h d) -> p h d", d=HD),
                                  banks[6][0:r].rearrange("p (h d) -> p h d", d=HD),
                                  rden[0:r, t % 2].unsqueeze(2).to_broadcast([r, B_HEADS, HD]), ALU.mult).then_inc(o_read, 1)

            for n in range(A_GROUPS + 1):
                gate(n)
            scores(0)
            for t in range(NT):
                if t + 1 < NT:
                    scores(t + 1)
                outputs(t)

        @block.tensor
        def _(pe):
            for n, slot in enumerate(KEY_ORDER):
                r = DEC if slot == OWN else P
                if n >= 2:
                    pe.wait_ge(kt_read, n - 1)
                if slot == CACHE:
                    pe.wait_ge(cache_arrived, 16)
                pe.transpose(banks[4 + n % 2][:, 0:r], kb[0:r, slot], ident[0:r, 0:r]).then_inc(kt_done, 1)
            pe.wait_ge(loaded, 64)
            pe.wait_ge(wmask, 1)
            for n in range(A_GROUPS + 1):
                if n >= 2:
                    pe.wait_ge(gate_read, n - 1)
                out = banks[n % 2 + 2]
                if n < A_GROUPS:
                    mm = pe.matmul(out[:], wsT[:, n], va[:, 0:NP_TILES, n * A_GD:(n + 1) * A_GD], start=True, stop=True)
                else:
                    for g in range(A_GROUPS):
                        mm = pe.matmul(out[0:DEC, g * A_GD:(g + 1) * A_GD], wsT[0:DEC, g, 0:DEC],
                                       va[0:DEC, SAMPLE, g * A_GD:(g + 1) * A_GD], start=True, stop=True)
                mm.then_inc(gate_done, 1)

            def q_transpose(t):
                r = rows(t)
                if t >= 1:
                    pe.wait_ge(qt_read, t)
                for b in range(4):
                    mm = pe.transpose(banks[7][:, b * P:b * P + r], A[0:r, t, A_WIDTH + b * P:A_WIDTH + (b + 1) * P],
                                      ident[0:r, 0:r])
                mm.then_inc(qt_done, 1)

            def scores(t):
                r, nk = rows(t), nkeys(t)
                pe.wait_ge(qt_read, t + 1)
                pe.wait_ge(kt_read, NT + 1)
                if t == 0:
                    pe.wait_ge(gate_read, A_GROUPS + 1)
                for half in range(2):
                    for b in range(4):
                        if t >= 1 and b % 2 == 0:
                            pe.wait_ge(s_read, B_HEADS * (t - 1) + 4 * half + b + 2)
                        mm = pe.matmul(banks[2 * half + b // 2][0:r, (b % 2) * 2 * P:(b % 2) * 2 * P + nk],
                                       qT[half * HD:half * HD + HD, t % 2, b, 0:r], kT_keys(t, half), start=True, stop=True)
                        if b % 2:
                            mm.then_inc(s_done, 1)

            def p_transpose(t):
                r = rows(t)
                for n in range(4):
                    pe.wait_ge(e_done, B_HEADS * t + 2 * n + 2)
                    if 4 * t + n >= 2:
                        pe.wait_ge(pt_read, 4 * t + n - 1)
                    for hh in range(2):
                        for b in range(nblocks(t)):
                            w = kwidth(t, b)
                            at = (2 * hh + b) * P
                            mm = pe.transpose(banks[4 + n % 2][0:w, at:at + r], E[0:r, 2 * n + hh, b * P:b * P + w],
                                              ident[0:r, 0:r])
                    mm.then_inc(pt_done, 1)

            def values(t):
                r, nb = rows(t), nblocks(t)
                if t >= 1:
                    pe.wait_ge(o_read, t)
                for h in range(B_HEADS):
                    if h % 2 == 0:
                        pe.wait_ge(pt_read, 4 * t + h // 2 + 1)
                    kv = h // 4
                    for b in range(nb):
                        w = kwidth(t, b)
                        mm = pe.matmul(banks[6][0:r, h * HD:(h + 1) * HD], pT[0:w, h, b, 0:r],
                                       vb[0:w, first_slot(t) + b, kv * HD:(kv + 1) * HD], start=(b == 0), stop=(b == nb - 1))
                mm.then_inc(o_done, 1)

            q_transpose(0)
            q_transpose(1)
            scores(0)
            for t in range(NT):
                if t + 1 < NT:
                    scores(t + 1)
                p_transpose(t)
                if t + 2 < NT:
                    q_transpose(t + 2)
                values(t)


class Turn:

    def __init__(self, nc, c, tag, name, A, xt_hi, xt_lo, ident, bank_of):
        self.A, self.hi, self.lo, self.ident, self.bank_of = A, xt_hi, xt_lo, ident, bank_of
        self.turned = c(nc.semaphore(tag + f"{name}_turned"))
        self.hi_made = c(nc.semaphore(tag + f"{name}_hi_made"))

    def transpose(self, pe, n):
        t, h = divmod(n, 2)
        r = rows(t)
        for b in range(4):
            c0 = (4 * h + b) * P
            mm = pe.transpose(self.bank_of(n)[:, b * P:b * P + r], self.A[0:r, t, c0:c0 + P], self.ident[0:r, 0:r])
        mm.then_inc(self.turned, 1)

    def view(self, x, n):
        t, h = divmod(n, 2)
        a, b = tok(t)
        return x[:, 4 * h:4 * h + 4, a:b]

    def bank(self, n):
        return self.bank_of(n)[:].rearrange("p (b q) -> p b q", q=P)[:, :, 0:rows(n // 2)]

    def high(self, act, n):
        act.wait_ge(self.turned, n + 1)
        act.copy(self.view(self.hi, n), self.bank(n)).then_inc(self.hi_made, 1)

    def low(self, dve, n, freed):
        dve.wait_ge(self.hi_made, n + 1)
        dve.tensor_tensor(self.view(self.lo, n), self.bank(n), self.view(self.hi, n), ALU.subtract).then_inc(freed, 1)


def block_layer(nc, aps, room, w_room, layer, resid, w_out, A, xt_hi, xt_lo, ident, mhalf, stored, early, ps, next_early=None):
    w1 = aps["ff_w1"][layer].rearrange("(k p) (n f) -> p k n f", p=P, f=FC)
    w2 = aps["ff_w2"][layer].rearrange("(n f p) d -> p n f d", p=P, f=FT)
    NR = len(RANGES)
    G1 = FT * NR
    G2 = 2 * NT
    PAIRS = (N_FC - 4) // 2
    LAST = N_FC - 1
    LAG = 2
    RESID = 4
    tag = f"layer{layer}_"
    banks = [ps[:, i] for i in range(8)]

    both = lambda kind, t: [(kind, 2 * t), (kind, 2 * t + 1)]
    EARLY_PIECES = [range(0, 2), range(2, W_SLOTS)]
    GROUPS = both("mix", 0) + both("mix", 1)
    for t in range(NT):
        GROUPS += [("out", 0, t)] + (both("mix", t + 2) if t + 2 < NT else [])
    for t in range(NT):
        GROUPS += [("out", 1, t)] + (both("x1", t - LAG) if t >= LAG else [])
    TAIL = [both("x1", t) for t in range(NT - LAG, NT)]
    for pair in TAIL:
        GROUPS += pair
    number = {group: k for k, group in enumerate(GROUPS)}
    SHIFT = (4 - number[TAIL[0][0]]) % 8
    bank_number = lambda group: (number[group] + SHIFT) % 8
    emptied = lambda bank: max(k for k, group in enumerate(GROUPS) if bank_number(group) == bank) + 1

    with ExitStack() as s:
        c = s.enter_context
        sb = lambda name, shape, dt=F32: room.take(name, shape, dt)
        sem = lambda name: c(nc.semaphore(tag + name))
        chunks = [(0, COLS), (COLS, COLS)]
        done = sem("products_done")
        h_room = w_room.from_here(tag)
        st = Stream(nc, c, tag, w_room, w_out, chunks, done, early.pieces, early.arrived)
        w1_at = (w_room.end - 2 * 4 * KT * FC) // 32 * 32
        top = Room(nc, tag, w1_at)
        assert w_room.at <= top.at
        w1_hi, w1_lo = [top.take(n, [P, KT, FC], F32R) for n in ("w1_hi", "w1_lo")]
        w2_hi, w2_lo = [h_room.take(n, [P, FT, D], F32R) for n in ("w2_hi", "w2_lo")]
        h = h_room.take("h_split", [P, 2, FT, 2 * TOK], F32R)
        h_hi = lambda buf, f, a, b: h[:, buf, f, a:b]
        h_lo = lambda buf, f, a, b: h[:, buf, f, TOK + DEC + a:TOK + DEC + b] if a < SEQ else h[:, buf, f, TOK:TOK + DEC]
        assert h_room.at <= w1_at
        ln1 = Norm(nc, c, tag, room, "ln1", D, aps["ln1_g"][layer:layer + 1], aps["ln1_b"][layer:layer + 1])
        w1_raw, w2_raw = sb("w1_raw", [P, KT, FC]), sb("w2_raw", [P, FT, D])
        h_raw = sb("h_raw", [P, 2, 384])
        xr = room.from_here(tag).take("resid", [P, RESID, COLS], F32)
        ln2 = Norm(nc, c, tag, room, "ln2", D, aps["ln2_g"][layer:layer + 1], aps["ln2_b"][layer:layer + 1], tail=2)
        r_arrived = [sem(f"resid_arrived{i}") for i in range(RESID)]
        freed, scaled = sem("banks_freed"), sem("alpha_scaled")
        turns = {"mix": Turn(nc, c, tag, "mix", A, xt_hi, xt_lo, ident, lambda n: banks[bank_number(("mix", n))]),
                 "x1": Turn(nc, c, tag, "x1", A, xt_hi, xt_lo, ident, lambda n: banks[bank_number(("x1", n))])}
        w1_in, w2_in = sem("w1_arrived"), sem("w2_arrived")
        w1_hi_made, w1_lo_made = sem("w1_hi_made"), sem("w1_lo_made")
        w2_hi_made, w2_lo_made = sem("w2_hi_made"), sem("w2_lo_made")
        h_done, relu_done, square_done = sem("h_product_done"), sem("relu_done"), sem("square_done")
        h_hi_made, h_lo_made = sem("h_hi_made"), sem("h_lo_made")
        y_done, y_read, y_low_read = sem("y_product_done"), sem("y_banks_read"), sem("y_low_rows_read")
        x2_freed = sem("x2_banks_freed")
        turn2 = Turn(nc, c, tag, "x2", A, xt_hi, xt_lo, ident, lambda n: banks[n % 4])
        reads_before = lambda g: g - 3 if g >= 4 else max(x for x in range(G2) if x % 4 == g % 4) + 1 - G2
        block = c(nc.Block())

        def load_w1(sp, i, wait):
            if wait:
                sp.wait_ge(w1_lo_made, FT * i)
            sp.dma_start(w1_raw[:], w1[:, :, bass.ds(i, 1)].rearrange("p k n f -> p k (n f)")).then_inc(w1_in, 16)

        def load_w2(sp, i, wait):
            if wait:
                sp.wait_ge(w2_lo_made, i)
            sp.dma_start(w2_raw[:], w2[:, bass.ds(i, 1)].rearrange("p n f d -> p (n f) d")).then_inc(w2_in, 16)

        @block.sync
        def _(sp):
            def load_resid(g):
                j, t = divmod(g, NT)
                a, b = tok(t)
                if g >= RESID:
                    before = divmod(g - RESID, NT)
                    sp.wait_ge(freed, number[("out",) + before] + 1)
                sp.dma_start(xr[0:b - a, g % RESID], resid[a:b, j * COLS:(j + 1) * COLS]).then_inc(r_arrived[g % RESID], 16)

            for n in range(W_SLOTS + 2):
                st.load(sp, n)
                if n == 1:
                    ln1.load(sp)
                    load_resid(0)
                    load_resid(1)
            load_w1(sp, 0, False)
            load_w2(sp, 0, False)
            for g in range(2, NT + RESID - 1):
                load_resid(g)
            for n in range(W_SLOTS + 2, st.n):
                st.load(sp, n)
            for g in range(NT + RESID - 1, G2):
                load_resid(g)
            sp.wait_ge(freed, number[("out", 1, NT - 1)] + 1)
            ln2.load(sp)
            with sp.Fori(1, N_FC) as i:
                load_w1(sp, i, True)
                load_w2(sp, i, True)
            if next_early is not None:
                for n in range(len(next_early.pieces)):
                    next_early.load(sp, n)
            for t in range(NT):
                a, b = tok(t)
                ln2.wait_done(sp, t)
                if layer == 0:
                    dst = aps["x2"][a:b]
                else:
                    dst = aps["y_prompt"][a:b] if t < SAMPLE else aps["y_sample"]
                sp.dma_start(dst, A[0:b - a, t]).then_inc(stored, 16)
            if layer == 1:
                sp.wait_ge(stored, 16 * NT)

        @block.gpsimd
        def _(pool):
            for ln in (ln1, ln2):
                for t in range(NT + 1):
                    if 1 <= t <= ln.pool_tiles:
                        ln.offset(pool, A[:, t - 1], t - 1)
                    if t < NT:
                        ln.rsqrt(pool, mhalf, t)

        def w1_high(act, i, f, wait):
            if f == 0:
                act.wait_ge(w1_in, 16 * i + 16)
            if wait:
                act.wait_ge(h_done, G1 * i - G1 + NR * (f + 1))
            part = slice(f * P, (f + 1) * P)
            act.copy(w1_hi[:, :, part], w1_raw[:, :, part]).then_inc(w1_hi_made, 1)

        def w2_high(act, i, wait):
            act.wait_ge(w2_in, 16 * i + 16)
            if wait:
                act.wait_ge(y_done, G2 * i)
            act.copy(w2_hi[:], w2_raw[:]).then_inc(w2_hi_made, 1)

        w2_place = lambda x, f: x[:, :, f * P:(f + 1) * P]
        w2_part = lambda f: w2_raw[:, f].rearrange("p (k q) -> p k q", q=P)

        def w2_high_last(act, f):
            if f == 0:
                act.wait_ge(w2_in, 16 * N_FC)
            act.wait_ge(h_done, G1 * LAST + NR * (f + 1))
            act.copy(w2_place(w1_hi, f), w2_part(f)).then_inc(w2_hi_made, 1)

        def h_high(act, i, buf, f, settled=True):
            for n in range(NR):
                g = NR * f + n
                a, b = RANGES[n]
                raw = h_raw[:, g % 2, 0:b - a]
                act.wait_ge(h_done, G1 * i + g + 1)
                if settled or g >= 2:
                    act.wait_ge(h_lo_made, G1 * i + g - 1)
                act.activation(raw, banks[g % 3][:, 0:b - a], ACT.Relu).then_inc(relu_done, 1)
                act.wait_ge(relu_done, G1 * i + g + 1)
                act.activation(raw, raw, ACT.Square).then_inc(square_done, 1)
                act.wait_ge(square_done, G1 * i + g + 1)
                act.copy(h_hi(buf, f, a, b), raw).then_inc(h_hi_made, 1)

        def normalised_x1(act, t):
            for n in (2 * t, 2 * t + 1):
                turns["x1"].high(act, n)
            r = rows(t)
            act.mul(A[0:r, t], A[0:r, t], ALPHA).then_inc(scaled, 1)

        @block.scalar
        def _(act):
            for t in range(2):
                for n in (2 * t, 2 * t + 1):
                    turns["mix"].high(act, n)
                for n in EARLY_PIECES[t]:
                    st.split_hi(act, n)
            for t in range(2, NT):
                for n in (2 * t, 2 * t + 1):
                    turns["mix"].high(act, n)
            for n in st.next_pieces(0):
                st.split_hi(act, n)
            w1_high(act, 0, 0, False)
            w1_high(act, 0, 1, False)
            for t in range(NT):
                if t >= LAG:
                    normalised_x1(act, t - LAG)
                ln1.normalise(act, A[:, t], t)
            normalised_x1(act, NT - 2)
            act.wait_ge(done, G2)
            w2_high(act, 0, False)
            normalised_x1(act, NT - 1)
            for i in range(2):
                if i == 1:
                    act.wait_ge(h_lo_made, G1)
                h_high(act, i, i, 0, settled=i > 0)
                w1_high(act, i + 1, 0, True)
                h_high(act, i, i, 1)
                w1_high(act, i + 1, 1, True)
            w2_high(act, 1, True)
            with act.Fori(0, PAIRS) as m:
                for u in range(2):
                    i = 2 * m + (u + 2)
                    act.wait_ge(y_done, G2 * (i - 1))
                    h_high(act, i, u, 0)
                    w1_high(act, i + 1, 0, True)
                    h_high(act, i, u, 1)
                    w1_high(act, i + 1, 1, True)
                    w2_high(act, i, True)
            act.wait_ge(y_done, G2 * (N_FC - 3))
            h_high(act, N_FC - 2, 0, 0)
            w1_high(act, LAST, 0, True)
            h_high(act, N_FC - 2, 0, 1)
            w1_high(act, LAST, 1, True)
            w2_high(act, N_FC - 2, True)
            h_high(act, LAST, 1, 0)
            w2_high_last(act, 0)
            h_high(act, LAST, 1, 1)
            w2_high_last(act, 1)
            for t in range(NT + LAG):
                if layer == 0 and t >= LAG:
                    for n in (2 * (t - LAG), 2 * (t - LAG) + 1):
                        turn2.high(act, n)
                if t < NT:
                    ln2.normalise(act, A[:, t], t)

        def w1_low(dve, i, f):
            part = slice(f * P, (f + 1) * P)
            dve.wait_ge(w1_hi_made, FT * i + f + 1)
            dve.tensor_tensor(w1_lo[:, :, part], w1_raw[:, :, part], w1_hi[:, :, part], ALU.subtract).then_inc(w1_lo_made, 1)

        def w2_low(dve, i):
            dve.wait_ge(w2_hi_made, i + 1)
            dve.tensor_tensor(w2_lo[:], w2_raw[:], w2_hi[:], ALU.subtract).then_inc(w2_lo_made, 1)

        def w2_low_last(dve, f):
            dve.wait_ge(w2_hi_made, LAST + f + 1)
            dve.tensor_tensor(w2_place(w1_lo, f), w2_part(f), w2_place(w1_hi, f), ALU.subtract).then_inc(w2_lo_made, 1)

        def h_low(dve, i, buf, f):
            for n in range(NR):
                g = NR * f + n
                a, b = RANGES[n]
                dve.wait_ge(h_hi_made, G1 * i + g + 1)
                raw = h_raw[:, g % 2]
                if b == TOK:
                    dve.tensor_tensor(h_lo(buf, f, SEQ, TOK), raw[:, SEQ - a:TOK - a], h_hi(buf, f, SEQ, TOK), ALU.subtract)
                    b = SEQ
                dve.tensor_tensor(h_lo(buf, f, a, b), raw[:, 0:b - a], h_hi(buf, f, a, b), ALU.subtract).then_inc(h_lo_made, 1)

        def add_y(dve, i, g):
            t, j = divmod(g, 2)
            r = rows(t)
            if g % 2 == 0 and isinstance(i, int) and i == 0:
                dve.wait_ge(scaled, t + 1)
            dve.wait_ge(y_done, G2 * i + g + 1)
            acc = A[0:r, t, j * COLS:(j + 1) * COLS]
            if t == SAMPLE:
                dve.tensor_tensor(acc, banks[4 + g % 4][DEC:2 * DEC], acc, ALU.add).then_inc(y_low_read, 1)
                dve.wait_ge(y_low_read, 2 * i + j + 1)
            dve.tensor_tensor(acc, banks[4 + g % 4][0:r], acc, ALU.add).then_inc(y_read, 1)

        @block.vector
        def _(dve):
            def empty(kind, n):
                turns[kind].low(dve, n, freed)

            def add_resid(j, t):
                g, r = j * NT + t, rows(t)
                if t == NT - 1:
                    for n in st.next_pieces(j):
                        st.split_lo(dve, n)
                dve.wait_ge(r_arrived[g % RESID], 16 * (g // RESID + 1))
                dve.wait_ge(done, g + 1)
                dve.scalar_tensor_tensor(out=A[0:r, t, j * COLS:(j + 1) * COLS], in0=xr[0:r, g % RESID], scalar=ALPHA,
                                         in1=banks[bank_number(("out", j, t))][0:r], op0=ALU.mult, op1=ALU.add).then_inc(freed, 1)

            for k, group in enumerate(GROUPS):
                if group[0] != "out":
                    empty(*group)
                    if group in (("mix", 1), ("mix", 3)):
                        for n in EARLY_PIECES[group[1] // 2]:
                            st.split_lo(dve, n)
                    if group == ("x1", 2 * (NT - 1 - LAG) + 1):
                        ln1.scale(dve, A[:, NT - 1], NT - 1)
                    if group == ("x1", 2 * (NT - 2) + 1):
                        w2_low(dve, 0)
                else:
                    _, j, t = group
                    if j == 1 and t >= 1:
                        ln1.scale(dve, A[:, t - 1], t - 1)
                    add_resid(j, t)
                    if j == 1:
                        dve.wait_ge(freed, k + 1)
                        ln1.statistics(dve, A[:, t], t)
                        if t < FT:
                            w1_low(dve, 0, t)
            for i in range(2):
                for f in range(FT):
                    h_low(dve, i, i, f)
                    w1_low(dve, i + 1, f)
            for g in range(G2):
                add_y(dve, 0, g)
            w2_low(dve, 1)
            with dve.Fori(0, PAIRS) as m:
                for u in range(2):
                    i = 2 * m + (u + 2)
                    for f in range(FT):
                        h_low(dve, i, u, f)
                        w1_low(dve, i + 1, f)
                    for g in range(G2):
                        add_y(dve, i - 1, g)
                    w2_low(dve, i)
            for f in range(FT):
                h_low(dve, N_FC - 2, 0, f)
                w1_low(dve, LAST, f)
            for g in range(G2):
                add_y(dve, N_FC - 3, g)
            w2_low(dve, N_FC - 2)
            for f in range(FT):
                h_low(dve, LAST, 1, f)
                w2_low_last(dve, f)
            for t in range(NT + LAG):
                if 1 <= t <= NT:
                    ln2.scale(dve, A[:, t - 1], t - 1)
                    if t > ln2.pool_tiles:
                        ln2.offset(dve, A[:, t - 1], t - 1)
                if t < NT:
                    add_y(dve, N_FC - 2, 2 * t)
                    add_y(dve, N_FC - 2, 2 * t + 1)
                    dve.wait_ge(y_read, G2 * (N_FC - 2) + 2 * t + 2)
                    ln2.statistics(dve, A[:, t], t)
                if layer == 0 and t >= LAG:
                    for n in (2 * (t - LAG), 2 * (t - LAG) + 1):
                        turn2.low(dve, n, x2_freed)

        def first_group(pe, i, g):
            f, n = divmod(g, NR)
            a, b = RANGES[n]
            if n == 0:
                pe.wait_ge(w1_lo_made, FT * i + f + 1)
            out = banks[g % 3][:, 0:b - a]
            for k in range(KT):
                w = slice(f * P, (f + 1) * P)
                pe.matmul(out, w1_hi[:, k, w], xt_hi[:, k, a:b], start=(k == 0), stop=False)
                pe.matmul(out, w1_hi[:, k, w], xt_lo[:, k, a:b], start=False, stop=False)
                mm = pe.matmul(out, w1_lo[:, k, w], xt_hi[:, k, a:b], start=False, stop=(k == KT - 1))
            mm.then_inc(h_done, 1)

        def first_product(pe, i):
            for g in range(G1):
                pe.wait_ge(relu_done, G1 * i + g - 2)
                first_group(pe, i, g)

        def second_product(pe, i, buf, prior, last=False):
            pe.wait_ge(w2_lo_made, i + 1)
            pe.wait_ge(h_lo_made, G1 * i + G1)
            for g in range(G2):
                t, j = divmod(g, 2)
                a, b = tok(t)
                if prior or g >= 4:
                    pe.wait_ge(y_read, G2 * i + reads_before(g))
                else:
                    pe.wait_ge(freed, emptied(4 + g % 4))
                bank = banks[4 + g % 4]
                out = bank[0:b - a]
                d = slice(j * COLS, (j + 1) * COLS)
                parts = [(buf, f, w2_hi[:, f, d], w2_lo[:, f, d]) for f in range(FT)]
                if last:
                    k = slice(j * COLS // P, (j + 1) * COLS // P)
                    parts += [(1 - buf, f, w2_place(w1_hi, f)[:, k], w2_place(w1_lo, f)[:, k]) for f in range(FT)]
                for n, (hb, f, high, low) in enumerate(parts):
                    if g == 0 and n >= FT:
                        pe.wait_ge(w2_lo_made, i + 1 + n - FT + 1)
                        pe.wait_ge(h_lo_made, G1 * N_FC)
                    end = n == len(parts) - 1
                    if t < SAMPLE:
                        pe.matmul(out, h_hi(hb, f, a, b), high, start=(n == 0), stop=False)
                        pe.matmul(out, h_hi(hb, f, a, b), low, start=False, stop=False)
                        mm = pe.matmul(out, h_lo(hb, f, a, b), high, start=False, stop=end)
                    else:
                        both_parts = lambda: pe.matmul(bank, h[:, hb, f, SEQ:TOK + DEC], high, start=(n == 0), stop=end)
                        if not end:
                            both_parts()
                        pe.matmul(out, h_hi(hb, f, a, b), low, start=False, stop=False)
                        if end:
                            mm = both_parts()
                mm.then_inc(y_done, 1)
                if last and layer == 0 and j == 1 and t >= LAG:
                    turn_x2(pe, t - LAG)

        def turn_x2(pe, t):
            ln2.wait_done(pe, t)
            for n in (2 * t, 2 * t + 1):
                if n >= 4:
                    pe.wait_ge(x2_freed, n - 3)
                else:
                    pe.wait_ge(relu_done, G1 * N_FC)
                turn2.transpose(pe, n)

        @block.tensor
        def _(pe):
            def turn_group(kind, n):
                k = number[(kind, n)]
                if k >= 8:
                    pe.wait_ge(freed, k - 7)
                if kind == "x1":
                    ln1.wait_done(pe, n // 2)
                turns[kind].transpose(pe, n)

            for k, group in enumerate(GROUPS[:number[TAIL[0][0]]]):
                if group[0] == "out":
                    _, j, t = group
                    pe.wait_ge(freed, max(k - 7, number[("mix", 2 * t + 1)] + 1 if j == 0 else 0))
                    st.product(pe, banks[bank_number(group)], t, j, xt_hi, xt_lo)
                else:
                    turn_group(*group)
            for n in range(NR):
                pe.wait_ge(freed, max(emptied(n), number[("x1", 2 * (-(-RANGES[n][1] // P) - 1) + 1)] + 1))
                first_group(pe, 0, n)
                if n < len(TAIL):
                    for group in TAIL[n]:
                        turn_group(*group)
            for g in range(NR, G1):
                pe.wait_ge(relu_done, g - 2)
                first_group(pe, 0, g)
            first_product(pe, 1)
            second_product(pe, 0, 0, False)
            with pe.Fori(0, PAIRS) as m:
                for u in range(2):
                    i = 2 * m + (u + 2)
                    first_product(pe, i)
                    second_product(pe, i - 1, (u + 1) % 2, True)
            first_product(pe, N_FC - 2)
            second_product(pe, N_FC - 3, 1, True)
            first_product(pe, LAST)
            second_product(pe, N_FC - 2, 0, True, last=True)
            if layer == 0:
                for t in range(NT - LAG, NT):
                    turn_x2(pe, t)


def ranges_of(numbers):
    found = []
    for n in sorted(numbers):
        if found and found[-1].stop == n:
            found[-1] = range(found[-1].start, n + 1)
        else:
            found.append(range(n, n + 1))
    return found


class Ranking:

    def __init__(self, nc, c, tag, first, idx, top8, wi, rel, where):
        self.first, self.idx, self.top8, self.wi, self.rel, self.where = first, idx, top8, wi, rel, where
        s = lambda what: c(nc.semaphore(tag + what))
        self.i_done, self.relu_done, self.mixed = s("idx_product_done"), s("relu_done"), s("idx_head_added")
        self.chain = s("ranking_steps")
        self.steps = 0
        self.last = {}

    def count(self, m, i):
        return IDX_HEADS * (m - self.first) + i

    def scored(self, m):
        w, nk = IDX_WIDTH[m % RING], nkeys(C_RANKED[m])
        return self.idx[m % RING][0:rows(C_RANKED[m]), w - nk:w]

    def relu(self, act, m, i):
        t, y = C_RANKED[m], self.count(m, i)
        r, nk = rows(t), nkeys(t)
        act.wait_ge(self.i_done, y + 1)
        if y >= 2:
            act.wait_ge(self.mixed, y - 1)
        act.activation(self.rel[0:r, i % 2, 0:nk], self.where(m, i), ACT.Relu,
                       scale=(HD * IDX_HEADS) ** -0.5).then_inc(self.relu_done, 1)

    def step(self, m, ins):
        self.steps += 1
        self.last[m] = self.steps
        ins.then_inc(self.chain, 1)

    def mix(self, dve, m, i):
        t, y, out = C_RANKED[m], self.count(m, i), self.scored(m)
        r, nk = rows(t), nkeys(t)
        dve.wait_ge(self.relu_done, y + 1)
        src, w = self.rel[0:r, i % 2, 0:nk], self.wi[0:r, t, i:i + 1]
        if i == 0:
            dve.tensor_scalar(out, src, w, None, ALU.mult).then_inc(self.mixed, 1)
        else:
            dve.wait_ge(self.mixed, y)
            dve.scalar_tensor_tensor(out=out, in0=src, scalar=w, in1=out, op0=ALU.mult, op1=ALU.add).then_inc(self.mixed, 1)
        if i == IDX_HEADS - 1:
            dve.wait_ge(self.mixed, y + 1)
            if t < SAMPLE:
                self.step(m, dve.memset(out[0:CHUNK, nk - CHUNK:nk], BARRED))

    def eight(self, m):
        return self.top8[0:rows(C_RANKED[m]), m % RING]

    def find(self, dve, ranks):
        for m in ranks:
            if m in self.last:
                dve.wait_ge(self.chain, self.last[m])
            self.step(m, dve.max(self.eight(m), self.scored(m)))

    def mark(self, dve, ranks):
        for m in ranks:
            dve.wait_ge(self.chain, self.last[m])
            self.step(m, dve.match_replace(self.scored(m), self.eight(m), self.scored(m), TAKEN))

    def take(self, dve, ranks):
        self.find(dve, ranks)
        self.mark(dve, ranks)

    def close(self, dve, m):
        dve.wait_ge(self.chain, self.last[m])
        self.step(m, dve.tensor_scalar(self.scored(m), self.scored(m), TAKEN, MASKED, ALU.not_equal, ALU.mult))

    def product(self, pe, out, q, m, ki_hh, ki_ll):
        t = C_RANKED[m]
        k0, nk = key0(t), nkeys(t)
        for c0 in range(0, nk, COLS):
            w = min(COLS, nk - c0)
            at = out[c0 // COLS][0:rows(t), 0:w]
            pe.matmul(at, q, ki_hh[:, k0 + c0:k0 + c0 + w], start=True, stop=False)
            mm = pe.matmul(at, q, ki_ll[:, k0 + c0:k0 + c0 + w], start=False, stop=True)
        mm.then_inc(self.i_done, 1)


def copy_key_quad(copy, out, bank, quad):
    full = [sl for sl in quad if sl != OWN]
    last = copy(out[:, full[0] * P:(full[-1] + 1) * P], bank[:, 0:len(full) * P])
    if OWN in quad:
        last = copy(out[:, OWN * P:OWN * P + DEC], bank[:, len(full) * P:len(full) * P + DEC])
    return last


KEY_PARTS = [(slice(0, OWN), P), (slice(OWN, KEY_SLOTS), DEC)]


def block_c_in(nc, aps, room, scratch, A, xt_hi, xt_lo, kc, vc, ki, qi, wi, idx, top8, ident_r, x2_stored, early, ps):
    tag = "c_in_"
    banks = [ps[:, i] for i in range(8)]
    ITEMS_AT = {4: [(0, i) for i in range(IDX_HEADS)], 5: [(1, 0), (1, 1)], 6: [(1, 2), (1, 3)],
                7: [(2, 0), (2, 1)], 8: [(2, 2), (2, 3)]}
    item_banks = lambda m, i: [4 + i] if m == 0 else [4 + i % 2 * 2, 5 + i % 2 * 2]
    with ExitStack() as s:
        c = s.enter_context
        chunks = [(IDX_COL, IDX_W), (C_Q, 2 * C_KVW), (0, COLS), (COLS, COLS)]
        done = c(nc.semaphore(tag + "products_done"))
        st = Stream(nc, c, tag, room, aps["c_w_in"], chunks, done, early.pieces, early.arrived)
        table = room.take("rope_table", [P, NT, P], F32)
        tmp = room.take("rope_tmp", [P, 2, 8, HD], F32)
        over = scratch.from_here(tag)
        ih, il = [scratch.take(n, [P, KEY_SLOTS, P], F32R) for n in ("k_idx_split_hi", "k_idx_split_lo")]
        rel = over.take("relu", [P, 2, SEQ])
        ki_hh, ki_ll = [scratch.take(n, [P, KEY_SLOTS * P], F32R) for n in ("k_idx_hi_hi", "k_idx_lo_lo")]
        qi_tok = scratch.take("q_idx_split", [P, RING, IDX_HEADS, 2, HD], F32R)
        qiS = scratch.take("q_idx_stacked", [P, RING, IDX_HEADS, P], F32R)
        item_out = lambda m, i: ps[0:rows(C_RANKED[m]), item_banks(m, i)[0]:item_banks(m, i)[-1] + 1].rearrange(
            "p b c -> p (b c)")[:, 0:nkeys(C_RANKED[m])]
        ranking = Ranking(nc, c, tag, 0, idx, top8, wi, rel, item_out)
        ih_made, il_made = [c(nc.semaphore(tag + n)) for n in ("k_idx_hi_made", "k_idx_lo_made")]
        hi_turned, lo_turned = [c(nc.semaphore(tag + n)) for n in ("k_idx_hi_turned", "k_idx_lo_turned")]
        hi_copied, lo_copied = [c(nc.semaphore(tag + n)) for n in ("k_idx_hi_copied", "k_idx_lo_copied")]
        qi_hi_made, qi_lo_made = [c(nc.semaphore(tag + n)) for n in ("q_idx_hi_made", "q_idx_lo_made")]
        q_turned, q_copied = [c(nc.semaphore(tag + n)) for n in ("q_idx_turned", "q_idx_copied")]
        loaded = c(nc.semaphore(tag + "table_and_caches_arrived"))
        read = c(nc.semaphore(tag + "banks_read"))
        chain = c(nc.semaphore(tag + "vector_chain"))
        stored = c(nc.semaphore(tag + "outputs_stored"))
        block = c(nc.Block())
        finished = ranges_of(nc.released_uncleared_semaphores)
        tiles = lambda x: x.rearrange("(t p) c -> p t c", p=P)
        CACHE = slice(NP_TILES, NP_TILES + 2)
        heads_of = lambda x, r: x[0:r].rearrange("p (h d) -> p h d", d=HD)
        HI_BANKS, LO_BANKS, Q_BANKS = [4, 5, 6], [7, 4, 5], [6, 4, 5]

        @block.sync
        def _(sp):
            for n in range(W_SLOTS + 2):
                st.load(sp, n)
                if n == 2:
                    sp.dma_start(table[:, 0:NP_TILES], tiles(aps["rope"][0:SEQ])).then_inc(loaded, 16)
                    sp.dma_start(table[0:DEC, SAMPLE], aps["rope"][SEQ:TOK]).then_inc(loaded, 16)
            sp.dma_start(kc[:, CACHE], tiles(aps["cache_c_k"])).then_inc(loaded, 16)
            sp.dma_start(vc[:, CACHE], tiles(aps["cache_c_v"])).then_inc(loaded, 16)
            for h in range(2):
                sp.dma_start(ki[:, CACHE, h * HD:(h + 1) * HD], tiles(aps["cache_c_idx"])).then_inc(loaded, 16)
            for n in range(W_SLOTS + 2, st.n):
                st.load(sp, n)
            sp.wait_ge(read, 2 * NT)
            sp.dma_start(tiles(aps["p_c_k"]), kc[:, 0:NP_TILES]).then_inc(stored, 16)
            sp.dma_start(tiles(aps["p_c_v"]), vc[:, 0:NP_TILES]).then_inc(stored, 16)
            sp.dma_start(tiles(aps["p_c_idx"]), ki[:, 0:NP_TILES, 0:HD]).then_inc(stored, 16)
            sp.dma_start(aps["s_c_k"], kc[0:DEC, OWN]).then_inc(stored, 16)
            sp.dma_start(aps["s_c_v"], vc[0:DEC, OWN]).then_inc(stored, 16)
            sp.dma_start(aps["s_c_idx"], ki[0:DEC, OWN, 0:HD]).then_inc(stored, 16)
            sp.wait_ge(stored, 96)
            sp.wait_ge(loaded, 96)
            sp.wait_ge(x2_stored, 16 * NT)

        @block.gpsimd
        def _(pool):
            for sem_range in finished:
                pool.sem_clear(sem_range)
            for m in range(RING):
                r = rows(C_RANKED[m])
                pool.wait_ge(qi_hi_made, m + 1)
                pool.tensor_tensor(qi_tok[0:r, m, :, 1], heads_of(qi[:, C_RANKED[m]], r), qi_tok[0:r, m, :, 0],
                                   ALU.subtract).then_inc(qi_lo_made, 1)

        @block.scalar
        def _(act):
            for n in range(W_SLOTS):
                st.split_hi(act, n)
            for n in st.next_pieces(0):
                st.split_hi(act, n)
            act.wait_ge(x2_stored, 16 * NT)
            act.wait_ge(read, NT)
            act.wait_ge(loaded, 96)
            for part, r in KEY_PARTS:
                act.copy(ih[0:r, part], ki[0:r, part]).then_inc(ih_made, 1)
            for m in range(RING):
                r = rows(C_RANKED[m])
                act.copy(qi_tok[0:r, m, :, 0], heads_of(qi[:, C_RANKED[m]], r)).then_inc(qi_hi_made, 1)
            for n, quad in enumerate(KEY_QUADS):
                act.wait_ge(hi_turned, n + 1)
                copy_key_quad(act.copy, ki_hh, banks[HI_BANKS[n]], quad).then_inc(hi_copied, 1)
            for m in range(RING):
                r = rows(C_RANKED[m])
                act.wait_ge(q_turned, m + 1)
                act.copy(qiS[:, m, :, 0:r], banks[Q_BANKS[m]].rearrange("p (b q) -> p b q", q=P)[:, :, 0:r]).then_inc(q_copied, 1)
            for t in range(NT):
                if t == NT - 1:
                    for n in st.next_pieces(1):
                        st.split_hi(act, n)
                for m, i in ITEMS_AT.get(t, []):
                    ranking.relu(act, m, i)
            for j in range(2, len(chunks)):
                for n in st.next_pieces(j):
                    st.split_hi(act, n)

        @block.vector
        def _(dve):
            links = [0]

            def link(ins):
                links[0] += 1
                ins.then_inc(chain, 1)
                dve.wait_ge(chain, links[0])

            for n in range(W_SLOTS):
                st.split_lo(dve, n)
            dve.wait_ge(loaded, 96)
            for j in range(len(chunks)):
                for t in range(NT):
                    g, r = j * NT + t, rows(t)
                    turn = tmp[0:r]
                    slot = t if t < SAMPLE else OWN
                    bank = banks[g % 4][0:r]
                    if t == NT - 1:
                        for n in st.next_pieces(j):
                            st.split_lo(dve, n)
                    dve.wait_ge(done, g + 1)
                    if g >= 1:
                        dve.wait_ge(read, g)
                    if j == 0:
                        n = IDX_HEADS + 1
                        rope(dve, link, bank[:, 0:n * HD].rearrange("p (h d) -> p h d", d=HD), table[0:r, t], turn, n)
                        dve.tensor_tensor(qi[0:r, t].rearrange("p (h d) -> p h d", d=HD), turn[:, 0, 0:IDX_HEADS],
                                          turn[:, 1, 0:IDX_HEADS], ALU.add)
                        twice = lambda i: turn[:, i, IDX_HEADS:IDX_HEADS + 1].to_broadcast([r, 2, HD])
                        dve.tensor_tensor(ki[0:r, slot].rearrange("p (h d) -> p h d", d=HD), twice(0), twice(1), ALU.add)
                        dve.tensor_copy(wi[0:r, t], bank[:, n * HD:IDX_W]).then_inc(read, 1)
                    elif j >= 2:
                        if g == 2 * NT:
                            dve.wait_ge(ranking.mixed, RING * IDX_HEADS)
                        rope(dve, link, bank.rearrange("p (h d) -> p h d", d=HD), table[0:r, t], turn, 8)
                        out = A[0:r, t, (j - 2) * COLS:(j - 1) * COLS].rearrange("p (h d) -> p h d", d=HD)
                        dve.tensor_tensor(out, turn[:, 0], turn[:, 1], ALU.add).then_inc(read, 1)
                    else:
                        rope(dve, link, bank[:, 0:C_KVW].rearrange("p (h d) -> p h d", d=HD), table[0:r, t], turn, C_KV)
                        dve.tensor_tensor(kc[0:r, slot].rearrange("p (h d) -> p h d", d=HD), turn[:, 0, 0:C_KV],
                                          turn[:, 1, 0:C_KV], ALU.add)
                        dve.tensor_copy(vc[0:r, slot], bank[:, C_KVW:2 * C_KVW]).then_inc(read, 1)
                    if j == 1:
                        if t == 0:
                            for n, (part, kr) in enumerate(KEY_PARTS):
                                dve.wait_ge(ih_made, n + 1)
                                dve.tensor_tensor(il[0:kr, part], ki[0:kr, part], ih[0:kr, part], ALU.subtract).then_inc(il_made, 1)
                        if t == 2:
                            for n, quad in enumerate(KEY_QUADS):
                                dve.wait_ge(lo_turned, n + 1)
                                copy_key_quad(dve.tensor_copy, ki_ll, banks[LO_BANKS[n]], quad).then_inc(lo_copied, 1)
                        for m, i in ITEMS_AT.get(t, []):
                            ranking.mix(dve, m, i)
                        if t > min(ITEMS_AT):
                            for _ in range(2):
                                ranking.take(dve, [0])
                    elif j >= 2:
                        x = t + ROUND_TILES * (j - 2)
                        if t < ROUND_TILES:
                            ranking.take(dve, [0, 1] if x < rounds(0) - 8 else [1])
            ranking.close(dve, 0)

        @block.tensor
        def _(pe):
            turn = lambda bank, at, src: pe.transpose(bank[:, at:at + src.shape[0]].bitcast(F32R), src,
                                                      ident_r[0:src.shape[0], 0:src.shape[0]])

            def turn_queries(m):
                r = rows(C_RANKED[m])
                pe.wait_ge(qi_lo_made, m + 1)
                for h in range(IDX_HEADS):
                    mm = turn(banks[Q_BANKS[m]], h * P, qi_tok[0:r, m, h].rearrange("p two d -> p (two d)"))
                mm.then_inc(q_turned, 1)

            def beside(t):
                if t == 1:
                    pe.wait_ge(ih_made, len(KEY_PARTS))
                    for n, quad in enumerate(KEY_QUADS):
                        for b, sl in enumerate(quad):
                            mm = turn(banks[HI_BANKS[n]], b * P, ih[0:rows_of_slot(sl), sl])
                        mm.then_inc(hi_turned, 1)
                if t == 2:
                    pe.wait_ge(il_made, len(KEY_PARTS))
                    pe.wait_ge(hi_copied, len(KEY_QUADS))
                    for n, quad in enumerate(KEY_QUADS):
                        for b, sl in enumerate(quad):
                            mm = turn(banks[LO_BANKS[n]], b * P, il[0:rows_of_slot(sl), sl])
                        mm.then_inc(lo_turned, 1)
                    turn_queries(0)
                if t == 3:
                    pe.wait_ge(lo_copied, len(KEY_QUADS))
                    turn_queries(1)
                    turn_queries(2)
                if t == 4:
                    pe.wait_ge(q_copied, RING)
                for m, i in ITEMS_AT.get(t, []):
                    y = ranking.count(m, i)
                    if m >= 1:
                        pe.wait_ge(ranking.relu_done, max(y - 1, IDX_HEADS))
                    ranking.product(pe, [banks[b] for b in item_banks(m, i)], qiS[:, m, i, 0:rows(C_RANKED[m])], m,
                                    ki_hh, ki_ll)

            for j in range(len(chunks)):
                for t in range(NT):
                    g = j * NT + t
                    if g >= 4:
                        pe.wait_ge(read, g - 3)
                    st.product(pe, banks[g % 4], t, j, xt_hi, xt_lo)
                    if j == 1:
                        beside(t)


def block_c_mixer(nc, room, A, kc, vc, ki, qi, wi, idx, top8, ident, ident_r, next_early, ps):
    tag = "c_mix_"
    NS, HP = KEY_SLOTS, C_HEADS
    ORDER, RANKED, FIRST = C_ORDER, C_RANKED, UNRANKED
    NR = len(RANKED)

    slot0 = lambda t: 0 if t < SAMPLE else NP_TILES
    blocks = lambda t: -(-nkeys(t) // P)
    width = lambda t, b: min(P, nkeys(t) - b * P)
    groups = lambda t: -(-blocks(t) // 4)

    items_at = [[] for _ in range(HP * NT)]
    mixes_at = [[] for _ in range(HP * NT)]
    rounds_at = [[] for _ in range(HP * NT)]
    for m in range(RING, NR):
        for i, (x_item, x_mix) in enumerate([(-2, 0), (-1, 1), (2, 3), (3, 4)]):
            items_at[HP * m + x_item].append((m, i))
            mixes_at[HP * m + x_mix].append((m, i))

    def spread(m, count, lo, hi):
        for j in range(count):
            rounds_at[lo + j * (hi - lo) // count].append(m)

    early_2 = rounds(2) - 2
    spread(1, rounds(1) - ROUNDS_BEFORE - ROUNDS_AHEAD, 0, RING * HP)
    spread(2, early_2 - ROUNDS_AHEAD, 0, RING * HP)
    spread(2, rounds(2) - early_2, RING * HP, (RING + 1) * HP)
    for m in range(RING, NR):
        spread(m, rounds(m) // 2, HP * m + 5, HP * (m + 1))
        spread(m, rounds(m) // 2, HP * (m + 1), HP * (m + 2))
    tile_of = lambda use: ORDER[use[1] // HP] if use[0] == "head" else RANKED[use[1]]
    uses = []
    for x in range(HP * NT):
        uses += [("head", x)] + [("item",) + item for item in items_at[x]]
    place, before, owner, at = {}, {}, {}, 0
    for use in uses:
        n = -(-nkeys(tile_of(use)) // COLS)
        at += at % n
        place[use] = [(at + b) % 4 for b in range(n)]
        before[use] = sorted({owner[b] for b in place[use] if b in owner})
        owner.update({b: use for b in place[use]})
        at += n

    def deep(x):
        return all(len(place[("head", z)]) == 1 for z in range(max(x, 0), x + 3)) if x + 2 < HP * NT else False

    QUERY_AT = [10, 11, 12, 13]

    with ExitStack() as s:
        c = s.enter_context
        sb = lambda name, shape, dt=F32: room.take(name, shape, dt)
        sem = lambda name: c(nc.semaphore(tag + name))
        k_hh = sb("k_hi_hi", [P, C_KV, NS * P], F32R)
        k_ll = sb("k_lo_lo", [P, C_KV, NS * P], F32R)
        ki_hh = sb("k_idx_hi_hi", [P, NS * P], F32R)
        ki_ll = sb("k_idx_lo_lo", [P, NS * P], F32R)
        q_tok = sb("q_split", [P, HP, 2, HD], F32R)
        qS = sb("q_stacked", [P, 2, HP, P], F32R)
        qi_tok = sb("q_idx_split", [P, 2, IDX_HEADS, 2, HD], F32R)
        qiS = sb("q_idx_stacked", [P, IDX_HEADS, P], F32R)
        early = sb("early_mask", [P, 2 * P])
        nm = sb("minus_max", [P, 2, HP])
        rs = sb("row_sum", [P, 2, HP])
        rden = sb("rden", [P, 2, HP])
        rel = sb("relu", [P, 2, SEQ])
        prep = room.from_here(tag)
        S = sb("scores", [P, 2, SEQ])
        E = sb("probs", [P, 2, SEQ])
        pT = sb("probs_T", [P, 2, 8, P])
        ih = prep.take("k_idx_split_hi", [P, NS, P], F32R)
        il = prep.take("k_idx_split_lo", [P, NS, P], F32R)
        KRING = 3
        kh = prep.take("k_split_hi", [P, KRING, C_KV, 2, HD], F32R)
        kl = prep.take("k_split_lo", [P, KRING, C_KV, 2, HD], F32R)
        ih_made, il_made = sem("k_idx_hi_made"), sem("k_idx_lo_made")
        ihi_turned, ilo_turned = sem("k_idx_hi_turned"), sem("k_idx_lo_turned")
        ihi_copied, ilo_copied = sem("k_idx_hi_copied"), sem("k_idx_lo_copied")
        kh_made, kl_made = sem("k_hi_made"), sem("k_lo_made")
        k_turned, k_copied = sem("keys_turned"), sem("keys_copied")
        q_hi_made, q_lo_made = sem("q_hi_made"), sem("q_lo_made")
        qi_hi_made, qi_lo_made = sem("q_idx_hi_made"), sem("q_idx_lo_made")
        masks = sem("masks_made")
        turned, copied = sem("transposed"), sem("transposes_copied")
        s_done, s_read, e_done = sem("scores_done"), sem("scores_read"), sem("probs_ready")
        o_done, o_read, rden_made = sem("outputs_done"), sem("outputs_read"), sem("rden_made")
        banks = [ps[:, i] for i in range(8)]
        srows = rows_of_slot
        IDX_HI_BANKS, IDX_LO_BANKS = [0, 1, 2], [3, 6, 7]
        wide = lambda use, r, n: ps[0:r, place[use][0]:place[use][-1] + 1].rearrange("p b c -> p (b c)")[:, 0:n]
        ranking = Ranking(nc, c, tag, RING, idx, top8, wi, rel,
                          lambda m, i: wide(("item", m, i), rows(RANKED[m]), nkeys(RANKED[m])))
        heads_of = lambda x, r: x[0:r].rearrange("p (h d) -> p h d", d=HD)
        quads = lambda bank, r: bank.rearrange("p (b q) -> p b q", q=P)[:, :, 0:r]
        block = c(nc.Block())

        @block.sync
        def _(sp):
            next_early.load(sp, 0)
            sp.wait_ge(s_read, HP * (4 + FIRST + 1))
            next_early.load(sp, 1)

        @block.gpsimd
        def _(pool):
            pool.memset(early[:], 0.0).then_inc(masks, 1)
            pool.wait_ge(masks, 1)
            pool.memset(early[0:CHUNK, 3 * CHUNK:], MASKED).then_inc(masks, 1)

            def q_idx_low(m):
                r = rows(RANKED[m])
                pool.wait_ge(qi_hi_made, m - RING + 1)
                pool.tensor_tensor(qi_tok[0:r, m % 2, :, 1], heads_of(qi[:, RANKED[m]], r), qi_tok[0:r, m % 2, :, 0],
                                   ALU.subtract).then_inc(qi_lo_made, 1)

            def q_low(p):
                r = rows(ORDER[p])
                pool.wait_ge(q_hi_made, p + 1)
                pool.tensor_tensor(q_tok[0:r, :, 1], heads_of(A[:, ORDER[p]], r), q_tok[0:r, :, 0],
                                   ALU.subtract).then_inc(q_lo_made, 1)

            for sl in range(NS):
                r = srows(sl)
                pool.wait_ge(kh_made, sl + 1)
                pool.tensor_tensor(kl[0:r, sl % KRING], heads_of(kc[:, sl], r).unsqueeze(2).to_broadcast([r, C_KV, 2, HD]),
                                   kh[0:r, sl % KRING], ALU.subtract).then_inc(kl_made, 1)
                if sl == 0:
                    q_low(0)
            for p in range(NT - 1):
                if RING <= p + 1 < NR:
                    q_idx_low(p + 1)
                q_low(p + 1)

        @block.scalar
        def _(act):
            n = [0]

            def copy(out, bank):
                act.wait_ge(turned, n[0] + 1)
                act.copy(out, bank).then_inc(copied, 1)
                n[0] += 1

            def q_idx_high(m):
                r = rows(RANKED[m])
                if m >= RING + 2:
                    act.wait_ge(ranking.i_done, IDX_HEADS * (m - 1 - RING))
                act.copy(qi_tok[0:r, m % 2, :, 0], heads_of(qi[:, RANKED[m]], r)).then_inc(qi_hi_made, 1)

            def q_high(p):
                r = rows(ORDER[p])
                if p >= 1:
                    act.wait_ge(s_done, HP * (p - 1) + 1)
                act.copy(q_tok[0:r, :, 0], heads_of(A[:, ORDER[p]], r)).then_inc(q_hi_made, 1)

            def idx_queries(m):
                r = rows(RANKED[m])
                if m > RING:
                    act.wait_ge(ranking.i_done, IDX_HEADS * (m - RING))
                copy(qiS[:, :, 0:r], quads(banks[4 + n[0] % 2], r))

            def k_high(sl):
                r = srows(sl)
                if sl >= KRING:
                    act.wait_ge(k_turned, 2 * (sl - KRING) + 2)
                act.copy(kh[0:r, sl % KRING], heads_of(kc[:, sl], r).unsqueeze(2).to_broadcast([r, C_KV, 2, HD])).then_inc(kh_made, 1)

            def queries(p, g):
                r = rows(ORDER[p])
                if p >= 2 and g == 0:
                    act.wait_ge(s_done, HP * (p - 1))
                copy(qS[:, p % 2, 4 * g:4 * g + 4, 0:r], quads(banks[4 + n[0] % 2], r))

            def exp(x):
                p, h = divmod(x, HP)
                r, nk = rows(ORDER[p]), nkeys(ORDER[p])
                act.wait_ge(s_read, x + 1)
                act.activation(E[0:r, x % 2, 0:nk], S[0:r, x % 2, 0:nk], ACT.Exp, bias=nm[0:r, p % 2, h:h + 1],
                               scale=-1.0, accum_out=rs[0:r, p % 2, h:h + 1]).then_inc(e_done, 1)

            def copy_probs(x):
                t = ORDER[x // HP]
                r = rows(t)
                if x >= 2:
                    act.wait_ge(o_done, x - 1)
                for g in range(groups(t)):
                    nb = min(4, blocks(t) - 4 * g)
                    bank = quads(banks[4 + n[0] % 2], r)
                    last = width(t, 4 * g + nb - 1)
                    if last == P:
                        copy(pT[:, x % 2, 4 * g:4 * g + nb, 0:r], bank[:, 0:nb])
                    else:
                        act.wait_ge(turned, n[0] + 1)
                        act.copy(pT[:, x % 2, 4 * g:4 * g + nb - 1, 0:r], bank[:, 0:nb - 1])
                        copy(pT[0:last, x % 2, 4 * g + nb - 1, 0:r], bank[0:last, nb - 1])

            k_high(0)
            q_high(0)
            for sl in range(NS):
                r = srows(sl)
                if sl + 1 < NS:
                    k_high(sl + 1)
                for part, keys in enumerate((k_hh, k_ll)):
                    act.wait_ge(k_turned, 2 * sl + part + 1)
                    act.copy(keys[:, :, sl * P:sl * P + r], quads(banks[2 * part + sl % 2], r)).then_inc(k_copied, 1)
            for g in range(4):
                queries(0, g)
            for part, r in KEY_PARTS:
                act.copy(ih[0:r, part], ki[0:r, part]).then_inc(ih_made, 1)
            for g, quad in enumerate(KEY_QUADS):
                act.wait_ge(ihi_turned, g + 1)
                copy_key_quad(act.copy, ki_hh, banks[IDX_HI_BANKS[g]], quad).then_inc(ihi_copied, 1)
            def next_exp(x):
                if x + 1 < HP * NT:
                    exp(x + 1)
                    for m, i in items_at[x + 1]:
                        ranking.relu(act, m, i)

            for x in range(-1, HP * NT):
                p, h = divmod(x, HP)
                if deep(x):
                    next_exp(x)
                if x >= 0:
                    copy_probs(x)
                    if p + 1 < NT:
                        if h == 2 and RING <= p + 1 < NR:
                            q_idx_high(p + 1)
                        if h == 5:
                            q_high(p + 1)
                        if h == 7 and RING <= p + 1 < NR:
                            idx_queries(p + 1)
                        if h in QUERY_AT:
                            queries(p + 1, QUERY_AT.index(h))
                if not deep(x):
                    next_exp(x)

        @block.vector
        def _(dve):
            def scores(x):
                p, h = divmod(x, HP)
                t = ORDER[p]
                r, nk = rows(t), nkeys(t)
                mask = ranking.scored(p - FIRST) if p >= FIRST else early[0:r, 2 * P - nk:2 * P]
                if h == 0 and p > FIRST:
                    dve.wait_ge(ranking.chain, ranking.last[p - FIRST])
                dve.wait_ge(s_done, x + 1)
                if x >= 2:
                    dve.wait_ge(e_done, x - 1)
                dve.tensor_tensor_reduce(S[0:r, x % 2, 0:nk], wide(("head", x), r, nk), mask, -HD ** -0.5, LARGE,
                                         ALU.add, ALU.min, nm[0:r, p % 2, h:h + 1]).then_inc(s_read, 1)

            def outputs(p, b):
                t, r = ORDER[p], rows(ORDER[p])
                dve.wait_ge(e_done, HP * p + 8 * b + 8)
                if p >= 2:
                    dve.wait_ge(o_read, 2 * (p - 2) + b + 1)
                dve.reciprocal(rden[0:r, p % 2, 8 * b:8 * b + 8], rs[0:r, p % 2, 8 * b:8 * b + 8]).then_inc(rden_made, 1)
                dve.wait_ge(rden_made, 2 * p + b + 1)
                dve.wait_ge(o_done, HP * p + 8 * b + 8)
                dve.tensor_tensor(A[0:r, t, b * COLS:(b + 1) * COLS].rearrange("p (h d) -> p h d", d=HD),
                                  heads_of(banks[6 + b], r), rden[0:r, p % 2, 8 * b:8 * b + 8].unsqueeze(2).to_broadcast([r, 8, HD]),
                                  ALU.mult).then_inc(o_read, 1)

            for _ in range(ROUNDS_AHEAD):
                ranking.take(dve, [1, 2])
            for part, r in KEY_PARTS:
                dve.wait_ge(ih_made, 1 if r == P else 2)
                dve.tensor_tensor(il[0:r, part], ki[0:r, part], ih[0:r, part], ALU.subtract).then_inc(il_made, 1)
            for g, quad in enumerate(KEY_QUADS):
                dve.wait_ge(ilo_turned, g + 1)
                copy_key_quad(dve.tensor_copy, ki_ll, banks[IDX_LO_BANKS[g]], quad).then_inc(ilo_copied, 1)
            dve.wait_ge(masks, 2)
            for x in range(HP * NT):
                p, h = divmod(x, HP)
                left = list(rounds_at[x])
                together = sorted(set(left))
                if len(together) == 1:
                    ranking.find(dve, together)
                    scores(x)
                    ranking.mark(dve, together)
                    left.remove(together[0])
                else:
                    scores(x)
                for m, i in mixes_at[x]:
                    if i == 0:
                        dve.wait_ge(s_read, HP * m)
                    ranking.mix(dve, m, i)
                while left:
                    together = sorted(set(left))
                    ranking.take(dve, together)
                    for m in together:
                        left.remove(m)
                if h == 3 and p >= 1:
                    outputs(p - 1, 1)
                if h == 11:
                    outputs(p, 0)
                if h == HP - 1 and 2 <= p < NT - 1:
                    ranking.close(dve, p - 1)
            outputs(NT - 1, 1)

        @block.tensor
        def _(pe):
            n = [0]

            def group(pairs, unit):
                bank = banks[4 + n[0] % 2]
                if n[0] >= 2:
                    pe.wait_ge(copied, n[0] - 1)
                for at, src, r in pairs:
                    out = bank[0:src.shape[1], at:at + r]
                    mm = pe.transpose(out if unit is ident else out.bitcast(F32R), src, unit[0:r, 0:r])
                mm.then_inc(turned, 1)
                n[0] += 1

            flat = lambda x: x.rearrange("p two d -> p (two d)")
            turn = lambda bank, at, src: pe.transpose(bank[:, at:at + src.shape[0]].bitcast(F32R), src,
                                                      ident_r[0:src.shape[0], 0:src.shape[0]])

            def queries(p, g):
                r = rows(ORDER[p])
                if g == 0:
                    pe.wait_ge(q_lo_made, p + 1)
                group([(i * P, flat(q_tok[0:r, 4 * g + i]), r) for i in range(4)], ident_r)

            def banks_of(use):
                for kind, *which in before[use]:
                    if kind == "item":
                        pe.wait_ge(ranking.relu_done, ranking.count(*which) + 1)
                    else:
                        pe.wait_ge(s_read, which[0] + 1)
                return [banks[b] for b in place[use]]

            idx_group = {}

            def idx_queries(m):
                r = rows(RANKED[m])
                pe.wait_ge(qi_lo_made, m - RING + 1)
                group([(h * P, flat(qi_tok[0:r, m % 2, h]), r) for h in range(IDX_HEADS)], ident_r)
                idx_group[m] = n[0]

            def item(m, i):
                if i == 0:
                    pe.wait_ge(copied, idx_group[m])
                ranking.product(pe, banks_of(("item", m, i)), qiS[:, i, 0:rows(RANKED[m])], m, ki_hh, ki_ll)

            query_groups = {}

            def scores(x):
                p, h = divmod(x, HP)
                t = ORDER[p]
                r, nk, k0 = rows(t), nkeys(t), key0(t)
                kv = h // (C_HEADS // C_KV)
                if h == 0:
                    pe.wait_ge(copied, query_groups[p])
                out = banks_of(("head", x))
                for c0 in range(0, nk, COLS):
                    w = min(COLS, nk - c0)
                    at, q = out[c0 // COLS][0:r, 0:w], qS[:, p % 2, h, 0:r]
                    pe.matmul(at, q, k_hh[:, kv, k0 + c0:k0 + c0 + w], start=True, stop=False)
                    mm = pe.matmul(at, q, k_ll[:, kv, k0 + c0:k0 + c0 + w], start=False, stop=True)
                mm.then_inc(s_done, 1)

            def transposes(x):
                t = ORDER[x // HP]
                r = rows(t)
                pe.wait_ge(e_done, x + 1)
                for g in range(groups(t)):
                    group([(b % 4 * P, E[0:r, x % 2, b * P:b * P + width(t, b)], r)
                           for b in range(4 * g, min(4 * g + 4, blocks(t)))], ident)

            def values(x, at):
                p, h = divmod(x, HP)
                t = ORDER[p]
                r = rows(t)
                kv, b = h // (C_HEADS // C_KV), h // 8
                pe.wait_ge(copied, at)
                if h % 8 == 0 and p >= 1:
                    pe.wait_ge(o_read, 2 * p + b - 1)
                o = h % 8 * HD
                for kb in range(blocks(t)):
                    w = width(t, kb)
                    mm = pe.matmul(banks[6 + b][0:r, o:o + HD], pT[0:w, x % 2, kb, 0:r],
                                   vc[0:w, slot0(t) + kb, kv * HD:(kv + 1) * HD], start=(kb == 0), stop=(kb == blocks(t) - 1))
                mm.then_inc(o_done, 1)

            for sl in range(NS):
                r = srows(sl)
                for part, (split, made) in enumerate(((kh, kh_made), (kl, kl_made))):
                    pe.wait_ge(made, sl + 1)
                    if sl >= 2:
                        pe.wait_ge(k_copied, 2 * (sl - 2) + part + 1)
                    for kv in range(C_KV):
                        mm = turn(banks[2 * part + sl % 2], kv * P, flat(split[0:r, sl % KRING, kv]))
                    mm.then_inc(k_turned, 1)
            for g in range(4):
                queries(0, g)
            query_groups[0] = n[0]
            pe.wait_ge(k_copied, 2 * NS)
            for split, made, done, its_banks in ((ih, ih_made, ihi_turned, IDX_HI_BANKS), (il, il_made, ilo_turned, IDX_LO_BANKS)):
                pe.wait_ge(made, len(KEY_PARTS))
                for g, quad in enumerate(KEY_QUADS):
                    for b, sl in enumerate(quad):
                        mm = turn(banks[its_banks[g]], b * P, split[0:srows(sl), sl])
                    mm.then_inc(done, 1)
            pe.wait_ge(ihi_copied, len(KEY_QUADS))
            pe.wait_ge(ilo_copied, len(KEY_QUADS))
            ready = {}
            issued = 0
            for x in range(-1, HP * NT):
                p, h = divmod(x, HP)
                while issued < HP * NT and issued <= x + (2 if deep(x) else 1):
                    scores(issued)
                    for m, i in items_at[issued]:
                        item(m, i)
                    issued += 1
                if x >= 0:
                    transposes(x)
                    ready[x] = n[0]
                    if h == 7 and RING <= p + 1 < NR:
                        idx_queries(p + 1)
                    if h in QUERY_AT and p + 1 < NT:
                        queries(p + 1, QUERY_AT.index(h))
                        query_groups[p + 1] = n[0]
                    if x >= 1:
                        values(x - 1, ready[x - 1])
            values(HP * NT - 1, ready[HP * NT - 1])


def rope_table():
    inv = np.exp(-np.float32(np.log(THETA)) * np.arange(HALF, dtype=np.float32) / np.float32(HALF)).astype(np.float32)
    pos = np.concatenate([np.arange(SEQ), PAST + np.arange(DEC)]).astype(np.float32)
    ang = (pos[:, None] * inv[None, :]).astype(np.float32)
    cos, sin = np.cos(ang), np.sin(ang)
    return np.concatenate([cos, cos, -sin, sin], axis=1).astype(np.float32)


OUTPUTS = [
    ("y_prompt", (SEQ, D), (1, SEQ, D)),
    ("y_sample", (DEC, D), (1, DEC, D)),
    ("p_b_k", (B_WIN, B_KV * HD), (1, 1, B_WIN, B_KV, HD)),
    ("p_b_v", (B_WIN, B_KV * HD), (1, 1, B_WIN, B_KV, HD)),
    ("p_c_k", (SEQ, C_KVW), (1, 1, SEQ, C_KV, HD)),
    ("p_c_v", (SEQ, C_KVW), (1, 1, SEQ, C_KV, HD)),
    ("p_c_idx", (SEQ, HD), (1, 1, SEQ, HD)),
    ("s_a_v", (DEC, A_WIDTH), (1, 1, DEC, A_WIDTH)),
    ("s_b_k", (DEC, B_KV * HD), (1, 1, DEC, B_KV, HD)),
    ("s_b_v", (DEC, B_KV * HD), (1, 1, DEC, B_KV, HD)),
    ("s_c_k", (DEC, C_KVW), (1, 1, DEC, C_KV, HD)),
    ("s_c_v", (DEC, C_KVW), (1, 1, DEC, C_KV, HD)),
    ("s_c_idx", (DEC, HD), (1, 1, DEC, HD)),
]


def kernel(x_prompt, x_sample, cache_b_k, cache_b_v, cache_c_k, cache_c_v, cache_c_idx,
           ab_w_in, a_ln_g, a_ln_b, a_ws, a_bs, b_sinks, ab_w_out, c_w_in, c_w_out,
           ln1_g, ln1_b, ln2_g, ln2_b, ff_w1, ff_w2):
    import concourse.bacc as bacc
    from concourse.bass_utils import run_bass_kernel_spmd

    x = np.concatenate([np.asarray(x_prompt)[0], np.asarray(x_sample)[0]], axis=0)
    ins = {
        "x": x,
        "xT": x.T,
        "cache_b_k": np.asarray(cache_b_k).reshape(B_WIN, B_KV * HD),
        "cache_b_v": np.asarray(cache_b_v).reshape(B_WIN, B_KV * HD),
        "cache_c_k": np.asarray(cache_c_k).reshape(PAST, C_KVW),
        "cache_c_v": np.asarray(cache_c_v).reshape(PAST, C_KVW),
        "cache_c_idx": np.asarray(cache_c_idx).reshape(PAST, HD),
        "ab_w_in": np.asarray(ab_w_in)[0],
        "a_ln_g": np.asarray(a_ln_g),
        "a_ln_b": np.asarray(a_ln_b),
        "ws_T": np.asarray(a_ws)[0].transpose(2, 0, 1),
        "bs_T": np.asarray(a_bs)[0].T,
        "sinks": np.asarray(b_sinks),
        "ab_w_out": np.asarray(ab_w_out)[0],
        "c_w_in": np.asarray(c_w_in)[0],
        "c_w_out": np.asarray(c_w_out)[0],
        "ln1_g": np.asarray(ln1_g), "ln1_b": np.asarray(ln1_b),
        "ln2_g": np.asarray(ln2_g), "ln2_b": np.asarray(ln2_b),
        "ff_w1": np.asarray(ff_w1), "ff_w2": np.asarray(ff_w2),
        "rope": rope_table(),
    }
    ins = {k: np.ascontiguousarray(v) for k, v in ins.items()}
    nc = bacc.Bacc("TRN2", target_bir_lowering=False, num_devices=1)
    aps, arrays = {}, {}
    for k, v in ins.items():
        arrays[f"in_{k}"] = v
        aps[k] = nc.dram_tensor(f"in_{k}", v.shape, mybir.dt.from_np(v.dtype), kind="ExternalInput").ap()
    for k, shape, _ in OUTPUTS:
        aps[k] = nc.dram_tensor(f"out_{k}", shape, F32, kind="ExternalOutput").ap()
    encoder(nc, aps)
    got = run_bass_kernel_spmd(nc, [arrays], core_ids=[0]).results[0]
    return tuple(np.asarray(got[f"out_{k}"]).reshape(shape) for k, _, shape in OUTPUTS)
```
